# Optimizing a Trainium2 kernel written in Bass

```python
import jax
import jax.numpy as jnp
from jax import lax
import numpy as np

D_MODEL = 1024
BATCH = 1
SEQ = 512
DEPTH = 1
DEC_BATCH = 8
DEC_SEQ = 1
PAST_LEN = 2048
PAGE_SIZE = 128

EPS = 1e-6
POOL_WINDOWS = (2, 4, 8, 16)
N_POOL_GROUPS = len(POOL_WINDOWS)
D_POOL = D_MODEL
POOL_GROUP = D_POOL // N_POOL_GROUPS
POOL_HIST = max(POOL_WINDOWS) - 1
ATT_GROUPS = ((128, 1), (512, 4), (2048, 16))
N_ATT_GROUPS = len(ATT_GROUPS)
N_SLOTS = 8
HEAD_DIM = 64
N_HEADS = N_ATT_GROUPS * N_SLOTS
D_ATT = N_HEADS * HEAD_DIM
D_ATT_OUT = N_SLOTS * HEAD_DIM
D_FF = 2816
CONV_W = 3
D_IN = D_POOL + 3 * D_ATT + 2 * D_MODEL
IN_SPLITS = (D_POOL, D_POOL + D_ATT, D_POOL + 2 * D_ATT, D_POOL + 3 * D_ATT, D_POOL + 3 * D_ATT + D_MODEL)

kernel_name = 'hybrid_pool_dilated_attn_convffn_step'

def rms_norm(x, g):
    xf = x.astype(jnp.float32)
    y = xf * lax.rsqrt(jnp.mean(xf * xf, axis=-1, keepdims=True) + EPS)
    return (y * g.astype(jnp.float32)).astype(x.dtype)

def modulate(x, shift, scale):
    return x * (1 + scale) + shift

def pool_mix(u_ext, pos, w_map, scale):
    B, n_ext, _ = u_ext.shape
    T = pos.shape[0]
    P = n_ext - T
    uf = u_ext.astype(jnp.float32)
    cs = jnp.concatenate([jnp.zeros_like(uf[:, :1]), jnp.cumsum(uf, axis=1)], axis=1)
    cs_end = cs[:, P + 1:]
    u_new = uf[:, P:]
    groups = []
    for gi, win in enumerate(POOL_WINDOWS):
        lo, hi = gi * POOL_GROUP, (gi + 1) * POOL_GROUP
        window_sum = cs_end[..., lo:hi] - cs[:, P + 1 - win:P + 1 - win + T, lo:hi]
        count = jnp.minimum(pos + 1, win).astype(jnp.float32)[None, :, None]
        groups.append(window_sum / count - u_new[..., lo:hi])
    pooled = jnp.stack(groups, axis=2)
    mixed = jnp.einsum('btgc,gcd->btgd', pooled, w_map.astype(jnp.float32)).reshape(B, T, D_POOL)
    return (mixed * scale.astype(jnp.float32)).astype(u_ext.dtype)

def strided_window_attn(q, k, v, dil, span):
    B, T, S, Dh = q.shape
    n_sub = T // dil
    nb = -(-n_sub // span)
    pad = nb * span - n_sub

    def to_blocks(a):
        a = a.reshape(B, n_sub, dil, S, Dh).transpose(0, 2, 1, 3, 4)
        a = jnp.pad(a, ((0, 0), (0, 0), (0, pad), (0, 0), (0, 0)))
        return a.reshape(B, dil, nb, span, S, Dh)

    def with_prev(a):
        prev = jnp.pad(a[:, :, :-1], ((0, 0), (0, 0), (1, 0), (0, 0), (0, 0), (0, 0)))
        return jnp.concatenate([prev, a], axis=3)

    qb, kb, vb = to_blocks(q), to_blocks(k), to_blocks(v)
    kc, vc = with_prev(kb), with_prev(vb)
    s = jnp.einsum('brnqsd,brnksd->brnsqk', qb.astype(jnp.float32), kc.astype(jnp.float32)) * (HEAD_DIM ** -0.5)
    qi = jnp.arange(span)[:, None] + span
    ki = jnp.arange(2 * span)[None, :]
    dist = qi - ki
    band = (dist >= 0) & (dist <= span)
    no_prev = (jnp.arange(nb) == 0)[:, None, None] & (ki < span)[None]
    mask = band[None] & ~no_prev
    s = jnp.where(mask[None, None, :, None], s, -jnp.inf)
    m = jnp.max(s, axis=-1, keepdims=True)
    p = jnp.exp(s - m)
    den = jnp.sum(p, axis=-1, keepdims=True)
    den_t = den[..., 0].transpose(0, 1, 2, 4, 3)
    o = jnp.einsum('brnsqk,brnksd->brnqsd', p, vc.astype(jnp.float32)) / den_t[..., None]
    lse = (m[..., 0] + jnp.log(den[..., 0])).transpose(0, 1, 2, 4, 3)
    o = o.reshape(B, dil, nb * span, S, Dh)[:, :, :n_sub].transpose(0, 2, 1, 3, 4).reshape(B, T, S, Dh)
    lse = lse.reshape(B, dil, nb * span, S)[:, :, :n_sub].transpose(0, 2, 1, 3).reshape(B, T, S)
    return o, lse

def strided_window_attn_step(q, k_ext, v_ext, dil, span):
    B, T, S, Dh = q.shape
    L = k_ext.shape[1] - T
    ki = (L + jnp.arange(T))[:, None] - dil * jnp.arange(span + 1)[None, :]
    valid = ki >= 0
    idx = jnp.maximum(ki, 0)
    kg = k_ext[:, idx].astype(jnp.float32)
    vg = v_ext[:, idx].astype(jnp.float32)
    s = jnp.einsum('btsd,btjsd->btsj', q.astype(jnp.float32), kg) * (HEAD_DIM ** -0.5)
    s = jnp.where(valid[None, :, None, :], s, -jnp.inf)
    m = jnp.max(s, axis=-1, keepdims=True)
    p = jnp.exp(s - m)
    den = jnp.sum(p, axis=-1, keepdims=True)
    o = jnp.einsum('btsj,btjsd->btsd', p, vg) / den
    lse = m[..., 0] + jnp.log(den[..., 0])
    return o, lse

def merge_groups(outs, lses):
    o = jnp.stack(outs, axis=2)
    w = jax.nn.softmax(jnp.stack(lses, axis=2), axis=2)
    return jnp.sum(o * w[..., None], axis=2)

def hybrid_layer(x, c, pos, pool_hist, conv_hist, kv_hist, prm, prompt):
    (w_ada, b_ada, g_pre_mix, g_post_mix, g_pre_ffn, g_post_ffn, w_in, w_pool_map, pool_scale,
     w_proj_pool, w_proj_att, w_out, w_up, w_conv, b_conv, w_down) = prm
    B, T, _ = x.shape
    mod = (jax.nn.silu(c) @ w_ada + b_ada)[:, None, :]
    shift_m, scale_m, gate_m, shift_f, scale_f, gate_f = jnp.split(mod, 6, axis=-1)

    h = modulate(rms_norm(x, g_pre_mix), shift_m, scale_m)
    u, q, k, v, z_pool, z_att = jnp.split(h @ w_in, IN_SPLITS, axis=-1)
    u_ext = jnp.concatenate([pool_hist, u], axis=1)
    y_pool = pool_mix(u_ext, pos, w_pool_map, pool_scale) @ w_proj_pool
    q = q.reshape(B, T, N_ATT_GROUPS, N_SLOTS, HEAD_DIM)
    k = k.reshape(B, T, N_ATT_GROUPS, N_SLOTS, HEAD_DIM)
    v = v.reshape(B, T, N_ATT_GROUPS, N_SLOTS, HEAD_DIM)
    outs, lses, new_kv = [], [], []
    for gi, (win, dil) in enumerate(ATT_GROUPS):
        span = win // dil
        q_g, k_g, v_g = q[:, :, gi], k[:, :, gi], v[:, :, gi]
        if prompt:
            k_ext, v_ext = k_g, v_g
            o_g, lse_g = strided_window_attn(q_g, k_g, v_g, dil, span)
        else:
            k_hist, v_hist = kv_hist[gi]
            k_ext = jnp.concatenate([k_hist, k_g], axis=1)
            v_ext = jnp.concatenate([v_hist, v_g], axis=1)
            o_g, lse_g = strided_window_attn_step(q_g, k_ext, v_ext, dil, span)
        keep = min(win, k_ext.shape[1])
        new_kv.append(k_ext[:, -keep:])
        new_kv.append(v_ext[:, -keep:])
        outs.append(o_g)
        lses.append(lse_g)
    o = merge_groups(outs, lses).reshape(B, T, D_ATT_OUT).astype(x.dtype)
    y_att = o @ w_proj_att
    mix = (jax.nn.sigmoid(z_pool) * y_pool + jax.nn.sigmoid(z_att) * y_att) @ w_out
    x = x + gate_m * rms_norm(mix, g_post_mix)

    h = modulate(rms_norm(x, g_pre_ffn), shift_f, scale_f)
    hu_ext = jnp.concatenate([conv_hist, h @ w_up], axis=1)
    hc = b_conv
    for j in range(CONV_W):
        hc = hc + hu_ext[:, j:j + T] * w_conv[j]
    a, b = jnp.split(hc, 2, axis=-1)
    ffn = (jax.nn.gelu(a, approximate=True) * b) @ w_down
    x = x + gate_f * rms_norm(ffn, g_post_ffn)
    new_state = (new_kv[0], new_kv[1], new_kv[2], new_kv[3], new_kv[4], new_kv[5],
                 u_ext[:, -POOL_HIST:], hu_ext[:, -(CONV_W - 1):])
    return x, new_state

def setup_inputs(seed: int = 0) -> dict:
    key = jax.random.key(seed)
    ks = jax.random.split(key, 28)
    f32 = jnp.float32

    def nrm(k, shape, s=1.0):
        return jax.random.normal(k, shape, f32) * s

    def gain(k):
        return 1.0 + nrm(k, (DEPTH, D_MODEL), 0.05)

    L = [min(win, PAST_LEN) for win, _ in ATT_GROUPS]
    return {
        'x_prompt': nrm(ks[0], (BATCH, SEQ, D_MODEL)),
        'x_sample': nrm(ks[1], (DEC_BATCH, DEC_SEQ, D_MODEL)),
        'c_prompt': nrm(ks[2], (BATCH, D_MODEL)),
        'c_sample': nrm(ks[3], (DEC_BATCH, D_MODEL)),
        'cache_k_w128': nrm(ks[4], (DEPTH, DEC_BATCH, L[0], N_SLOTS, HEAD_DIM)),
        'cache_v_w128': nrm(ks[5], (DEPTH, DEC_BATCH, L[0], N_SLOTS, HEAD_DIM)),
        'cache_k_w512': nrm(ks[6], (DEPTH, DEC_BATCH, L[1], N_SLOTS, HEAD_DIM)),
        'cache_v_w512': nrm(ks[7], (DEPTH, DEC_BATCH, L[1], N_SLOTS, HEAD_DIM)),
        'cache_k_w2048': nrm(ks[8], (DEPTH, DEC_BATCH, L[2], N_SLOTS, HEAD_DIM)),
        'cache_v_w2048': nrm(ks[9], (DEPTH, DEC_BATCH, L[2], N_SLOTS, HEAD_DIM)),
        'state_pool': nrm(ks[10], (DEPTH, DEC_BATCH, POOL_HIST, D_POOL)),
        'state_conv': nrm(ks[11], (DEPTH, DEC_BATCH, CONV_W - 1, 2 * D_FF)),
        'w_ada': nrm(ks[12], (DEPTH, D_MODEL, 6 * D_MODEL), 0.5 * D_MODEL ** -0.5),
        'b_ada': nrm(ks[13], (DEPTH, 6 * D_MODEL), 0.01),
        'g_pre_mix': gain(ks[14]),
        'g_post_mix': gain(ks[15]),
        'g_pre_ffn': gain(ks[16]),
        'g_post_ffn': gain(ks[17]),
        'w_in': nrm(ks[18], (DEPTH, D_MODEL, D_IN), D_MODEL ** -0.5),
        'w_pool_map': nrm(ks[19], (DEPTH, N_POOL_GROUPS, POOL_GROUP, POOL_GROUP), POOL_GROUP ** -0.5),
        'pool_scale': 1.0 + nrm(ks[20], (DEPTH, D_POOL), 0.1),
        'w_proj_pool': nrm(ks[21], (DEPTH, D_POOL, D_MODEL), D_POOL ** -0.5),
        'w_proj_att': nrm(ks[22], (DEPTH, D_ATT_OUT, D_MODEL), D_ATT_OUT ** -0.5),
        'w_out': nrm(ks[23], (DEPTH, D_MODEL, D_MODEL), D_MODEL ** -0.5),
        'w_up': nrm(ks[24], (DEPTH, D_MODEL, 2 * D_FF), D_MODEL ** -0.5),
        'w_conv': nrm(ks[25], (DEPTH, CONV_W, 2 * D_FF), CONV_W ** -0.5),
        'b_conv': nrm(ks[26], (DEPTH, 2 * D_FF), 0.01),
        'w_down': nrm(ks[27], (DEPTH, D_FF, D_MODEL), D_FF ** -0.5),
    }

def reference(x_prompt, x_sample, c_prompt, c_sample, cache_k_w128, cache_v_w128, cache_k_w512, cache_v_w512,
              cache_k_w2048, cache_v_w2048, state_pool, state_conv, w_ada, b_ada, g_pre_mix, g_post_mix,
              g_pre_ffn, g_post_ffn, w_in, w_pool_map, pool_scale, w_proj_pool, w_proj_att, w_out, w_up,
              w_conv, b_conv, w_down):
    params = (w_ada, b_ada, g_pre_mix, g_post_mix, g_pre_ffn, g_post_ffn, w_in, w_pool_map, pool_scale,
              w_proj_pool, w_proj_att, w_out, w_up, w_conv, b_conv, w_down)
    caches = ((cache_k_w128, cache_v_w128), (cache_k_w512, cache_v_w512), (cache_k_w2048, cache_v_w2048))
    bp, tp = x_prompt.shape[0], x_prompt.shape[1]
    pos_p = jnp.arange(tp)
    pos_s = PAST_LEN + jnp.arange(x_sample.shape[1])
    zeros_pool = jnp.zeros((bp, POOL_HIST, D_POOL), x_prompt.dtype)
    zeros_conv = jnp.zeros((bp, CONV_W - 1, 2 * D_FF), x_prompt.dtype)
    xp, xs = x_prompt, x_sample
    st_p, st_s = [], []
    for l in range(DEPTH):
        prm = tuple(w[l] for w in params)
        xp, sp = hybrid_layer(xp, c_prompt, pos_p, zeros_pool, zeros_conv, None, prm, True)
        kv_l = tuple((kc[l], vc[l]) for kc, vc in caches)
        xs, ss = hybrid_layer(xs, c_sample, pos_s, state_pool[l], state_conv[l], kv_l, prm, False)
        st_p.append(sp)
        st_s.append(ss)
    new_p = [jnp.stack([s[i] for s in st_p], axis=0) for i in range(8)]
    new_s = [jnp.stack([s[i] for s in st_s], axis=0) for i in range(8)]
    return (xp, xs, new_p[0], new_s[0], new_p[1], new_s[1], new_p[2], new_s[2], new_p[3], new_s[3],
            new_p[4], new_s[4], new_p[5], new_s[5], new_p[6], new_s[6], new_p[7], new_s[7])


_drawn_inputs = setup_inputs


def setup_inputs(seed=0):
    import zlib

    import numpy as np

    out = dict(_drawn_inputs(seed))
    spreads = {}
    factors = {'b_ada': 3.604, 'g_post_mix': 4.027, 'g_post_ffn': 4.133, 'b_conv': 8.0}
    for name, (base, spread) in spreads.items():
        noise = np.random.default_rng([zlib.crc32(name.encode()), seed]).standard_normal(out[name].shape)
        drawn = base * np.exp(spread * noise) if base else spread * noise
        out[name] = jnp.asarray(drawn.astype(out[name].dtype))
    for name, factor in factors.items():
        out[name] = (out[name] * factor).astype(out[name].dtype)
    return out
```

```python
from contextlib import ExitStack

import concourse.bass as bass
from concourse import mybir

F32 = mybir.dt.float32
F32R = mybir.dt.float32r
BF16 = mybir.dt.bfloat16
ALU = mybir.AluOpType
ACT = mybir.ActivationFunctionType
AX_X = mybir.AxisListType.X
ds = bass.ds

P = 128
D = 1024
KT = D // P
TP = 512
NB = 8
TC = TP + NB
HALF = TC // 2
NS, HD = 8, 64
DA = NS * HD
DILS = (1, 4, 16)
NG = len(DILS)
WINS = tuple(P * d for d in DILS)
PAIRS = NS // 2
NR = 4
POOL_HIST = 15
FF = 2816
FT = FF // P
EPS = 1e-6
NEG = -1e30
BIG = 3e38
NADA = 6 * KT
MC = NB + 1
PROMPT = NB
BLK = 8
RAW, HL = 4, 2
UW = BLK * P
TAIL = POOL_HIST + NB
CONV_TAIL = 2 + NB

TURN = (
    [("unit", k) for k in range(4)] + [("turn", 0)] + [("unit", k) for k in range(4, 7)] + [("turn", 1)]
    + [("unit", k) for k in range(7, 10)] + [("turn", 2), ("step", 0), ("unit", 10), ("step", 1), ("ada", 0), ("step", 2),
       ("unit", 11), ("step", 3), ("ada", 2), ("step", 4), ("unit", 12), ("step", 5), ("unit", 13), ("step", 6),
       ("ada", 4), ("step", 7), ("unit", 14), ("step", 8), ("ada", 6), ("step", 9)]
)
TURN_UNITS = 15
IDLE, last = {}, 1
for what, k in TURN:
    if what == "unit":
        last = k % 2
    else:
        IDLE[what, k] = 1 - last
TASKS = 2 * NR
SEGMENTS = {"pairs": (PAIRS, TURN_UNITS), "mid": (1, 14), "out": (2, 4), "up": (11, 4), "down": (3, 6), "last": (1, 6)}


class Stream:

    def __init__(self):
        self.first, self.fills, n, prev = {}, {}, 0, None
        fills = [0] * RAW
        self.dist = {}
        for name, (iters, units) in SEGMENTS.items():
            self.first[name], self.fills[name] = n, list(fills)
            for pos in range(units):
                gaps = []
                if pos >= RAW:
                    gaps = [RAW]
                else:
                    for u in ([units] if iters > 1 else []) + ([prev] if prev else []):
                        gaps.append(pos + u - max(q for q in range(u) if q % RAW == pos % RAW))
                self.dist[name, pos] = min(gaps, default=RAW)
            n += iters * units
            for s in range(RAW):
                fills[s] += iters * len(range(s, units, RAW))
            prev = units
        self.total = n

    def number(self, seg, it, pos):
        return it * SEGMENTS[seg][1] + (self.first[seg] + pos)

    def fill(self, seg, it, pos):
        units = SEGMENTS[seg][1]
        s = 0 if pos == units else pos % RAW
        per = len(range(s, units, RAW))
        done = per + 1 if pos == units else pos // RAW + 1
        return it * per + (self.fills[seg][s] + done)


def tiles(x):
    return x.rearrange("(k p) n -> p k n", p=P)


def program(nc, ins, outs):
    st = Stream()
    w_in, w_up, w_down = ins["w_in"][0], ins["w_up"][0], ins["w_down"][0]
    w_ada, w_out = ins["w_ada"][0], ins["w_out"][0]
    caches = [(ins[f"cache_k_w{w}"], ins[f"cache_v_w{w}"]) for w in WINS]
    scratch = nc.dram_tensor("sample_qkv", (3 * NG, NB, DA), F32, kind="Internal").ap()

    with ExitStack() as ctx:
        def sem(name):
            return ctx.enter_context(nc.semaphore(name))

        def psum(name, shape):
            return ctx.enter_context(nc.psum_tensor(name, shape, F32))

        top = [2048]

        def region(nbytes):
            at = top[0]
            top[0] = at + (nbytes + 31) // 32 * 32
            assert top[0] <= 229344, top[0]
            return at

        def put(name, shape, dt, at):
            return nc.alloc_sbuf_tensor_at(name, [P, *shape], dt, offset=at)

        def new(name, shape, dt=F32):
            n = 2 if dt == BF16 else 4
            for s in shape:
                n *= s
            return put(name, shape, dt, region(n))

        FULL = KT * TC * 4
        r_act = region(2 * FULL)
        act_hi, act_lo = put("act_hi", [KT, TC], F32R, r_act), put("act_lo", [KT, TC], F32R, r_act + FULL)
        ffn = put("ffn", [KT, TC], F32, r_act)
        r_x = region(FULL)
        xT = put("xT", [KT, TC], F32, r_x)
        raw = new("raw", [RAW, UW])
        w_hi, w_lo = new("w_hi", [HL, UW], F32R), new("w_lo", [HL, UW], F32R)
        r_ff = top[0]
        r_z = region(2 * FULL)
        thp, tha = put("thp", [KT, TC], F32, r_z), put("tha", [KT, TC], F32, r_z + FULL)
        x_rows = put("x_rows", [4, D], F32, r_z)
        xs_rows = put("xs_rows", [D], F32, r_z + FULL)
        c_rows, c_tanh, c_silu = (put(n, [D], F32, r_z + FULL + 4096 * i) for i, n in ((1, "c_rows"), (2, "c_tanh"), (3, "c_silu")))
        r_u = region(FULL)
        uT = put("uT", [KT, TC], F32, r_u)
        mix_hi = put("mixed_hi", [KT, TC], F32R, r_u)
        mixT = put("mixT", [KT, TC], F32, r_u)
        norm_u = put("norm_u", [KT, TC], F32, r_z)
        r_att = region(9 * TC * 4)
        qkvT = put("qkvT", [9, TC], F32, r_att)
        mix_lo = put("mixed_lo", [KT, TC], F32R, r_att)
        o_hi, o_lo = new("o_hi", [PAIRS, TC], F32R), new("o_lo", [PAIRS, TC], F32R)
        r_ada = region(4 * UW * 4)
        ada_raw = put("ada_raw", [4, UW], F32, r_ada)
        vN = new("vN", [NG, 4, P])
        kN = new("kN", [4, P])
        mask = new("mask", [NR, 768], BF16)
        r_s = region(2 * 768 * 4)
        S = put("S", [2, 768], F32, r_s)
        sq = put("sq", [2, TC], F32, r_s)
        r_pt = region(2 * 768 * 4)
        PT = put("PT", [2, 768], F32, r_pt)
        rs = put("rs", [TC], F32, r_pt)
        ssq = put("ssq", [TC], F32, r_pt + 2080)
        pw = new("pw", [2, 16 + TP])
        vec_rows = put("vec_rows", [3, P], F32, r_u)
        hist_rows = put("hist_rows", [D], F32, r_u + 2048)
        mod = new("mod", [NADA, MC])
        siluT = new("siluT", [KT, MC])
        vec = new("vec", [3 * 88])
        a_m, a_f, gg_m, gg_f = (new(n, [KT, MC]) for n in ("a_m", "a_f", "gg_m", "gg_f"))
        ident, ones = new("ident", [P]), new("ones", [P])
        smpT = new("smpT", [PAIRS, 9, NB])
        u_tail = new("u_tail", [KT, TAIL])
        hist_sum = new("hist_sum", [KT, NB])
        inv_count = new("inv_count", [16])
        eps = new("eps", [1])
        ind4 = new("ind4", [2, 4])
        neg_max, den, rden = new("neg_max", [2, 1]), new("den", [2, 1]), new("rden", [2, 1])
        small = new("small", [KT, NB])
        seed = new("seed", [11])
        kq = [put(f"kq{i}", [4, DA], F32, r_ada + 8192 * i) for i in range(2)]
        r_more = r_ada + 16384
        kq += [put(f"kq{i}", [4, DA], F32, r_more + 8192 * (i - 2)) for i in range(2, 4)]
        r_sa = r_more + 16384
        bh = put("bh", [9, HD], F32, r_sa)
        sc = put("sc", [NG * P + NG], F32, r_sa + 2304)
        sall = put("sall", [NG, NB, NS], F32, r_sa + 2304 + 1568)
        prT = put("prT", [NG, NB * NS], F32, r_sa + 2304 + 1568 + 768)
        o_new = put("o_new", [2, HD], F32, r_sa + 2304 + 1568 + 1536)
        bh_tmp = put("bh_tmp", [NG, HD], F32, r_sa + 2304 + 1568 + 2048)
        bh_stat = put("bh_stat", [4], F32, r_sa + 2304 + 1568 + 2816)
        smp_rows = put("smp_rows", [DA], F32, r_sa + 2304 + 1568 + 2848)
        assert r_sa + 2304 + 1568 + 2848 + 2048 <= r_pt + 6144
        tail_rows = put("tail_rows", [D], F32, r_pt + 6144)
        g_hi, g_lo = put("g_hi", [FT, TC], F32R, r_ff), put("g_lo", [FT, TC], F32R, r_ff + FT * TC * 4)
        r_cv = r_ff + 2 * FT * TC * 4
        cv = [[put(f"cv{a}{b}", [TC], F32, r_cv + (2 * a + b) * 2080) for b in range(2)] for a in range(2)]
        gm = [put(f"gm{b}", [TC], F32, r_cv + (4 + b) * 2080) for b in range(2)]
        r_he = r_cv + 6 * 2080
        he = [[put(f"he{a}{b}", [2 + TC], F32, r_he + (2 * a + b) * 2112) for b in range(2)] for a in range(2)]
        r_cs = r_he + 4 * 2112
        hsc = put("hsc", [NB, 2 * FT], F32, r_cs)
        assert r_cs + NB * 2 * FT * 4 <= r_s
        hu_tail = put("hu_tail", [2 * FT, CONV_TAIL], F32, r_pt + 6144)
        conv_rows = put("conv_rows", [2 * NB, P], F32, r_ada)
        cst = put("cst", [2, NB * 2 * FT], F32, r_ada + 8192)
        hu_rows = put("hu_rows", [CONV_TAIL, P], F32, r_cv)
        y_rows = put("y_rows", [4, D], F32, r_ff)
        ys_rows = put("ys_rows", [D], F32, r_ff + 16384)

        acc = [psum("acc0", [P, 2, 512]), psum("acc1", [P, 2, 512])]
        psS = psum("psS", [P, 1024])
        psT = psum("psT", [P, 1024])
        psO, psA = [a[:, 0, 264:392] for a in acc], [a[:, 0, 392:392 + 2 * MC] for a in acc]
        psA0 = psS[:, 896:896 + 8 * MC]
        accv = [a[:, :, 0:HALF] for a in acc]
        acc_uses, used = {}, [0, 0]
        for name, counts in (("pairs", (PAIRS * 8, PAIRS * 7)), ("map", (4, 4)), ("pool", (4, 4)), ("att", (4, 4)), ("out", (4, 4)),
                             ("up", (FT, FT)), ("down", (3, 3)), ("last", (1, 1))):
            acc_uses[name] = tuple(used)
            used = [u + c for u, c in zip(used, counts)]

        def halves(x):
            return x.rearrange("p (a b) -> p a b", a=2)

        def halves_at(x, i):
            return x[:, ds(i, 1), :].rearrange("p o (a b) -> p o a b", a=2)

        raw_full = [sem(f"raw_full{i}") for i in range(RAW)]
        ada_full = [sem(f"ada_full{i}") for i in range(4)]
        kq_full = [sem(f"kq_full{i}") for i in range(4)]
        hi_ready, lo_ready = sem("hi_ready"), sem("lo_ready")
        unit_done, part_done = sem("unit_done"), sem("part_done")
        acc_free = [sem("acc_free0"), sem("acc_free1")]
        ada_done, ada_out = sem("ada_done"), sem("ada_out")
        c_loaded, vec_loaded, x_loaded, hist_loaded, conv_loaded = (
            sem(x) for x in ("c_loaded", "vec_loaded", "x_loaded", "hist_loaded", "conv_loaded"))
        pool_k, pool_step, pooled = sem("pool_constants"), sem("pool_step"), sem("pooled")
        dve_step = sem("dve_step")
        c_tanhed, c_ready, silu_turned, silu_out, vec_turned, vec_out = (
            sem(x) for x in ("c_tanhed", "c_ready", "silu_turned", "silu_out", "vec_turned", "vec_out"))
        x_turned, x_out, xs_turned, xs_out, hist_turned, hist_ready = (
            sem(x) for x in ("x_turned", "x_out", "xs_turned", "xs_out", "hist_turned", "hist_ready"))
        squared, summed, std_ready = sem("squared"), sem("summed"), sem("std_ready")
        u_ready, act_ready, act_split, x_upd = sem("u_ready"), sem("act_ready"), sem("act_split"), sem("x_upd")
        v_turned, k_turned, v_nat, k_nat = sem("v_turned"), sem("k_turned"), sem("v_nat"), sem("k_nat")
        v_out, k_out = sem("v_out"), sem("k_out")
        scored, maxed, expd, rdend, normed = sem("scored"), sem("maxed"), sem("expd"), sem("rdend"), sem("normed")
        turned, copied, weighted, o_hid, o_lod = sem("turned"), sem("copied"), sem("weighted"), sem("o_hid"), sem("o_lod")
        smpT_ready, rows_turned, smp_ready, smp_stored, smp_back, new_rows = (
            sem(x) for x in ("smpT_ready", "rows_turned", "smp_ready", "smp_stored", "smp_back", "new_rows"))
        tail_turned, tail_ready, tail_stored = sem("tail_turned"), sem("tail_ready"), sem("tail_stored")
        pooled_split, mixed_hid, merged, merged_split = sem("pooled_split"), sem("mixed_hid"), sem("merged"), sem("merged_split")
        prod_done, score_sum, smp_in, smp_max, smp_exp = sem("prod_done"), sem("score_sum"), sem("smp_in"), sem("smp_max"), sem("smp_exp")
        o_new_ready, smp_turned, pr_ready, v_used, smp_summed, os_hid, os_lod = (
            sem(x) for x in ("o_new_ready", "smp_turned", "pr_ready", "v_used", "smp_summed", "os_hid", "os_lod"))
        conv_turned, ssqd = sem("conv_turned"), sem("ssqd")
        tap1, taps, hu_tailed, gelud, gated, g_hid, g_lod = (
            sem(x) for x in ("tap1", "taps", "hu_tailed", "gelud", "gated", "g_hid", "g_lod"))
        hu_turned, hu_rowed, y_turned, ys_turned, y_ready, ys_ready, y_out = (
            sem(x) for x in ("hu_turned", "hu_rowed", "y_turned", "ys_turned", "y_ready", "ys_ready", "y_out"))
        copy_done, rows_done = sem("copy_done"), sem("rows_done")

        block = ctx.enter_context(nc.Block())

        @block.sync
        def _(sp):
            def unit(seg, it, pos, src, cols=UW):
                sp.wait_ge(lo_ready, st.number(seg, it, pos) - st.dist[seg, pos] + 1 + RAW)
                s = pos % RAW
                sp.dma_start(raw[:, s, 0:cols].rearrange("p (k n) -> p k n", n=src.shape[-1]), src).then_inc(raw_full[s], 16)

            def block_of(w, at, cols=P):
                return tiles(w)[:, :, ds(at, cols)]

            def ada(at, slot):
                sp.dma_start(ada_raw[:, slot, :].rearrange("p (k n) -> p k n", n=P), block_of(w_ada, at)).then_inc(ada_full[slot], 16)

            def shifted(g, kv):
                j, n = ((4, 1016), (16, 1022), (89, 736))[g]
                a = caches[g][kv][0].rearrange("b l s d -> b (l s d)")[:, DA:]
                o = outs["new"][g][kv][1][0].rearrange("b l s d -> b (l s d)")[:, 0:(WINS[g] - 1) * DA]
                return tuple(x.rearrange("b (e j n) -> e b j n", e=16, n=n) for x in (o, a)), j

            def copy(g, j):
                for kv in range(2):
                    (o, a), _ = shifted(g, kv)
                    sp.dma_start(o[:, :, ds(j, 1), :], a[:, :, ds(j, 1), :]).then_inc(copy_done, 16)

            sp.dma_start(c_rows[0:NB, :], ins["c_sample"]).then_inc(c_loaded, 16)
            sp.dma_start(c_rows[NB:MC, :], ins["c_prompt"]).then_inc(c_loaded, 16)
            rows = lambda x: x.rearrange("a (m c) -> (a m) c", c=P)
            sp.dma_start(vec_rows[0:48, 0, :], rows(ins["b_ada"])).then_inc(vec_loaded, 16)
            for i, n in enumerate(("g_pre_mix", "g_post_mix", "g_pre_ffn", "g_post_ffn", "pool_scale")):
                sp.dma_start(vec_rows[48 + 8 * i:56 + 8 * i, 0, :], rows(ins[n])).then_inc(vec_loaded, 16)
            wc = rows(ins["w_conv"][0])
            sp.dma_start(vec_rows[0:88, 1, :], wc[0:88, :]).then_inc(vec_loaded, 16)
            sp.dma_start(vec_rows[0:44, 2, :], wc[88:132, :]).then_inc(vec_loaded, 16)
            sp.dma_start(vec_rows[44:88, 2, :], rows(ins["b_conv"])).then_inc(vec_loaded, 16)
            for t in range(16):
                if t >= 4:
                    sp.wait_ge(ada_done, t - 3)
                ada(t * P, t % 4)

            with sp.Fori(0, PAIRS) as it:
                for k in range(TURN_UNITS):
                    if k < 9:
                        g, part = divmod(k, 3)
                        at = it * P + (D + part * NG * DA + g * DA)
                    elif k < 11:
                        at = it * (2 * P) + (k - 9) * P
                    else:
                        at = it * (2 * P) + (D + 3 * NG * DA + (k - 11) // 2 * D + (k - 11) % 2 * P)
                    unit("pairs", it, k, block_of(w_in, at))
                    if k in (1, 3, 4, 6, 7, 9, 10, 12, 13):
                        copy(2, it * 9 + (1, 3, 4, 6, 7, 9, 10, 12, 13).index(k))
                    if k in (0, 2, 5, 11):
                        copy(1, it * 4 + (0, 2, 5, 11).index(k))
                    if k == 8:
                        copy(0, it)
                        for i in range(4):
                            sp.wait_ge(ada_done, it * 8 + (16 + i - 3))
                            ada(it * (8 * P) + (16 + i) * P, i)
                    if k in (8, 11, 14):
                        g = (k - 8) // 3
                        for kv, (src, ready, done) in enumerate(((kN[:, :, :], k_nat, k_out), (vN[:, g, :, :], v_nat, v_out))):
                            sp.wait_ge(ready, it * 3 + (g + 1))
                            o = outs["new"][g][kv][0][0, 0].rearrange("t s d -> t (s d)")[:, ds((it + PAIRS) * P - DA, P)]
                            if g:
                                o = o.rearrange("(i r) c -> i r c", r=NR)
                            else:
                                src = src[:, 0, :] if kv == 0 else src[:, 3, :]
                            sp.dma_start(o, src).then_inc(done, 16)
                    if k == 14:
                        for i in range(4, 8):
                            sp.wait_ge(ada_done, it * 8 + (16 + i - 3))
                            ada(it * (8 * P) + (16 + i) * P, i - 4)

            for i in range(2):
                wm = ins["w_pool_map"][0, 2 * i:2 * i + 2].rearrange("g (k p) n -> p (g k) n", p=P)
                unit("mid", 0, i, wm)
            def load_kq(i):
                g, h = divmod(i, 2)
                b = 2 * (i % 2)
                if i >= 2:
                    sp.wait_ge(score_sum, i - 1)
                src = caches[g][0][0, 4 * h:4 * h + 4].rearrange("b (i e) s d -> i b e (s d)", e=DILS[g])[:, :, 0, :]
                sp.dma_start(kq[b][:, :, :], src).then_inc(kq_full[b], 16)
                sp.dma_start(kq[b + 1][:, :, :], scratch[3 * g, 4 * h:4 * h + 4, :].partition_broadcast(P)).then_inc(kq_full[b + 1], 16)

            def load_v(i):
                g, h = divmod(i, 2)
                if i < 4:
                    sp.wait_ge(score_sum, 6)
                else:
                    sp.wait_ge(v_used, i - 3)
                src = caches[g][1][0, 4 * h:4 * h + 4].rearrange("b (i e) s d -> i b e (s d)", e=DILS[g])[:, :, 0, :]
                sp.dma_start(kq[i % 4][:, :, :], src).then_inc(kq_full[i % 4], 16)

            def proj_pool(i):
                unit("mid", 0, 2 + i, block_of(ins["w_proj_pool"][0], i * P))

            def proj_att(i):
                unit("mid", 0, 10 + i, tiles(ins["w_proj_att"][0])[:, :, i * 2 * P:(i + 1) * 2 * P])

            proj_pool(0)
            proj_pool(1)
            sp.wait_ge(smp_ready, 1)
            sp.dma_start(scratch.rearrange("m b n -> (m b) n"), smp_rows[0:3 * NG * NB, :]).then_inc(smp_stored, 16)
            for g in range(NG):
                for kv in range(2):
                    o = outs["new"][g][kv][1][0, :, WINS[g] - 1].rearrange("b s d -> b (s d)")
                    r0 = (3 * g + 1 + kv) * NB
                    sp.dma_start(o, smp_rows[r0:r0 + NB, :]).then_inc(new_rows, 16)
            sp.wait_ge(smp_stored, 16)
            sp.dma_start(bh[0:NB * NS, :, :], scratch.rearrange("m b (h d) -> (b h) m d", d=HD)).then_inc(smp_back, 16)
            load_kq(0)
            load_kq(1)
            proj_pool(2)
            for i in range(4):
                proj_pool(3 + i)
                load_kq(2 + i)
            proj_pool(7)
            proj_att(0)
            for i in range(4):
                load_v(i)
            proj_att(1)
            load_v(4)
            load_v(5)
            proj_att(2)
            proj_att(3)
            sp.dma_start(outs["pool"][1][0, :, 0:POOL_HIST - 1], ins["state_pool"][0, :, 1:]).then_inc(rows_done, 16)
            sp.wait_ge(tail_ready, 1)
            sp.dma_start(outs["pool"][0][0, 0], tail_rows[0:POOL_HIST, :]).then_inc(tail_stored, 16)
            sp.dma_start(outs["pool"][1][0, :, POOL_HIST - 1], tail_rows[POOL_HIST:TAIL, :]).then_inc(tail_stored, 16)
            sp.dma_start(outs["conv"][1][0, :, 0], ins["state_conv"][0, :, 1]).then_inc(rows_done, 16)
            sp.wait_ge(v_used, 6)
            sp.dma_start(conv_rows[0:2 * FT, :, :], ins["state_conv"][0].rearrange("b j (m c) -> m (b j) c", c=P)).then_inc(conv_loaded, 16)
            with sp.Fori(0, 2) as it:
                for k in range(4):
                    unit("out", it, k, block_of(w_out, it * (4 * P) + k * P))
            with sp.Fori(0, FT // 2) as it:
                for k in range(4):
                    unit("up", it, k, block_of(w_up, it * (2 * P) + (k // 2 * P + k % 2 * FF)))
                    copy(2, it * 4 + (36 + k))
            def down(seg, it, m0):
                for k in range(6):
                    r0, r1 = 8 * (k % 3), min(8 * (k % 3) + 8, FT)
                    unit(seg, it, k, tiles(w_down)[:, r0:r1, ds(m0 + k // 3 * P, P)], cols=(r1 - r0) * P)
                    if seg == "down" and k % 2 == 1:
                        copy(2, it * 3 + (80 + k // 2))

            with sp.Fori(0, 3) as it:
                down("down", it, it * (2 * P))
            down("last", 0, 6 * P)
            sp.wait_ge(hu_rowed, 2)
            for j in range(CONV_TAIL):
                o = outs["conv"][0][0, 0, j] if j < 2 else outs["conv"][1][0, j - 2, 1]
                sp.dma_start(o.rearrange("(m c) -> m c", c=P), hu_rows[0:2 * FT, j, :]).then_inc(rows_done, 16)
            for q in range(4):
                sp.wait_ge(y_ready, 2 * q + 2)
                o = outs["y"][0][0].rearrange("(t p) n -> p t n", p=P)
                sp.dma_start(o[:, :, 2 * P * q:2 * P * q + 2 * P], y_rows[:, :, 2 * P * q:2 * P * q + 2 * P]).then_inc(y_out, 16)
            sp.wait_ge(ys_ready, 1)
            sp.dma_start(outs["y"][1].rearrange("b t n -> (b t) n"), ys_rows[0:NB, :]).then_inc(y_out, 16)
            sp.wait_ge(y_out, 16 * 5)
            sp.wait_ge(rows_done, 16 * (2 + CONV_TAIL))
            sp.wait_ge(new_rows, 16 * 2 * NG)
            sp.wait_ge(tail_stored, 32)
            sp.wait_ge(copy_done, 16 * 2 * (89 + 16 + 4))
            sp.wait_ge(k_out, 16 + 16 * 12)
            sp.wait_ge(v_out, 16 + 16 * 12)

        @block.gpsimd
        def _(pool):
            n = [0]

            def step(ins_):
                n[0] += 1
                ins_.then_inc(pool_step, 1)
                pool.wait_ge(pool_step, n[0])

            step(pool.memset(ident[:, :], 0.0))
            step(pool.memset(ones[:, :], 1.0))
            step(pool.memset(eps[:, :], EPS))
            pool.affine_select(out=ident[:, :], in_=ident[:, :], compare_op=ALU.not_equal, fill=1.0, base=0,
                               pattern=[[-1, P]], channel_multiplier=1).then_inc(pool_k, 1)
            step(pool.memset(mask[:, :, :], 0.0))
            step(pool.memset(pw[:, :, 0:16], 0.0))
            for t in range(16):
                step(pool.memset(inv_count[:, t:t + 1], 1.0 / (t + 1)))
            for r in range(NR):
                m0, m1 = mask[:, r, 0:TP], mask[:, r, TP:TP + P]
                step(pool.affine_select(out=m0, in_=m0, compare_op=ALU.is_ge, fill=NEG, base=r, pattern=[[-1, TP]], channel_multiplier=4))
                step(pool.affine_select(out=m0, in_=m0, compare_op=ALU.is_ge, fill=NEG, base=P - r, pattern=[[1, TP]], channel_multiplier=-4))
                step(pool.affine_select(out=m1, in_=m1, compare_op=ALU.is_ge, fill=NEG, base=0, pattern=[[-1, P]], channel_multiplier=1))
                m2 = mask[:, r, TP + P:TP + 2 * P]
                ins_ = pool.affine_select(out=m2, in_=m2, compare_op=ALU.is_ge, fill=NEG, base=0, pattern=[[-1, P]], channel_multiplier=1)
                if r == NR - 1:
                    ins_.then_inc(pool_k, 1)
                else:
                    step(ins_)

            for gi in range(4):
                win = 2 ** (gi + 1)
                pool.wait_ge(acc_free[0], 1 + 8 * gi + 6)
                t0 = 2 * gi
                step(pool.tensor_copy(u_tail[:, t0:t0 + 2, :], uT[:, t0:t0 + 2, TP - POOL_HIST:TC]))
                for t in (t0, t0 + 1):
                    u = uT[:, t, 0:TP]
                    step(pool.tensor_copy(pw[:, 0, 16:17], uT[:, t, 0:1]))
                    step(pool.tensor_tensor(pw[:, 0, 17:16 + TP], uT[:, t, 1:TP], uT[:, t, 0:TP - 1], ALU.add))
                    b = 0
                    for lv in range(1, gi + 1):
                        sh = 2 ** lv
                        step(pool.tensor_tensor(pw[:, 1 - b, 16:16 + TP], pw[:, b, 16:16 + TP], pw[:, b, 16 - sh:16 + TP - sh], ALU.add))
                        b = 1 - b
                    head = win - 1
                    step(pool.tensor_tensor(pw[:, b, 16:16 + head], pw[:, b, 16:16 + head], inv_count[:, 0:head], ALU.mult))
                    step(pool.tensor_scalar(pw[:, b, 16 + head:16 + TP], pw[:, b, 16 + head:16 + TP], 1.0 / win, 0.0, ALU.mult, ALU.add))
                    step(pool.tensor_tensor(u, pw[:, b, 16:16 + TP], u, ALU.subtract))
                if gi == 0:
                    pool.wait_ge(hist_ready, 1)
                us = uT[:, t0:t0 + 2, TP:TC]
                tmp = pw[:, 0, 16:32].rearrange("p (a b) -> p a b", a=2)
                step(pool.tensor_tensor(tmp, us, hist_sum[:, t0:t0 + 2, :], ALU.add))
                step(pool.tensor_scalar(tmp, tmp, 1.0 / win, 0.0, ALU.mult, ALU.add))
                pool.tensor_tensor(us, tmp, us, ALU.subtract).then_inc(pooled, 1)
                if gi < 3:
                    pool.wait_ge(pooled, gi + 1)

            for i in range(6):
                b = 2 * (i % 2)
                pool.wait_ge(kq_full[b], 16 * (i // 2 + 1))
                pool.wait_ge(kq_full[b + 1], 16 * (i // 2 + 1))
                pool.tensor_tensor(kq[b][:, :, :], kq[b][:, :, :], kq[b + 1][:, :, :], ALU.mult).then_inc(prod_done, 1)

            pool.wait_ge(tail_stored, 32)
            with pool.Fori(0, FT // 2) as it:
                for k in range(4):
                    pool.wait_ge(acc_free[k % 2], it * 2 + (acc_uses["up"][k % 2] + k // 2 + 2))
                    m, half = k // 2, k % 2
                    pool.tensor_copy(hu_tail[:, ds(it * 2 + (m + half * FT), 1), :], he[half][m][:, 2 + TP - 2:2 + TC].unsqueeze(1)).then_inc(hu_tailed, 1)

        @block.scalar
        def _(act):
            def split(seg, it, pos):
                units = SEGMENTS[seg][1]
                s = 0 if pos == units else pos
                cols = 6 * P if seg in ("down", "last") and pos in (2, 5) else UW
                act.wait_ge(raw_full[s % RAW], st.fill(seg, it, pos) * 16)
                back = 1 if pos == units and units % 2 else 2
                if pos != 1:
                    act.wait_ge(unit_done, st.number(seg, it, pos) - back + 1)
                act.activation(w_hi[:, s % HL, 0:cols], raw[:, s % RAW, 0:cols], ACT.Copy).then_inc(hi_ready, 1)

            act.dma_start(x_rows[:, :, :], ins["x_prompt"][0].rearrange("(t p) n -> p t n", p=P)).then_inc(x_loaded, 16)
            act.dma_start(xs_rows[0:NB, :], ins["x_sample"].rearrange("b t n -> (b t) n")).then_inc(x_loaded, 16)
            act.dma_start(hist_rows[0:NB * POOL_HIST, :], ins["state_pool"][0].rearrange("b t n -> (b t) n")).then_inc(hist_loaded, 16)
            act.wait_ge(c_loaded, 32)
            act.activation(c_tanh[0:MC, :], c_rows[0:MC, :], ACT.Tanh, scale=0.5).then_inc(c_tanhed, 1)
            act.wait_ge(silu_turned, 1)
            act.activation(siluT[:, :, :].rearrange("p a b -> p (a b)"), acc[1][:, 0, 0:KT * MC], ACT.Copy, scale=0.5).then_inc(silu_out, 1)
            act.wait_ge(vec_turned, 1)
            act.activation(vec[:, :], psS[:, 96:96 + 3 * 88], ACT.Copy).then_inc(vec_out, 1)
            for k in range(KT):
                act.wait_ge(x_turned, k + 1)
                act.activation(xT[:, k, 0:TP], psT[:, 512 * (k % 2):512 * (k % 2) + 512], ACT.Copy).then_inc(x_out, 1)
            act.wait_ge(xs_turned, 1)
            act.activation(xT[:, :, TP:TC], psS[:, 384:384 + KT * NB].rearrange("p (a b) -> p a b", a=KT), ACT.Copy).then_inc(xs_out, 1)
            act.wait_ge(xs_out, 1)

            def squares(before):
                for k in range(KT):
                    if before:
                        act.wait_ge(x_upd, k + 1)
                    if k >= 2:
                        act.wait_ge(summed, before + k - 1)
                    act.activation(sq[:, k % 2, :], xT[:, k, :], ACT.Square).then_inc(squared, 1)

            def root(where, sums):
                act.wait_ge(summed, sums)
                act.activation(halves(rs[:, :]), where, ACT.Sqrt, bias=eps[:, :], scale=1.0 / D).then_inc(std_ready, 1)

            norm_view = psS[:, :].rearrange("p (a b) -> p a b", a=2)[:, :, 0:HALF]
            squares(0)
            root(accv[1], 8)
            def split_act(k):
                act.wait_ge(u_ready, k + 1)
                act.activation(act_hi[:, k, :], uT[:, k, :], ACT.Copy).then_inc(act_ready, 1)

            for k in range(KT):
                split_act(k)
            act.wait_ge(raw_full[0], 16)
            act.activation(w_hi[:, 0, :], raw[:, 0, :], ACT.Copy).then_inc(hi_ready, 1)

            with act.Fori(0, PAIRS) as it:
                for what, k in TURN:
                    if what == "unit":
                        split("pairs", it, k + 1)
                        if k < 9 and k % 3 == 2:
                            continue
                        b = k % 2
                        act.wait_ge(unit_done, it * TURN_UNITS + (k + 1))
                        if k < 9:
                            act.activation(halves(qkvT[:, k, :]), accv[b], ACT.Copy, scale=0.125 if k % 3 == 0 else 1.0).then_inc(acc_free[b], 1)
                            continue
                        t = (k - 9) % 2
                        dst = halves_at((uT, thp, tha)[(k - 9) // 2], it * 2 + t)
                        act.activation(dst, accv[b].unsqueeze(1), ACT.Copy if k < 11 else ACT.Tanh, scale=1.0 if k < 11 else 0.5).then_inc(acc_free[b], 1)
                    elif what == "turn":
                        act.wait_ge(k_turned, it * 3 + (k + 1))
                        act.wait_ge(k_out, it * 48 + (16 * k + 16))
                        w = 1 if k == 0 else 4
                        act.activation(kN[:, 0:w, :].rearrange("p a b -> p (a b)"), psT[:, 512:512 + w * P], ACT.Copy).then_inc(k_nat, 1)
                    elif what == "step":
                        if 0 <= k - 2 < TASKS:
                            j = k - 2
                            r, h = j // 2, j % 2
                            rows = slice(64 * h, 64 * h + 64)
                            act.wait_ge(weighted, it * TASKS + (j + 1))
                            dst = o_hi[rows, ds(it, 1), 0:TP].rearrange("p o (i r) -> p o r i", r=NR)[:, :, r, :]
                            act.activation(dst, psO[IDLE[what, k]][rows, :].unsqueeze(1), ACT.Copy).then_inc(o_hid, 1)
                        if 0 <= k - 1 < TASKS:
                            j = k - 1
                            act.wait_ge(turned, it * TASKS + (j + 1))
                            if j >= 2:
                                act.wait_ge(weighted, it * TASKS + (j - 1))
                            act.activation(PT[:, j % 2, :], psT[:, 0:768], ACT.Copy).then_inc(copied, 1)
                        if k < TASKS:
                            act.wait_ge(maxed, it * TASKS + (k + 1))
                            act.activation(S[:, k % 2, :], S[:, k % 2, :], ACT.Exp, bias=neg_max[:, k % 2, :], scale=-1.0,
                                           accum_out=den[:, k % 2, :]).then_inc(expd, 1)

            for q in range(4):
                act.wait_ge(pooled, q + 1)
                if q == 0:
                    act.wait_ge(unit_done, 60)
                act.activation(act_hi[:, 2 * q:2 * q + 2, :], uT[:, 2 * q:2 * q + 2, :], ACT.Copy).then_inc(act_ready, 1)
            act.wait_ge(rows_turned, 1)
            act.activation(smp_rows[0:3 * NG * NB, :], psT[0:3 * NG * NB, 0:DA], ACT.Copy).then_inc(smp_ready, 1)
            act.wait_ge(tail_turned, 1)
            act.activation(tail_rows[0:TAIL, :], psS[0:TAIL, :], ACT.Copy).then_inc(tail_ready, 1)
            act.wait_ge(pooled_split, 4)
            for pos in range(2):
                split("mid", 0, pos + 1)
                for q in range(4):
                    i = 4 * pos + q
                    act.wait_ge(*((part_done, 3 * pos + q + 1) if q < 3 else (unit_done, 61 + pos)))
                    act.activation(halves(mix_hi[:, i, :]), accv[i % 2], ACT.Identity, scale=vec[:, 80 + i:81 + i]).then_inc(mixed_hid, 1)
            for pos in range(2, 10):
                split("mid", 0, pos + 1)
                if pos == 8:
                    act.wait_ge(smp_max, 1)
                    act.activation(sc[0:NB * NS, :], sc[0:NB * NS, :], ACT.Exp, bias=bh_stat[0:NB * NS, 0:1], scale=1.0,
                                   accum_out=bh_stat[0:NB * NS, 1:2]).then_inc(smp_exp, 1)
                if pos == 9:
                    act.wait_ge(smp_summed, 1)
                    for h in range(2):
                        rows = slice(HD * h, HD * h + HD)
                        src = psT[rows, 0:NB * NS].rearrange("p (b q h) -> p q b h", b=NB, h=2)[:, :, :, h]
                        act.activation(o_hi[rows, :, TP:TC], src, ACT.Copy).then_inc(os_hid, 1)
            for pos in range(10, 14):
                split("mid", 0, pos + 1)
                for q in range(2):
                    i = 2 * (pos - 10) + q
                    act.wait_ge(merged, i + 1)
                    act.activation(act_hi[:, i, :], tha[:, i, :], ACT.Copy, scale=0.5).then_inc(act_ready, 1)

            with act.Fori(0, 2) as it:
                for k in range(4):
                    split("out", it, k + 1)
                    act.wait_ge(unit_done, it * 4 + (74 + k + 1))
                    act.activation(halves_at(mixT, it * 4 + k), accv[k % 2].unsqueeze(1), ACT.Copy)
                    act.wait_ge(ssqd, it * 4 + (k + 1))
                    act.activation(halves(sq[:, k % 2, :]), accv[k % 2], ACT.Square).then_inc(acc_free[k % 2], 1)
            root(norm_view, 9)
            squares(9)
            root(norm_view, 17)
            for k in range(KT):
                act.wait_ge(u_ready, KT + k + 1)
                act.activation(act_hi[:, k, :], norm_u[:, k, :], ACT.Copy).then_inc(act_ready, 1)

            with act.Fori(0, FT // 2) as it:
                for k in range(4):
                    m, half = k // 2, k % 2
                    split("up", it, k + 1)
                    act.wait_ge(unit_done, it * 4 + (82 + k + 1))
                    w2 = vec[:, ds(it * 2 + (176 + m + half * FT), 1)]
                    bc = vec[:, ds(it * 2 + (220 + m + half * FT), 1)]
                    act.wait_ge(taps, it * 4 + (k + 1))
                    act.wait_ge(hu_tailed, it * 4 + (k + 1))
                    act.activation(halves(he[half][m][:, 2:2 + TC]), accv[k % 2], ACT.Copy)
                    act.activation(halves(cv[half][m][:, :]), accv[k % 2], ACT.Identity, bias=bc, scale=w2).then_inc(acc_free[k % 2], 1)
                    if half == 1:
                        act.wait_ge(taps, it * 4 + (4 + 2 * m + 1))
                        act.wait_ge(g_lod, it * 2 + (m + 1))
                        act.activation(gm[m][:, :], cv[0][m][:, :], ACT.Gelu_apprx_tanh).then_inc(gelud, 1)
                        act.wait_ge(gated, it * 2 + (m + 1))
                        act.activation(g_hi[:, ds(it * 2 + m, 1), :].rearrange("p o n -> p (o n)"), gm[m][:, :], ACT.Copy).then_inc(g_hid, 1)

            for i, t in enumerate((psS, psT)):
                act.wait_ge(hu_turned, i + 1)
                act.activation(hu_rows[0:2 * FT, 5 * i:5 * i + 5, :].rearrange("p a b -> p (a b)"), t[0:2 * FT, 0:5 * P], ACT.Copy).then_inc(hu_rowed, 1)

            def down(seg, it, m0):
                for k in range(6):
                    if not (seg == "last" and k == 5):
                        split(seg, it, k + 1)
                    if k % 3 == 2:
                        b = k // 3
                        act.wait_ge(unit_done, it * 6 + (st.first[seg] + k + 1))
                        act.activation(halves_at(ffn, m0 + b), accv[b].unsqueeze(1), ACT.Copy)
                        act.wait_ge(ssqd, it * 2 + ((9 if seg == "down" else 15) + b))
                        act.activation(halves(sq[:, b, :]), accv[b], ACT.Square).then_inc(acc_free[b], 1)

            with act.Fori(0, 3) as it:
                down("down", it, it * 2)
            down("last", 0, 6)
            root(norm_view, 18)
            for k in range(KT):
                act.wait_ge(y_turned, k + 1)
                act.activation(y_rows[:, :, k * P:(k + 1) * P], psT[:, 512 * (k % 2):512 * (k % 2) + 512].rearrange("p (a b) -> p a b", a=4),
                               ACT.Copy).then_inc(y_ready, 1)
            act.wait_ge(ys_turned, 1)
            act.activation(ys_rows[0:NB, :], acc[0][0:NB, :, :].rearrange("p a b -> p (a b)"), ACT.Copy).then_inc(ys_ready, 1)

        @block.vector
        def _(dve):
            n = [0]

            def mark(ins_):
                n[0] += 1
                ins_.then_inc(dve_step, 1)
                return n[0]

            def mine():
                dve.wait_ge(dve_step, n[0])

            def split(seg, it, pos):
                units = SEGMENTS[seg][1]
                s = 0 if pos == units else pos
                cols = 6 * P if seg in ("down", "last") and pos in (2, 5) else UW
                dve.wait_ge(hi_ready, st.number(seg, it, pos) + 1)
                dve.tensor_tensor(w_lo[:, s % HL, 0:cols], raw[:, s % RAW, 0:cols], w_hi[:, s % HL, 0:cols].bitcast(F32), ALU.subtract).then_inc(lo_ready, 1)

            for i, (s, c) in enumerate(((acc_free[0], 1), (acc_free[1], 1), (lo_ready, RAW), (o_lod, 1), (k_out, 16), (v_out, 16), (ssqd, 1), (taps, 4),
                         (hu_tailed, 4), (g_lod, 2))):
                dve.memset(seed[:, i:i + 1], 0.0).then_inc(s, c)
            dve.wait_ge(c_tanhed, 1)
            dve.scalar_tensor_tensor(c_silu[0:MC, :], c_tanh[0:MC, :], 1.0, c_rows[0:MC, :], ALU.add, ALU.mult).then_inc(c_ready, 1)
            dve.wait_ge(pool_k, 1)
            mark(dve.tensor_reduce(ind4[:, 0, :], ident[:, :].rearrange("p (a b) -> p b a", b=4), AX_X, ALU.add))
            mine()
            mark(dve.tensor_scalar(ind4[:, 1, :], ind4[:, 0, :], -NEG, NEG, ALU.mult, ALU.add))
            mine()
            dve.wait_ge(pool_k, 2)
            for r in range(NR):
                m2 = mask[:, r, TP + P:TP + 2 * P].rearrange("p (a b) -> p a b", b=4)
                mark(dve.tensor_tensor(m2, m2, ind4[:, 1, :].unsqueeze(1).to_broadcast([P, 32, 4]), ALU.add))
            dve.wait_ge(hist_turned, 1)
            for gi in range(4):
                win = 2 ** (gi + 1)
                src = acc[0][:, gi // 2, (gi % 2) * 240:(gi % 2) * 240 + 240].rearrange("p (k b t) -> p k b t", k=2, b=NB)[:, :, :, 16 - win:]
                ins_ = dve.tensor_reduce(hist_sum[:, 2 * gi:2 * gi + 2, :], src, AX_X, ALU.add)
            ins_.then_inc(hist_ready, 1)

            def ada_evac(t0, count, src, n):
                dve.wait_ge(ada_done, count)
                dve.tensor_tensor(mod[:, ds(t0, n), :], src.rearrange("p (a b) -> p a b", a=n),
                                  vec[:, ds(t0, n)].unsqueeze(2).to_broadcast([P, n, MC]), ALU.add).then_inc(ada_out, 1)

            dve.wait_ge(vec_out, 1)
            ada_evac(0, 8, psA0, 8)
            dve.wait_ge(std_ready, 1)
            mark(dve.reciprocal(rs[:, :], rs[:, :]))
            ada_evac(8, 16, psA0, 8)
            dve.wait_ge(ada_out, 2)

            def gains(dst, scale0, g0, plus):
                v = vec[:, g0:g0 + 8].unsqueeze(2).to_broadcast([P, 8, MC])
                return mark(dve.scalar_tensor_tensor(dst[:, :, :], mod[:, scale0:scale0 + 8, :], plus, v, ALU.add, ALU.mult))

            gains(a_m, 8, 48, 1.0)
            mine()

            def modulated(u, a, shift0, base):
                us, xs = u[:, :, TP:TC], xT[:, :, TP:TC]
                mark(dve.tensor_tensor(small[:, :, :], xs, rs[:, TP:TC].unsqueeze(1).to_broadcast([P, KT, NB]), ALU.mult))
                mine()
                mark(dve.tensor_tensor(small[:, :, :], small[:, :, :], a[:, :, 0:NB], ALU.mult))
                mine()
                mark(dve.tensor_tensor(us, small[:, :, :], mod[:, shift0:shift0 + 8, 0:NB], ALU.add))
                for k in range(KT + 1):
                    if k < KT:
                        mark(dve.tensor_tensor(u[:, k, 0:TP], xT[:, k, 0:TP], rs[:, 0:TP], ALU.mult))
                        mine()
                        dve.tensor_scalar(u[:, k, 0:TP], u[:, k, 0:TP], a[:, k, PROMPT:MC], mod[:, shift0 + k, PROMPT:MC], ALU.mult, ALU.add).then_inc(u_ready, 1)
                    if k >= 1:
                        dve.wait_ge(act_ready, base + k)
                        dve.tensor_tensor(act_lo[:, k - 1, :], u[:, k - 1, :], act_hi[:, k - 1, :].bitcast(F32), ALU.subtract).then_inc(act_split, 1)

            modulated(uT, a_m, 0, 0)
            split("pairs", 0, 0)

            with dve.Fori(0, PAIRS) as it:
                for what, k in TURN:
                    if what == "unit":
                        split("pairs", it, k + 1)
                        if k < 9 and k % 3 == 2:
                            b = k % 2
                            dve.wait_ge(unit_done, it * TURN_UNITS + (k + 1))
                            dve.tensor_copy(halves(qkvT[:, k, :]), accv[b]).then_inc(acc_free[b], 1)
                    elif what == "turn":
                        dve.wait_ge(v_turned, it * 3 + (k + 1))
                        dve.wait_ge(v_out, it * 48 + 16)
                        dve.tensor_copy(vN[:, k, :, :].rearrange("p a b -> p (a b)"), psT[:, 0:512]).then_inc(v_nat, 1)
                        if k == 2:
                            dve.tensor_copy(smpT[:, ds(it, 1), :, :], qkvT[:, :, TP:TC].unsqueeze(1)).then_inc(smpT_ready, 1)
                    elif what == "step":
                        if 0 <= k - 2 < TASKS:
                            j = k - 2
                            r, h = j // 2, j % 2
                            rows = slice(64 * h, 64 * h + 64)
                            dve.wait_ge(o_hid, it * TASKS + (j + 1))
                            hi, lo = (x[rows, ds(it, 1), 0:TP].rearrange("p o (i r) -> p o r i", r=NR)[:, :, r, :] for x in (o_hi, o_lo))
                            dve.tensor_tensor(lo, psO[IDLE[what, k]][rows, :].unsqueeze(1), hi.bitcast(F32), ALU.subtract).then_inc(o_lod, 1)
                        if k < TASKS:
                            dve.wait_ge(scored, it * TASKS + (k + 1))
                            if k >= 2:
                                dve.wait_ge(turned, it * TASKS + (k - 1))
                            dve.memset(seed[:, 10:11], 0.0)
                            dve.tensor_tensor_reduce(S[:, k % 2, :], psS[:, 0:768], mask[:, k // 2, :], -1.0, BIG, ALU.add, ALU.min,
                                                     neg_max[:, k % 2, :]).then_inc(maxed, 1)
                            dve.wait_ge(expd, it * TASKS + (k + 1))
                            dve.reciprocal(rden[:, k % 2, :], den[:, k % 2, :]).then_inc(rdend, 1)
                            dve.wait_ge(rdend, it * TASKS + (k + 1))
                            dve.tensor_scalar(S[:, k % 2, :], S[:, k % 2, :], rden[:, k % 2, :], None, ALU.mult).then_inc(normed, 1)
                    elif what == "ada":
                        ada_evac(it * 8 + (16 + k), it * 8 + (18 + k), psA[IDLE[what, k]], 2)

            for q in range(4):
                dve.wait_ge(act_ready, 8 + q + 1)
                dve.tensor_tensor(act_lo[:, 2 * q:2 * q + 2, :], uT[:, 2 * q:2 * q + 2, :], act_hi[:, 2 * q:2 * q + 2, :].bitcast(F32),
                                  ALU.subtract).then_inc(pooled_split, 1)
            dve.wait_ge(ada_out, 2 + 4 * PAIRS)
            gains(gg_m, 16, 56, 0.0)
            gains(a_f, 32, 64, 1.0)
            gains(gg_f, 40, 72, 0.0)
            for pos in range(2):
                split("mid", 0, pos + 1)
                for q in range(4):
                    i = 4 * pos + q
                    dve.wait_ge(mixed_hid, i + 1)
                    dve.scalar_tensor_tensor(halves(mix_lo[:, i, :]), accv[i % 2], vec[:, 80 + i:81 + i], halves(mix_hi[:, i, :].bitcast(F32)), ALU.mult, ALU.subtract).then_inc(acc_free[i % 2], 1)

            def sample_scores(i):
                g, h = divmod(i, 2)
                dve.wait_ge(prod_done, i + 1)
                src = kq[2 * (i % 2)][:, :, :].rearrange("p b (s d) -> p b s d", d=HD)
                dve.tensor_reduce(sall[:, g, 4 * h:4 * h + 4, :], src, AX_X, ALU.add).then_inc(score_sum, 1)

            def sample_softmax():
                bs = slice(0, NB * NS)
                dve.wait_ge(smp_back, 16)
                parts = bh[bs, :, :].rearrange("p (g t) d -> p t g d", t=3)
                mark(dve.tensor_tensor(bh_tmp[bs, :, :], parts[:, 0], parts[:, 1], ALU.mult))
                mine()
                mark(dve.tensor_reduce(sc[bs, NG * P:], bh_tmp[bs, :, :], AX_X, ALU.add))
                dve.wait_ge(smp_in, 1)
                mark(dve.tensor_copy(sc[bs, 0:NG * P], psT[bs, 512:512 + NG * P]))
                mine()
                mark(dve.tensor_reduce(bh_stat[bs, 2:3], sc[bs, :], AX_X, ALU.max))
                mine()
                dve.tensor_scalar(bh_stat[bs, 0:1], bh_stat[bs, 2:3], -1.0, None, ALU.mult).then_inc(smp_max, 1)
                dve.wait_ge(smp_exp, 1)
                mark(dve.reciprocal(bh_stat[bs, 3:4], bh_stat[bs, 1:2]))
                mine()
                mark(dve.tensor_scalar(sc[bs, :], sc[bs, :], bh_stat[bs, 3:4], None, ALU.mult))
                mine()
                mark(dve.tensor_scalar(o_new[bs, 0, :], bh[bs, 2, :], sc[bs, NG * P:NG * P + 1], None, ALU.mult))
                for g in range(1, NG):
                    mine()
                    mark(dve.scalar_tensor_tensor(o_new[bs, 0, :], bh[bs, 3 * g + 2, :], sc[bs, NG * P + g:NG * P + g + 1],
                                                  o_new[bs, 0, :], ALU.mult, ALU.add))
                mine()
                dve.tensor_copy(o_new[bs, 1, :], o_new[bs, 0, :]).then_inc(o_new_ready, 1)

            for pos in range(2, 10):
                split("mid", 0, pos + 1)
                if pos <= 7:
                    sample_scores(pos - 2)
                if pos == 8:
                    sample_softmax()
                if pos == 9:
                    dve.wait_ge(smp_turned, 1)
                    dve.tensor_copy(prT[:, :, :].rearrange("p a b -> p (a b)"), psT[:, 0:NG * NB * NS]).then_inc(pr_ready, 1)
                m = pos - 2
                dve.wait_ge(unit_done, 62 + m + 1)
                v = halves(thp[:, m, :])
                dve.scalar_tensor_tensor(v, v, 1.0, accv[m % 2], ALU.add, ALU.mult).then_inc(acc_free[m % 2], 1)
                if pos == 9:
                    dve.wait_ge(os_hid, 2)
                    for h in range(2):
                        rows = slice(HD * h, HD * h + HD)
                        src = psT[rows, 0:NB * NS].rearrange("p (b q h) -> p q b h", b=NB, h=2)[:, :, :, h]
                        dve.tensor_tensor(o_lo[rows, :, TP:TC], src, o_hi[rows, :, TP:TC].bitcast(F32), ALU.subtract).then_inc(os_lod, 1)

            def merge_lo(i):
                dve.wait_ge(act_ready, 12 + i + 1)
                dve.scalar_tensor_tensor(act_lo[:, i, :], tha[:, i, :], 0.5, act_hi[:, i, :].bitcast(F32), ALU.mult, ALU.subtract).then_inc(merged_split, 1)

            for pos in range(10, 14):
                split("mid", 0, pos + 1)
                for q in range(2):
                    i = 2 * (pos - 10) + q
                    if i >= 1:
                        merge_lo(i - 1)
                    dve.wait_ge(*((part_done, 6 + pos - 9) if q == 0 else (unit_done, 71 + pos - 10)))
                    v = halves(tha[:, i, :])
                    dve.scalar_tensor_tensor(v, v, 1.0, accv[i % 2], ALU.add, ALU.mult).then_inc(acc_free[i % 2], 1)
                    dve.wait_ge(acc_free[i % 2], acc_uses["att"][i % 2] + i // 2 + 2)
                    dve.tensor_tensor(tha[:, i, :], tha[:, i, :], thp[:, i, :], ALU.add).then_inc(merged, 1)
            merge_lo(7)

            dve.wait_ge(conv_turned, 1)
            for j in range(2):
                src = psT[:, 512 * j:512 * j + NB * 2 * FT].rearrange("p (b m) -> p b m", b=NB)
                w = vec[:, 88 + 44 * j:132 + 44 * j].unsqueeze(1).to_broadcast([P, NB, 2 * FT])
                mark(dve.tensor_tensor(cst[:, j, :].rearrange("p (b m) -> p b m", b=NB), src, w, ALU.mult))
            mine()
            mark(dve.tensor_tensor(hsc[:, :, :].rearrange("p b m -> p (b m)"), cst[:, 0, :], cst[:, 1, :], ALU.add))
            dve.wait_ge(smp_stored, 16)
            dve.wait_ge(new_rows, 16 * 2 * NG)
            mark(dve.memset(ssq[:, :], 0.0))
            mine()

            with dve.Fori(0, 2) as it:
                for k in range(4):
                    split("out", it, k + 1)
                    dve.wait_ge(acc_free[k % 2], it * 2 + (acc_uses["out"][k % 2] + k // 2 + 2))
                    dve.wait_ge(ssqd, it * 4 + (k + 1))
                    dve.tensor_tensor(ssq[:, :], ssq[:, :], sq[:, k % 2, :], ALU.add).then_inc(ssqd, 1)

            def post_norm(src, gg, roots):
                dve.wait_ge(std_ready, roots)
                mark(dve.reciprocal(rs[:, :], rs[:, :]))
                mine()
                mark(dve.tensor_tensor(small[:, :, :], src[:, :, TP:TC], rs[:, TP:TC].unsqueeze(1).to_broadcast([P, KT, NB]), ALU.mult))
                mine()
                mark(dve.tensor_tensor(small[:, :, :], small[:, :, :], gg[:, :, 0:NB], ALU.mult))
                mine()
                mark(dve.tensor_tensor(xT[:, :, TP:TC], xT[:, :, TP:TC], small[:, :, :], ALU.add))
                for k in range(KT + 1):
                    if k < KT:
                        mark(dve.scalar_tensor_tensor(src[:, k, 0:TP], src[:, k, 0:TP], gg[:, k, PROMPT:MC], rs[:, 0:TP], ALU.mult, ALU.mult))
                        mine()
                        dve.tensor_tensor(xT[:, k, 0:TP], xT[:, k, 0:TP], src[:, k, 0:TP], ALU.add).then_inc(x_upd, 1)

            post_norm(mixT, gg_m, 2)
            for h in (*he[0], *he[1]):
                mark(dve.memset(h[:, 0:2], 0.0))
            dve.wait_ge(std_ready, 3)
            mark(dve.reciprocal(rs[:, :], rs[:, :]))
            mine()
            modulated(norm_u, a_f, 24, 20)
            mark(dve.memset(ssq[:, :], 0.0))
            mine()

            with dve.Fori(0, FT // 2) as it:
                for k in range(4):
                    m, half = k // 2, k % 2
                    split("up", it, k + 1)
                    dve.wait_ge(acc_free[k % 2], it * 2 + (acc_uses["up"][k % 2] + k // 2 + 2))
                    c, h = cv[half][m], he[half][m]
                    w0, w1 = (vec[:, ds(it * 2 + (88 + 44 * j + m + half * FT), 1)] for j in range(2))
                    dve.tensor_tensor(c[:, TP:TC], c[:, TP:TC], hsc[:, :, ds(it * 2 + (m + half * FT), 1)].rearrange("p b o -> p (b o)"), ALU.add)
                    dve.scalar_tensor_tensor(c[:, 0:TP], h[:, 1:1 + TP], w1, c[:, 0:TP], ALU.mult, ALU.add).then_inc(tap1, 1)
                    dve.wait_ge(tap1, it * 4 + (k + 1))
                    dve.scalar_tensor_tensor(c[:, 0:TP], h[:, 0:TP], w0, c[:, 0:TP], ALU.mult, ALU.add).then_inc(taps, 1)
                    if half == 1:
                        dve.wait_ge(gelud, it * 2 + (m + 1))
                        dve.wait_ge(taps, it * 4 + (4 + k + 1))
                        dve.tensor_tensor(gm[m][:, :], gm[m][:, :], c[:, :], ALU.mult).then_inc(gated, 1)
                        dve.wait_ge(g_hid, it * 2 + (m + 1))
                        hi, lo = (x[:, ds(it * 2 + m, 1), :].rearrange("p o n -> p (o n)") for x in (g_hi, g_lo))
                        dve.tensor_tensor(lo, gm[m][:, :], hi.bitcast(F32), ALU.subtract).then_inc(g_lod, 1)

            def down(seg, it):
                for k in range(6):
                    if not (seg == "last" and k == 5):
                        split(seg, it, k + 1)
                    if k % 3 == 2:
                        b = k // 3
                        dve.wait_ge(acc_free[b], it + (acc_uses[seg][b] + 2))
                        dve.wait_ge(ssqd, it * 2 + ((9 if seg == "down" else 15) + b))
                        dve.tensor_tensor(ssq[:, :], ssq[:, :], sq[:, b, :], ALU.add).then_inc(ssqd, 1)

            with dve.Fori(0, 3) as it:
                down("down", it)
            down("last", 0)
            post_norm(ffn, gg_f, 4)

        @block.tensor
        def _(pe):
            def blocks(b, s, pairs, hi, lo, first=True, last=True):
                for i, (blk, t) in enumerate(pairs):
                    wh, wl = w_hi[:, s, blk * P:(blk + 1) * P], w_lo[:, s, blk * P:(blk + 1) * P]
                    for j, (w, x) in enumerate(((wh, hi), (wh, lo), (wl, hi))):
                        for half in range(2):
                            ins_ = pe.matmul(acc[b][:, half, 0:HALF], w, x[:, t, half * HALF:(half + 1) * HALF],
                                             start=first and i == 0 and j == 0, stop=last and i == len(pairs) - 1 and j == 2)
                return ins_

            def ready(seg, it, pos):
                pe.wait_ge(lo_ready, st.number(seg, it, pos) + 1 + RAW)

            def free(b, uses):
                pe.wait_ge(acc_free[b], uses + 1)

            def ada(slot, where, col):
                for k in range(KT):
                    ins_ = pe.matmul(where[:, col * MC:(col + 1) * MC], ada_raw[:, slot, k * P:(k + 1) * P], siluT[:, k, :],
                                     start=k == 0, stop=k == KT - 1)
                ins_.then_inc(ada_done, 1)

            pe.wait_ge(pool_k, 1)
            pe.wait_ge(c_ready, 1)
            for k in range(KT):
                ins_ = pe.transpose(acc[1][:, 0, k * MC:(k + 1) * MC], c_silu[0:MC, k * P:(k + 1) * P], ident[0:MC, 0:MC])
            ins_.then_inc(silu_turned, 1)
            pe.wait_ge(vec_loaded, 16 * 9)
            for i in range(3):
                ins_ = pe.transpose(psS[:, 96 + 88 * i:184 + 88 * i], vec_rows[0:88, i, :], ident[0:88, 0:88])
            ins_.then_inc(vec_turned, 1)
            pe.wait_ge(x_loaded, 32)
            pe.wait_ge(silu_out, 1)
            for k in range(KT):
                if k >= 2:
                    pe.wait_ge(x_out, k - 1)
                for t in range(4):
                    at = 512 * (k % 2) + t * P
                    ins_ = pe.transpose(psT[:, at:at + P], x_rows[:, t, k * P:(k + 1) * P], ident[:, :])
                ins_.then_inc(x_turned, 1)
                pe.wait_ge(ada_full[k % 4], 16 * (k // 4 + 1))
                ada(k % 4, psA0, k)
            for k in range(KT):
                ins_ = pe.transpose(psS[:, 384 + k * NB:384 + (k + 1) * NB], xs_rows[0:NB, k * P:(k + 1) * P], ident[0:NB, 0:NB])
            ins_.then_inc(xs_turned, 1)
            pe.wait_ge(hist_loaded, 16)
            for k in range(KT):
                at = (k % 4) * NB * POOL_HIST
                ins_ = pe.transpose(acc[0][:, k // 4, at:at + NB * POOL_HIST], hist_rows[0:NB * POOL_HIST, k * P:(k + 1) * P],
                                    ident[0:NB * POOL_HIST, 0:NB * POOL_HIST])
            ins_.then_inc(hist_turned, 1)

            def sum_squares(src, where, start=True, stop=True):
                for half in range(2):
                    ins_ = pe.matmul(where[half], ones[:, :], src[:, half * HALF:(half + 1) * HALF], start=start, stop=stop)
                ins_.then_inc(summed, 1)

            norm_acc = [psS[:, 0:HALF], psS[:, 512:512 + HALF]]
            for k in range(KT):
                pe.wait_ge(squared, k + 1)
                sum_squares(sq[:, k % 2, :], [acc[1][:, h, 0:HALF] for h in range(2)], k == 0, k == KT - 1)
                pe.wait_ge(ada_full[k % 4], 16 * (k // 4 + 3))
                if k == 0:
                    pe.wait_ge(ada_out, 1)
                ada(k % 4, psA0, k)

            def idle_is_read(it, what, k, adas):
                b = IDLE[what, k]
                at = TURN.index((what, k))
                free(b, it * (8 - b) + sum(w == "unit" and u % 2 == b for w, u in TURN[:at]))
                pe.wait_ge(ada_out, it * 4 + (adas + 2))

            with pe.Fori(0, PAIRS) as it:
                steps, adas = 0, 0
                for what, k in TURN:
                    if what == "unit":
                        ready("pairs", it, k)
                        free(k % 2, it * (8 - k % 2) + k // 2)
                        pe.wait_ge(o_lod, it * TASKS + (steps + 1))
                        pe.wait_ge(ada_out, it * 4 + (adas + 2))
                        if k == 0:
                            pe.wait_ge(act_split, 8)
                        blocks(k % 2, k % HL, [(i, i) for i in range(KT)], act_hi, act_lo).then_inc(unit_done, 1)
                    elif what == "turn":
                        v = 3 * k + 2
                        pe.wait_ge(acc_free[v % 2], it * (8 - v % 2) + (v // 2 + 2))
                        if k:
                            pe.wait_ge(v_nat, it * 3 + k)
                            pe.wait_ge(k_nat, it * 3 + k)
                        for which, t0, done in ((v, 0, v_turned), (v - 1, 512, k_turned)):
                            for r in range(4):
                                if k == 0 and which == v - 1 and r:
                                    continue
                                if k == 0:
                                    src = qkvT[:, which, r * P:(r + 1) * P] if which == v else qkvT[:, which, TP - P:TP]
                                else:
                                    src = qkvT[:, which, 0:TP].rearrange("p (i r) -> p r i", r=NR)[:, r, :]
                                ins_ = pe.transpose(psT[:, t0 + r * P:t0 + (r + 1) * P], src, ident[:, :])
                            ins_.then_inc(done, 1)
                    elif what == "step":
                        if 0 <= k - 2 < TASKS:
                            j = k - 2
                            r, h = j // 2, j % 2
                            rows = slice(64 * h, 64 * h + 64)
                            pe.wait_ge(copied, it * TASKS + (j + 1))
                            idle_is_read(it, what, k, adas)
                            pe.wait_ge(o_lod, it * TASKS + (j + 1))
                            vs = [vN[:, 0, c, rows] for c in range(4)] + [vN[:, 1, r, rows], vN[:, 2, r, rows]]
                            for c in range(6):
                                ins_ = pe.matmul(psO[IDLE[what, k]][rows, :], vs[c], PT[:, j % 2, c * P:(c + 1) * P], start=c == 0, stop=c == 5)
                            ins_.then_inc(weighted, 1)
                            steps = j + 1
                        if k < TASKS:
                            r, h = k // 2, k % 2
                            rows = slice(64 * h, 64 * h + 64)
                            if k:
                                pe.wait_ge(maxed, it * TASKS + k)
                            def cls(i, r=r, rows=rows):
                                return qkvT[rows, i, 0:TP].rearrange("p (i r) -> p r i", r=NR)[:, r, :]
                            pe.matmul(psS[:, 0:TP], cls(0), qkvT[rows, 1, 0:TP], start=True, stop=True)
                            pe.matmul(psS[:, TP:TP + P], cls(3), cls(4), start=True, stop=True)
                            pe.matmul(psS[:, TP + P:TP + 2 * P], cls(6), cls(7), start=True, stop=True).then_inc(scored, 1)
                        if 0 <= k - 1 < TASKS:
                            j = k - 1
                            pe.wait_ge(normed, it * TASKS + (j + 1))
                            if j == 0:
                                pe.wait_ge(v_nat, it * 3 + 3)
                                pe.wait_ge(k_nat, it * 3 + 3)
                            else:
                                pe.wait_ge(copied, it * TASKS + j)
                            for c in range(6):
                                ins_ = pe.transpose(psT[:, c * P:(c + 1) * P], S[:, j % 2, c * P:(c + 1) * P], ident[:, :])
                            ins_.then_inc(turned, 1)
                    elif what == "ada":
                        for i in range(k, k + 2):
                            pe.wait_ge(ada_full[i % 4], it * 32 + 16 * (i // 4 + 5))
                            if i == k:
                                idle_is_read(it, what, k, adas)
                                pe.wait_ge(o_lod, it * TASKS + (steps + 1))
                            ada(i % 4, psA[IDLE[what, k]], i - k)
                        adas += 1

            pe.wait_ge(smpT_ready, PAIRS)
            pe.wait_ge(copied, PAIRS * TASKS)
            for p in range(PAIRS):
                ins_ = pe.transpose(psT[0:9 * NB, p * P:(p + 1) * P], smpT[:, p, :, :].rearrange("p a b -> p (a b)"), ident[:, :])
            ins_.then_inc(rows_turned, 1)
            pe.wait_ge(ada_out, 2 + 4 * PAIRS)
            pe.wait_ge(pooled, 4)
            pe.wait_ge(o_lod, PAIRS * TASKS + 1)
            for k in range(KT):
                ins_ = pe.transpose(psS[0:TAIL, k * P:(k + 1) * P], u_tail[:, k, :], ident[:, :])
            ins_.then_inc(tail_turned, 1)

            uses = [4 * 8, 4 * 7]

            def take(b):
                free(b, uses[b])
                uses[b] += 1

            for pos in range(2):
                ready("mid", 0, pos)
                for q in range(4):
                    g, d = 2 * pos + q // 2, q % 2
                    i = 4 * pos + q
                    pe.wait_ge(pooled_split, g + 1)
                    take(i % 2)
                    ins_ = blocks(i % 2, pos % HL, [(4 * (q // 2) + 2 * kt + d, 2 * g + kt) for kt in range(2)], act_hi, act_lo)
                    ins_.then_inc(unit_done if q == 3 else part_done, 1)

            def sample_in():
                pe.wait_ge(score_sum, 6)
                pe.wait_ge(smp_ready, 1)
                for g in range(NG):
                    ins_ = pe.transpose(psT[0:NB * NS, 512 + g * P:512 + (g + 1) * P], sall[:, g, :, :].rearrange("p a b -> p (a b)"), ident[:, :])
                ins_.then_inc(smp_in, 1)

            def sample_turn():
                pe.wait_ge(o_new_ready, 1)
                for g in range(NG):
                    ins_ = pe.transpose(psT[:, g * NB * NS:(g + 1) * NB * NS], sc[0:NB * NS, g * P:(g + 1) * P], ident[0:NB * NS, 0:NB * NS])
                ins_.then_inc(smp_turned, 1)

            def sample_out():
                pe.wait_ge(pr_ready, 1)
                pe.matmul(psT[:, 0:NB * NS], o_new[0:NB * NS, :, :].rearrange("p a b -> p (a b)"), ident[0:NB * NS, 0:NB * NS],
                          start=True, stop=False, skip_group_check=True)
                for i in range(6):
                    g, h = divmod(i, 2)
                    pe.wait_ge(kq_full[i % 4], 16 * (3 + i // 4 + 1))
                    for b in range(4):
                        for hp in range(PAIRS):
                            c = (4 * h + b) * NS + 2 * hp
                            ins_ = pe.matmul(psT[:, c:c + 2], kq[i % 4][:, b, hp * P:(hp + 1) * P], prT[:, g, c:c + 2], start=False,
                                             stop=(i == 5 and b == 3 and hp == PAIRS - 1), skip_group_check=True)
                    ins_.then_inc(v_used, 1)
                pe.matmul(psT[:, 512:513], ident[:, :], eps[:, :], start=True, stop=True).then_inc(smp_summed, 1)

            for m in range(8):
                ready("mid", 0, 2 + m)
                take(m % 2)
                if m == 0:
                    pe.wait_ge(acc_free[1], uses[1] + 1)
                ins_ = blocks(m % 2, m % HL, [(i, i) for i in range(KT)], mix_hi, mix_lo)
                ins_.then_inc(unit_done, 1)
                if m == 5:
                    sample_in()
                if m == 6:
                    sample_turn()
                if m == 7:
                    sample_out()
            pe.wait_ge(os_lod, 2)
            for u in range(4):
                ready("mid", 0, 10 + u)
                for q in range(2):
                    take(q)
                    ins_ = blocks(q, u % HL, [(2 * kt + q, kt) for kt in range(4)], o_hi, o_lo)
                    ins_.then_inc(unit_done if q else part_done, 1)
            pe.wait_ge(conv_loaded, 16)
            for j in range(2):
                for b in range(NB):
                    at = 512 * j + b * 2 * FT
                    ins_ = pe.transpose(psT[:, at:at + 2 * FT], conv_rows[0:2 * FT, 2 * b + j, :], ident[0:2 * FT, 0:2 * FT])
            ins_.then_inc(conv_turned, 1)

            with pe.Fori(0, 2) as it:
                for k in range(4):
                    ready("out", it, k)
                    free(k % 2, it * 2 + (uses[k % 2] + k // 2))
                    if k == 0:
                        pe.wait_ge(merged_split, 8)
                    blocks(k % 2, k % HL, [(i, i) for i in range(KT)], act_hi, act_lo).then_inc(unit_done, 1)
            assert tuple(uses) == acc_uses["out"]

            pe.wait_ge(ssqd, 9)
            sum_squares(ssq[:, :], norm_acc)
            for k in range(KT):
                pe.wait_ge(squared, KT + k + 1)
                sum_squares(sq[:, k % 2, :], norm_acc, k == 0, k == KT - 1)

            with pe.Fori(0, FT // 2) as it:
                for k in range(4):
                    ready("up", it, k)
                    free(k % 2, it * 2 + (acc_uses["up"][k % 2] + k // 2))
                    if k == 0:
                        pe.wait_ge(act_split, 16)
                    blocks(k % 2, k % HL, [(i, i) for i in range(KT)], act_hi, act_lo).then_inc(unit_done, 1)
            pe.wait_ge(g_lod, FT + 2)
            pe.wait_ge(hu_tailed, 2 * FT + 4)
            for j in range(CONV_TAIL):
                t, at = (psS, psT)[j // 5], j % 5 * P
                ins_ = pe.transpose(t[0:2 * FT, at:at + P], hu_tail[:, :, j], ident[:, :])
                if j % 5 == 4:
                    ins_.then_inc(hu_turned, 1)

            def down(seg, it):
                for k in range(6):
                    ready(seg, it, k)
                    b, part = divmod(k, 3)
                    if part == 0:
                        free(b, it + acc_uses[seg][b])
                    t0 = 8 * part
                    ins_ = blocks(b, k % HL, [(i, t0 + i) for i in range(min(8, FT - t0))], g_hi, g_lo, first=part == 0, last=part == 2)
                    ins_.then_inc(unit_done, 1)

            with pe.Fori(0, 3) as it:
                down("down", it)
            down("last", 0)
            pe.wait_ge(ssqd, 17)
            sum_squares(ssq[:, :], norm_acc)
            for k in range(KT):
                pe.wait_ge(x_upd, KT + k + 1)
                if k >= 2:
                    pe.wait_ge(y_ready, k - 1)
                for t in range(4):
                    at = 512 * (k % 2) + t * P
                    ins_ = pe.transpose(psT[:, at:at + P], xT[:, k, t * P:(t + 1) * P], ident[:, :])
                ins_.then_inc(y_turned, 1)
            for k in range(KT):
                ins_ = pe.transpose(acc[0][0:NB, k // 4, (k % 4) * P:(k % 4 + 1) * P], xT[:, k, TP:TC], ident[:, :])
            ins_.then_inc(ys_turned, 1)


def kernel(**inputs):
    import numpy as np
    from concourse import bacc
    from concourse.bass_utils import run_bass_kernel_spmd

    nc = bacc.Bacc("TRN2", target_bir_lowering=False, num_devices=1, dynamic_dma_scratch_size=1024)
    arrays, ins = {}, {}
    for name, a in inputs.items():
        a = np.ascontiguousarray(a)
        arrays[f"in_{name}"] = a
        ins[name] = nc.dram_tensor(f"in_{name}", a.shape, mybir.dt.from_np(a.dtype), kind="ExternalInput").ap()
    names = []

    def out(name, *shape):
        names.append(f"out_{name}")
        return nc.dram_tensor(f"out_{name}", shape, F32, kind="ExternalOutput").ap()

    outs = {"y": (out("y_prompt", 1, TP, D), out("y_sample", NB, 1, D)), "new": []}
    for w in WINS:
        outs["new"].append([(out(f"{x}{w}_prompt", 1, 1, min(w, TP), NS, HD), out(f"{x}{w}_sample", 1, NB, w, NS, HD)) for x in "kv"])
    outs["pool"] = (out("pool_prompt", 1, 1, POOL_HIST, D), out("pool_sample", 1, NB, POOL_HIST, D))
    outs["conv"] = (out("conv_prompt", 1, 1, 2, 2 * FF), out("conv_sample", 1, NB, 2, 2 * FF))
    program(nc, ins, outs)
    r = run_bass_kernel_spmd(nc, [arrays], core_ids=[0])
    return tuple(r.results[0][n] for n in names)
```

```python
from contextlib import ExitStack

import concourse.bass as bass
from concourse import mybir

F32 = mybir.dt.float32
F32R = mybir.dt.float32r
BF16 = mybir.dt.bfloat16
ALU = mybir.AluOpType
ACT = mybir.ActivationFunctionType
AX_X = mybir.AxisListType.X
ds = bass.ds

P = 128
D = 1024
KT = D // P
TP = 512
NB = 8
TC = TP + NB
HALF = TC // 2
NS, HD = 8, 64
DA = NS * HD
DILS = (1, 4, 16)
NG = len(DILS)
WINS = tuple(P * d for d in DILS)
PAIRS = NS // 2
NR = 4
POOL_HIST = 15
FF = 2816
FT = FF // P
EPS = 1e-6
NEG = -1e30
BIG = 3e38
NADA = 6 * KT
MC = NB + 1
PROMPT = NB
BLK = 8
RAW, HL = 4, 2
UW = BLK * P
TAIL = POOL_HIST + NB
CONV_TAIL = 2 + NB

TURN = (
    [("unit", k) for k in range(4)] + [("turn", 0)] + [("unit", k) for k in range(4, 7)] + [("turn", 1)]
    + [("unit", k) for k in range(7, 10)] + [("turn", 2), ("step", 0), ("half", 10), ("step", 1), ("unit", 10),
       ("step", 2), ("half", 11), ("step", 3), ("unit", 11), ("ada", 0), ("ada", 1), ("step", 4), ("half", 12), ("step", 5), ("unit", 12),
       ("step", 6), ("half", 13), ("step", 7), ("unit", 13), ("ada", 2), ("ada", 3), ("half", 14), ("step", 8), ("unit", 14),
       ("fold", 0), ("step", 9)]
)
STREAMED = [x for x in TURN if x[0] in ("unit", "ada")]
POS = {x: i for i, x in enumerate(STREAMED)}
NA = 4
IDLE, last = {}, 1
for what, k in TURN:
    if what in ("half", "unit"):
        last = k % 2
    else:
        IDLE[what, k] = 1 - last
TURN_UNITS = len(STREAMED)
TASKS = 2 * NR
MID = [("map", 0), ("map", 1)] + [x for q in range(4) for x in (("ada", 2 * q), ("ada", 2 * q + 1), ("pp", 2 * q), ("pp", 2 * q + 1))] + [("pa", q) for q in range(4)]
NSTART = 2 * KT
SEGMENTS = {"start": (1, NSTART), "pairs": (PAIRS, TURN_UNITS), "mid": (1, len(MID)), "out": (2, 8), "up": (11, 4), "down": (3, 6), "last": (1, 6)}


class Stream:

    def __init__(self):
        self.first, self.fills, n, prev = {}, {}, 0, None
        fills = [0] * RAW
        self.dist = {}
        for name, (iters, units) in SEGMENTS.items():
            self.first[name], self.fills[name] = n, list(fills)
            for pos in range(units):
                gaps = []
                if pos >= RAW:
                    gaps = [RAW]
                else:
                    for u in ([units] if iters > 1 else []) + ([prev] if prev else []):
                        gaps.append(pos + u - max(q for q in range(u) if q % RAW == pos % RAW))
                self.dist[name, pos] = min(gaps, default=RAW)
            n += iters * units
            for s in range(RAW):
                fills[s] += iters * len(range(s, units, RAW))
            prev = units
        self.total = n

    def number(self, seg, it, pos):
        return it * SEGMENTS[seg][1] + (self.first[seg] + pos)

    def fill(self, seg, it, pos):
        units = SEGMENTS[seg][1]
        s = (pos - units if pos >= units else pos) % RAW
        per = len(range(s, units, RAW))
        done = per + 1 if pos >= units else pos // RAW + 1
        return it * per + (self.fills[seg][s] + done)


def tiles(x):
    return x.rearrange("(k p) n -> p k n", p=P)


def program(nc, ins, outs):
    st = Stream()
    w_in, w_up, w_down = ins["w_in"][0], ins["w_up"][0], ins["w_down"][0]
    w_ada, w_out = ins["w_ada"][0], ins["w_out"][0]
    caches = [(ins[f"cache_k_w{w}"], ins[f"cache_v_w{w}"]) for w in WINS]
    scratch = nc.dram_tensor("sample_qkv", (3 * NG, NB, DA), F32, kind="Internal").ap()

    with ExitStack() as ctx:
        def sem(name):
            return ctx.enter_context(nc.semaphore(name))

        def psum(name, shape):
            return ctx.enter_context(nc.psum_tensor(name, shape, F32))

        top = [2048]

        def region(nbytes):
            at = top[0]
            top[0] = at + (nbytes + 31) // 32 * 32
            assert top[0] <= 229344, top[0]
            return at

        def put(name, shape, dt, at):
            return nc.alloc_sbuf_tensor_at(name, [P, *shape], dt, offset=at)

        def new(name, shape, dt=F32):
            n = 2 if dt == BF16 else 4
            for s in shape:
                n *= s
            return put(name, shape, dt, region(n))

        FULL = KT * TC * 4
        r_act = region(2 * FULL)
        act_hi, act_lo = put("act_hi", [KT, TC], F32R, r_act), put("act_lo", [KT, TC], F32R, r_act + FULL)
        ffn = put("ffn", [KT, TC], F32, r_act)
        r_x = region(FULL)
        xT = put("xT", [KT, TC], F32, r_x)
        raw = new("raw", [RAW, UW])
        w_hi, w_lo = new("w_hi", [HL, UW], F32R), new("w_lo", [HL, UW], F32R)
        r_ff = top[0]
        r_z = region(2 * FULL)
        thp, tha = put("thp", [KT, TC], F32, r_z), put("tha", [KT, TC], F32, r_z + FULL)
        x_rows = put("x_rows", [4, D], F32, r_z)
        xs_rows = put("xs_rows", [D], F32, r_z + FULL)
        c_rows, c_tanh, c_silu = (put(n, [D], F32, r_z + FULL + 4096 * i) for i, n in ((1, "c_rows"), (2, "c_tanh"), (3, "c_silu")))
        r_u = region(FULL)
        uT = put("uT", [KT, TC], F32, r_u)
        mix_hi = put("mixed_hi", [KT, TC], F32R, r_u)
        mixT = put("mixT", [KT, TC], F32, r_u)
        norm_u = put("norm_u", [KT, TC], F32, r_z)
        r_att = region(9 * TC * 4)
        qkvT = put("qkvT", [9, TC], F32, r_att)
        mix_lo = put("mixed_lo", [KT, TC], F32R, r_att)
        o_hi, o_lo = new("o_hi", [PAIRS, TC], F32R), new("o_lo", [PAIRS, TC], F32R)
        ada_rows = new("ada_rows", [NA, P])
        r_ada = region(4 * UW * 4)
        ada_start = put("ada_start", [NSTART, P], F32, r_ada)
        vN = new("vN", [NG, 4, P])
        kN = new("kN", [4, P])
        mask = new("mask", [NR, 768], BF16)
        r_s = region(2 * 768 * 4)
        S = put("S", [2, 768], F32, r_s)
        sq = put("sq", [2, TC], F32, r_s)
        r_pt = region(2 * 768 * 4)
        PT = put("PT", [2, 768], F32, r_pt)
        rs = put("rs", [TC], F32, r_pt)
        ssq = put("ssq", [TC], F32, r_pt + 2080)
        pw = new("pw", [2, 16 + TP])
        vec_rows = put("vec_rows", [3, P], F32, r_u)
        hist_rows = put("hist_rows", [D], F32, r_u + 2048)
        mod = new("mod", [NADA, MC])
        silu2 = new("silu2", [KT * 2 * MC + P - 2 * MC], F32R)
        fold = new("fold", [MC])
        vec = new("vec", [3 * 88])
        a_m, a_f, gg_m, gg_f = (new(n, [KT, MC]) for n in ("a_m", "a_f", "gg_m", "gg_f"))
        ident, ones = new("ident", [P]), new("ones", [P])
        smpT = new("smpT", [PAIRS, 9, NB])
        u_tail = new("u_tail", [KT, TAIL])
        hist_sum = new("hist_sum", [KT, NB])
        inv_count = new("inv_count", [16])
        eps = new("eps", [1])
        ind4 = new("ind4", [2, 4])
        neg_max, den, rden = new("neg_max", [2, 1]), new("den", [2, 1]), new("rden", [2, 1])
        small = new("small", [KT, NB])
        seed = new("seed", [13])
        kq = [put(f"kq{i}", [4, DA], F32, r_ada + 8192 * i) for i in range(2)]
        r_more = r_ada + 16384
        kq += [put(f"kq{i}", [4, DA], F32, r_more + 8192 * (i - 2)) for i in range(2, 4)]
        r_sa = r_more + 16384
        bh = put("bh", [9, HD], F32, r_sa)
        sc = put("sc", [NG * P + NG], F32, r_sa + 2304)
        sall = put("sall", [NG, NB, NS], F32, r_sa + 2304 + 1568)
        prT = put("prT", [NG, NB * NS], F32, r_sa + 2304 + 1568 + 768)
        o_new = put("o_new", [2, HD], F32, r_sa + 2304 + 1568 + 1536)
        bh_tmp = put("bh_tmp", [NG, HD], F32, r_sa + 2304 + 1568 + 2048)
        bh_stat = put("bh_stat", [4], F32, r_sa + 2304 + 1568 + 2816)
        smp_rows = put("smp_rows", [DA], F32, r_sa + 2304 + 1568 + 2848)
        assert r_sa + 2304 + 1568 + 2848 + 2048 <= r_pt + 6144
        tail_rows = put("tail_rows", [D], F32, r_pt + 6144)
        g_hi, g_lo = put("g_hi", [FT, TC], F32R, r_ff), put("g_lo", [FT, TC], F32R, r_ff + FT * TC * 4)
        r_cv = r_ff + 2 * FT * TC * 4
        cv = [[put(f"cv{a}{b}", [TC], F32, r_cv + (2 * a + b) * 2080) for b in range(2)] for a in range(2)]
        gm = [put(f"gm{b}", [TC], F32, r_cv + (4 + b) * 2080) for b in range(2)]
        r_he = r_cv + 6 * 2080
        he = [[put(f"he{a}{b}", [2 + TC], F32, r_he + (2 * a + b) * 2112) for b in range(2)] for a in range(2)]
        r_cs = r_he + 4 * 2112
        hsc = put("hsc", [NB, 2 * FT], F32, r_cs)
        assert r_cs + NB * 2 * FT * 4 <= r_s
        hu_tail = put("hu_tail", [2 * FT, CONV_TAIL], F32, r_pt + 6144)
        conv_rows = put("conv_rows", [2 * NB, P], F32, r_ada)
        cst = put("cst", [2, NB * 2 * FT], F32, r_ada + 8192)
        hu_rows = put("hu_rows", [CONV_TAIL, P], F32, r_cv)
        y_rows = put("y_rows", [4, D], F32, r_ff)
        ys_rows = put("ys_rows", [D], F32, r_ff + 16384)

        acc = [psum("acc0", [P, 2, 512]), psum("acc1", [P, 2, 512])]
        psS = psum("psS", [P, 1024])
        psT = psum("psT", [P, 1024])
        psO, psM = [a[:, 0, 264:392] for a in acc], [a[:, 1, 264:264 + NA * MC] for a in acc]
        psA, psA_mid, psM_mid = psT[:, 768:1024], psS[:, 0:256], psS[:, 512:512 + NA * MC]
        accv = [a[:, :, 0:HALF] for a in acc]
        def start_at(t):
            return psS[:, 512 * (t // 2 % 2):512 * (t // 2 % 2) + 256]

        acc_uses, used = {}, [0, 0]
        for name, counts in (("pairs", (PAIRS * 8, PAIRS * 7)), ("map", (4, 4)), ("pool", (4, 4)), ("att", (4, 4)), ("out", (4, 4)),
                             ("up", (FT, FT)), ("down", (3, 3)), ("last", (1, 1))):
            acc_uses[name] = tuple(used)
            used = [u + c for u, c in zip(used, counts)]

        def halves(x):
            return x.rearrange("p (a b) -> p a b", a=2)

        def halves_at(x, i):
            return x[:, ds(i, 1), :].rearrange("p o (a b) -> p o a b", a=2)

        raw_full = [sem(f"raw_full{i}") for i in range(RAW)]
        kq_full = [sem(f"kq_full{i}") for i in range(4)]
        hi_ready, lo_ready = sem("hi_ready"), sem("lo_ready")
        unit_done, part_done = sem("unit_done"), sem("part_done")
        acc_free = [sem("acc_free0"), sem("acc_free1")]
        ada_rowed, folded, ada_out = sem("ada_rowed"), sem("folded"), sem("ada_out")
        c_loaded, vec_loaded, x_loaded, hist_loaded, conv_loaded = (
            sem(x) for x in ("c_loaded", "vec_loaded", "x_loaded", "hist_loaded", "conv_loaded"))
        pool_k, pool_step, pooled = sem("pool_constants"), sem("pool_step"), sem("pooled")
        dve_step = sem("dve_step")
        c_tanhed, c_ready, silu_turned, silu_out, vec_turned, vec_out = (
            sem(x) for x in ("c_tanhed", "c_ready", "silu_turned", "silu_out", "vec_turned", "vec_out"))
        x_turned, x_out, xs_turned, xs_out, hist_turned, hist_ready = (
            sem(x) for x in ("x_turned", "x_out", "xs_turned", "xs_out", "hist_turned", "hist_ready"))
        squared, summed, std_ready = sem("squared"), sem("summed"), sem("std_ready")
        u_ready, act_ready, act_split, x_upd = sem("u_ready"), sem("act_ready"), sem("act_split"), sem("x_upd")
        v_turned, k_turned, v_nat, k_nat = sem("v_turned"), sem("k_turned"), sem("v_nat"), sem("k_nat")
        v_out, k_out = sem("v_out"), sem("k_out")
        scored, maxed, expd, rdend, normed = sem("scored"), sem("maxed"), sem("expd"), sem("rdend"), sem("normed")
        turned, copied, weighted, o_hid, o_lod = sem("turned"), sem("copied"), sem("weighted"), sem("o_hid"), sem("o_lod")
        smpT_ready, rows_turned, smp_ready, smp_stored, smp_back, new_rows = (
            sem(x) for x in ("smpT_ready", "rows_turned", "smp_ready", "smp_stored", "smp_back", "new_rows"))
        tail_turned, tail_ready, tail_stored = sem("tail_turned"), sem("tail_ready"), sem("tail_stored")
        pooled_split, mixed_hid, merged, merged_split = sem("pooled_split"), sem("mixed_hid"), sem("merged"), sem("merged_split")
        prod_done, score_sum, smp_in, smp_max, smp_exp = sem("prod_done"), sem("score_sum"), sem("smp_in"), sem("smp_max"), sem("smp_exp")
        o_new_ready, smp_turned, pr_ready, v_used, smp_summed, os_hid, os_lod = (
            sem(x) for x in ("o_new_ready", "smp_turned", "pr_ready", "v_used", "smp_summed", "os_hid", "os_lod"))
        conv_turned, ssqd = sem("conv_turned"), sem("ssqd")
        tap1, taps, hu_tailed, gelud, gated, g_hid, g_lod = (
            sem(x) for x in ("tap1", "taps", "hu_tailed", "gelud", "gated", "g_hid", "g_lod"))
        hu_turned, hu_rowed, y_turned, ys_turned, y_ready, ys_ready, y_out = (
            sem(x) for x in ("hu_turned", "hu_rowed", "y_turned", "ys_turned", "y_ready", "ys_ready", "y_out"))
        silu_zeroed, silu_hid, fold_ready = sem("silu_zeroed"), sem("silu_hid"), sem("fold_ready")
        copy_done, rows_done = sem("copy_done"), sem("rows_done")

        block = ctx.enter_context(nc.Block())

        @block.sync
        def _(sp):
            def unit(seg, it, pos, src, cols=UW):
                sp.wait_ge(lo_ready, st.number(seg, it, pos) - st.dist[seg, pos] + 1 + RAW)
                s = pos % RAW
                sp.dma_start(raw[:, s, 0:cols].rearrange("p (k n) -> p k n", n=src.shape[-1]), src).then_inc(raw_full[s], 16)

            def block_of(w, at, cols=P):
                return tiles(w)[:, :, ds(at, cols)]

            def ada_of(t, half):
                return tiles(w_ada)[:, half * 4:half * 4 + 4, ds(t * P, 2 * P)]

            def shifted(g, kv):
                j, n = ((4, 1016), (16, 1022), (89, 736))[g]
                a = caches[g][kv][0].rearrange("b l s d -> b (l s d)")[:, DA:]
                o = outs["new"][g][kv][1][0].rearrange("b l s d -> b (l s d)")[:, 0:(WINS[g] - 1) * DA]
                return tuple(x.rearrange("b (e j n) -> e b j n", e=16, n=n) for x in (o, a)), j

            def copy(g, j):
                for kv in range(2):
                    (o, a), _ = shifted(g, kv)
                    sp.dma_start(o[:, :, ds(j, 1), :], a[:, :, ds(j, 1), :]).then_inc(copy_done, 16)

            sp.dma_start(c_rows[0:NB, :], ins["c_sample"]).then_inc(c_loaded, 16)
            sp.dma_start(c_rows[NB:MC, :], ins["c_prompt"]).then_inc(c_loaded, 16)
            rows = lambda x: x.rearrange("a (m c) -> (a m) c", c=P)
            sp.dma_start(vec_rows[0:48, 0, :], rows(ins["b_ada"])).then_inc(vec_loaded, 16)
            for i, n in enumerate(("g_pre_mix", "g_post_mix", "g_pre_ffn", "g_post_ffn", "pool_scale")):
                sp.dma_start(vec_rows[48 + 8 * i:56 + 8 * i, 0, :], rows(ins[n])).then_inc(vec_loaded, 16)
            wc = rows(ins["w_conv"][0])
            sp.dma_start(vec_rows[0:88, 1, :], wc[0:88, :]).then_inc(vec_loaded, 16)
            sp.dma_start(vec_rows[0:44, 2, :], wc[88:132, :]).then_inc(vec_loaded, 16)
            sp.dma_start(vec_rows[44:88, 2, :], rows(ins["b_conv"])).then_inc(vec_loaded, 16)
            for t in range(NSTART):
                unit("start", 0, t, ada_of(t - t % 2, t % 2))

            with sp.Fori(0, PAIRS) as it:
                for pos, (what, k) in enumerate(STREAMED):
                    if what == "ada":
                        unit("pairs", it, pos, ada_of(it * NA + (NSTART + k - k % 2), k % 2))
                        continue
                    if k < 9:
                        g, part = divmod(k, 3)
                        at = it * P + (D + part * NG * DA + g * DA)
                    elif k < 11:
                        at = it * (2 * P) + (k - 9) * P
                    else:
                        at = it * (2 * P) + (D + 3 * NG * DA + (k - 11) // 2 * D + (k - 11) % 2 * P)
                    unit("pairs", it, pos, block_of(w_in, at))
                    if k in (1, 3, 4, 6, 7, 9, 10, 12, 13):
                        copy(2, it * 9 + (1, 3, 4, 6, 7, 9, 10, 12, 13).index(k))
                    if k in (0, 2, 5, 11):
                        copy(1, it * 4 + (0, 2, 5, 11).index(k))
                    if k == 8:
                        copy(0, it)
                    if k in (8, 11, 14):
                        g = (k - 8) // 3
                        for kv, (src, ready, done) in enumerate(((kN[:, :, :], k_nat, k_out), (vN[:, g, :, :], v_nat, v_out))):
                            sp.wait_ge(ready, it * 3 + (g + 1))
                            o = outs["new"][g][kv][0][0, 0].rearrange("t s d -> t (s d)")[:, ds((it + PAIRS) * P - DA, P)]
                            if g:
                                o = o.rearrange("(i r) c -> i r c", r=NR)
                            else:
                                src = src[:, 0, :] if kv == 0 else src[:, 3, :]
                            sp.dma_start(o, src).then_inc(done, 16)

            for i in range(2):
                wm = ins["w_pool_map"][0, 2 * i:2 * i + 2].rearrange("g (k p) n -> p (g k) n", p=P)
                unit("mid", 0, MID.index(("map", i)), wm)
            def load_kq(i):
                g, h = divmod(i, 2)
                b = 2 * (i % 2)
                if i >= 2:
                    sp.wait_ge(score_sum, i - 1)
                src = caches[g][0][0, 4 * h:4 * h + 4].rearrange("b (i e) s d -> i b e (s d)", e=DILS[g])[:, :, 0, :]
                sp.dma_start(kq[b][:, :, :], src).then_inc(kq_full[b], 16)
                sp.dma_start(kq[b + 1][:, :, :], scratch[3 * g, 4 * h:4 * h + 4, :].partition_broadcast(P)).then_inc(kq_full[b + 1], 16)

            def load_v(i):
                g, h = divmod(i, 2)
                if i < 4:
                    sp.wait_ge(score_sum, 6)
                else:
                    sp.wait_ge(v_used, i - 3)
                src = caches[g][1][0, 4 * h:4 * h + 4].rearrange("b (i e) s d -> i b e (s d)", e=DILS[g])[:, :, 0, :]
                sp.dma_start(kq[i % 4][:, :, :], src).then_inc(kq_full[i % 4], 16)

            def proj_pool(i):
                if i % 2 == 0:
                    for half in range(2):
                        unit("mid", 0, MID.index(("ada", i + half)), ada_of(NSTART + PAIRS * NA + i, half))
                unit("mid", 0, MID.index(("pp", i)), block_of(ins["w_proj_pool"][0], i * P))

            def proj_att(i):
                unit("mid", 0, MID.index(("pa", i)), tiles(ins["w_proj_att"][0])[:, :, i * 2 * P:(i + 1) * 2 * P])

            proj_pool(0)
            proj_pool(1)
            sp.wait_ge(smp_ready, 1)
            sp.dma_start(scratch.rearrange("m b n -> (m b) n"), smp_rows[0:3 * NG * NB, :]).then_inc(smp_stored, 16)
            for g in range(NG):
                for kv in range(2):
                    o = outs["new"][g][kv][1][0, :, WINS[g] - 1].rearrange("b s d -> b (s d)")
                    r0 = (3 * g + 1 + kv) * NB
                    sp.dma_start(o, smp_rows[r0:r0 + NB, :]).then_inc(new_rows, 16)
            sp.wait_ge(smp_stored, 16)
            sp.dma_start(bh[0:NB * NS, :, :], scratch.rearrange("m b (h d) -> (b h) m d", d=HD)).then_inc(smp_back, 16)
            load_kq(0)
            load_kq(1)
            proj_pool(2)
            for i in range(4):
                proj_pool(3 + i)
                load_kq(2 + i)
            proj_pool(7)
            proj_att(0)
            for i in range(4):
                load_v(i)
            proj_att(1)
            load_v(4)
            load_v(5)
            proj_att(2)
            proj_att(3)
            sp.dma_start(outs["pool"][1][0, :, 0:POOL_HIST - 1], ins["state_pool"][0, :, 1:]).then_inc(rows_done, 16)
            sp.wait_ge(tail_ready, 1)
            sp.dma_start(outs["pool"][0][0, 0], tail_rows[0:POOL_HIST, :]).then_inc(tail_stored, 16)
            sp.dma_start(outs["pool"][1][0, :, POOL_HIST - 1], tail_rows[POOL_HIST:TAIL, :]).then_inc(tail_stored, 16)
            sp.dma_start(outs["conv"][1][0, :, 0], ins["state_conv"][0, :, 1]).then_inc(rows_done, 16)
            sp.wait_ge(v_used, 6)
            sp.dma_start(conv_rows[0:2 * FT, :, :], ins["state_conv"][0].rearrange("b j (m c) -> m (b j) c", c=P)).then_inc(conv_loaded, 16)
            with sp.Fori(0, 2) as it:
                for k in range(4):
                    unit("out", it, 2 * k, block_of(w_out, it * (4 * P) + k * P))
                    unit("out", it, 2 * k + 1, ada_of(it * 4 + (NADA - 8 + k - k % 2), k % 2))
            with sp.Fori(0, FT // 2) as it:
                for k in range(4):
                    unit("up", it, k, block_of(w_up, it * (2 * P) + (k // 2 * P + k % 2 * FF)))
                    copy(2, it * 4 + (36 + k))
            def down(seg, it, m0):
                for k in range(6):
                    r0, r1 = 8 * (k % 3), min(8 * (k % 3) + 8, FT)
                    unit(seg, it, k, tiles(w_down)[:, r0:r1, ds(m0 + k // 3 * P, P)], cols=(r1 - r0) * P)
                    if seg == "down" and k % 2 == 1:
                        copy(2, it * 3 + (80 + k // 2))

            with sp.Fori(0, 3) as it:
                down("down", it, it * (2 * P))
            down("last", 0, 6 * P)
            sp.wait_ge(hu_rowed, 2)
            for j in range(CONV_TAIL):
                o = outs["conv"][0][0, 0, j] if j < 2 else outs["conv"][1][0, j - 2, 1]
                sp.dma_start(o.rearrange("(m c) -> m c", c=P), hu_rows[0:2 * FT, j, :]).then_inc(rows_done, 16)
            for q in range(4):
                sp.wait_ge(y_ready, 2 * q + 2)
                o = outs["y"][0][0].rearrange("(t p) n -> p t n", p=P)
                sp.dma_start(o[:, :, 2 * P * q:2 * P * q + 2 * P], y_rows[:, :, 2 * P * q:2 * P * q + 2 * P]).then_inc(y_out, 16)
            sp.wait_ge(ys_ready, 1)
            sp.dma_start(outs["y"][1].rearrange("b t n -> (b t) n"), ys_rows[0:NB, :]).then_inc(y_out, 16)
            sp.wait_ge(y_out, 16 * 5)
            sp.wait_ge(rows_done, 16 * (2 + CONV_TAIL))
            sp.wait_ge(new_rows, 16 * 2 * NG)
            sp.wait_ge(tail_stored, 32)
            sp.wait_ge(copy_done, 16 * 2 * (89 + 16 + 4))
            sp.wait_ge(k_out, 16 + 16 * 12)
            sp.wait_ge(v_out, 16 + 16 * 12)

        @block.gpsimd
        def _(pool):
            n = [0]

            def step(ins_):
                n[0] += 1
                ins_.then_inc(pool_step, 1)
                pool.wait_ge(pool_step, n[0])

            step(pool.memset(ident[:, :], 0.0))
            step(pool.memset(ones[:, :], 1.0))
            step(pool.memset(eps[:, :], EPS))
            pool.affine_select(out=ident[:, :], in_=ident[:, :], compare_op=ALU.not_equal, fill=1.0, base=0,
                               pattern=[[-1, P]], channel_multiplier=1).then_inc(pool_k, 1)
            step(pool.memset(mask[:, :, :], 0.0))
            step(pool.memset(pw[:, :, 0:16], 0.0))
            for t in range(16):
                step(pool.memset(inv_count[:, t:t + 1], 1.0 / (t + 1)))
            for r in range(NR):
                m0, m1 = mask[:, r, 0:TP], mask[:, r, TP:TP + P]
                step(pool.affine_select(out=m0, in_=m0, compare_op=ALU.is_ge, fill=NEG, base=r, pattern=[[-1, TP]], channel_multiplier=4))
                step(pool.affine_select(out=m0, in_=m0, compare_op=ALU.is_ge, fill=NEG, base=P - r, pattern=[[1, TP]], channel_multiplier=-4))
                step(pool.affine_select(out=m1, in_=m1, compare_op=ALU.is_ge, fill=NEG, base=0, pattern=[[-1, P]], channel_multiplier=1))
                m2 = mask[:, r, TP + P:TP + 2 * P]
                ins_ = pool.affine_select(out=m2, in_=m2, compare_op=ALU.is_ge, fill=NEG, base=0, pattern=[[-1, P]], channel_multiplier=1)
                if r == NR - 1:
                    ins_.then_inc(pool_k, 1)
                else:
                    step(ins_)

            for gi in range(4):
                win = 2 ** (gi + 1)
                pool.wait_ge(acc_free[0], 1 + 8 * gi + 6)
                t0 = 2 * gi
                step(pool.tensor_copy(u_tail[:, t0:t0 + 2, :], uT[:, t0:t0 + 2, TP - POOL_HIST:TC]))
                for t in (t0, t0 + 1):
                    u = uT[:, t, 0:TP]
                    step(pool.tensor_copy(pw[:, 0, 16:17], uT[:, t, 0:1]))
                    step(pool.tensor_tensor(pw[:, 0, 17:16 + TP], uT[:, t, 1:TP], uT[:, t, 0:TP - 1], ALU.add))
                    b = 0
                    for lv in range(1, gi + 1):
                        sh = 2 ** lv
                        step(pool.tensor_tensor(pw[:, 1 - b, 16:16 + TP], pw[:, b, 16:16 + TP], pw[:, b, 16 - sh:16 + TP - sh], ALU.add))
                        b = 1 - b
                    head = win - 1
                    step(pool.tensor_tensor(pw[:, b, 16:16 + head], pw[:, b, 16:16 + head], inv_count[:, 0:head], ALU.mult))
                    step(pool.tensor_scalar(pw[:, b, 16 + head:16 + TP], pw[:, b, 16 + head:16 + TP], 1.0 / win, 0.0, ALU.mult, ALU.add))
                    step(pool.tensor_tensor(u, pw[:, b, 16:16 + TP], u, ALU.subtract))
                if gi == 0:
                    pool.wait_ge(hist_ready, 1)
                us = uT[:, t0:t0 + 2, TP:TC]
                tmp = pw[:, 0, 16:32].rearrange("p (a b) -> p a b", a=2)
                step(pool.tensor_tensor(tmp, us, hist_sum[:, t0:t0 + 2, :], ALU.add))
                step(pool.tensor_scalar(tmp, tmp, 1.0 / win, 0.0, ALU.mult, ALU.add))
                pool.tensor_tensor(us, tmp, us, ALU.subtract).then_inc(pooled, 1)
                if gi < 3:
                    pool.wait_ge(pooled, gi + 1)

            for i in range(6):
                b = 2 * (i % 2)
                pool.wait_ge(kq_full[b], 16 * (i // 2 + 1))
                pool.wait_ge(kq_full[b + 1], 16 * (i // 2 + 1))
                pool.tensor_tensor(kq[b][:, :, :], kq[b][:, :, :], kq[b + 1][:, :, :], ALU.mult).then_inc(prod_done, 1)

            pool.wait_ge(tail_stored, 32)
            with pool.Fori(0, FT // 2) as it:
                for k in range(4):
                    pool.wait_ge(acc_free[k % 2], it * 2 + (acc_uses["up"][k % 2] + k // 2 + 2))
                    m, half = k // 2, k % 2
                    pool.tensor_copy(hu_tail[:, ds(it * 2 + (m + half * FT), 1), :], he[half][m][:, 2 + TP - 2:2 + TC].unsqueeze(1)).then_inc(hu_tailed, 1)

        @block.scalar
        def _(act):
            def split(seg, it, pos, ahead=2):
                units = SEGMENTS[seg][1]
                if units % 2 and pos >= units - 2:
                    if pos == units - 2:
                        return
                    if ahead == 2:
                        split(seg, it, pos, 1)
                pos += ahead
                s = pos - units if pos >= units else pos
                cols = 6 * P if seg in ("down", "last") and pos in (2, 5) else UW
                act.wait_ge(raw_full[s % RAW], st.fill(seg, it, pos) * 16)
                act.activation(w_hi[:, s % HL, 0:cols], raw[:, s % RAW, 0:cols], ACT.Copy).then_inc(hi_ready, 1)

            def done(seg, it, pos):
                act.wait_ge(unit_done, st.number(seg, it, pos) + 1)

            act.dma_start(x_rows[:, :, :], ins["x_prompt"][0].rearrange("(t p) n -> p t n", p=P)).then_inc(x_loaded, 16)
            act.dma_start(xs_rows[0:NB, :], ins["x_sample"].rearrange("b t n -> (b t) n")).then_inc(x_loaded, 16)
            act.dma_start(hist_rows[0:NB * POOL_HIST, :], ins["state_pool"][0].rearrange("b t n -> (b t) n")).then_inc(hist_loaded, 16)
            act.wait_ge(c_loaded, 32)
            act.activation(c_tanh[0:MC, :], c_rows[0:MC, :], ACT.Tanh, scale=0.5).then_inc(c_tanhed, 1)
            silu_hi = silu2[:, 0:KT * 2 * MC].rearrange("p (k j c) -> p k j c", k=KT, j=2)[:, :, 0, :]
            split("start", 0, -2)
            act.wait_ge(silu_turned, 1)
            act.wait_ge(silu_zeroed, 1)
            act.activation(silu_hi, acc[1][:, 0, 0:KT * MC].rearrange("p (k c) -> p k c", k=KT), ACT.Copy, scale=0.5).then_inc(silu_hid, 1)
            act.wait_ge(vec_turned, 1)
            act.activation(vec[:, :], acc[1][:, 1, 0:3 * 88], ACT.Copy).then_inc(vec_out, 1)
            split("start", 0, -1)
            for t in range(NSTART):
                done("start", 0, t)
                split("start", 0, t)
                if t % 2:
                    k = t // 2
                    act.wait_ge(x_turned, k + 1)
                    act.activation(xT[:, k, 0:TP], psT[:, 512 * (k % 2):512 * (k % 2) + 512], ACT.Copy).then_inc(x_out, 1)
            act.wait_ge(xs_turned, 1)
            act.activation(xT[:, :, TP:TC], acc[0][:, 1, 256:256 + KT * NB].rearrange("p (a b) -> p a b", a=KT), ACT.Copy).then_inc(xs_out, 1)
            act.wait_ge(xs_out, 1)

            def squares(before):
                for k in range(KT):
                    if before:
                        act.wait_ge(x_upd, k + 1)
                    if k >= 2:
                        act.wait_ge(summed, before + k - 1)
                    act.activation(sq[:, k % 2, :], xT[:, k, :], ACT.Square).then_inc(squared, 1)

            def root(where, sums):
                act.wait_ge(summed, sums)
                act.activation(halves(rs[:, :]), where, ACT.Sqrt, bias=eps[:, :], scale=1.0 / D).then_inc(std_ready, 1)

            norm_view = psS[:, :].rearrange("p (a b) -> p a b", a=2)[:, :, 0:HALF]
            squares(0)
            root(accv[1], 8)
            def split_act(k):
                act.wait_ge(u_ready, k + 1)
                act.activation(act_hi[:, k, :], uT[:, k, :], ACT.Copy).then_inc(act_ready, 1)

            for k in range(KT):
                split_act(k)
            act.activation(seed[:, 11:12], eps[:, :], ACT.Tanh)

            with act.Fori(0, PAIRS) as it:
                for what, k in TURN:
                    if what in ("unit", "ada"):
                        pos = POS[what, k]
                        done("pairs", it, pos)
                    if what == "ada":
                        split("pairs", it, pos)
                    elif what == "unit":
                        b = k % 2
                        if k < 9 and k % 3 != 2:
                            act.activation(halves(qkvT[:, k, :]), accv[b], ACT.Copy, scale=0.125 if k % 3 == 0 else 1.0).then_inc(acc_free[b], 1)
                        elif k >= 9:
                            dst = halves_at((uT, thp, tha)[(k - 9) // 2], it * 2 + (k - 9) % 2)
                            act.activation(dst, accv[b].unsqueeze(1), ACT.Copy if k < 11 else ACT.Tanh, scale=1.0 if k < 11 else 0.5).then_inc(acc_free[b], 1)
                        split("pairs", it, pos)
                    elif what == "turn":
                        act.wait_ge(k_turned, it * 3 + (k + 1))
                        act.wait_ge(k_out, it * 48 + (16 * k + 16))
                        w = 1 if k == 0 else 4
                        act.activation(kN[:, 0:w, :].rearrange("p a b -> p (a b)"), psT[:, 512:512 + w * P], ACT.Copy).then_inc(k_nat, 1)
                    elif what == "step":
                        if 0 <= k - 2 < TASKS:
                            j = k - 2
                            r, h = j // 2, j % 2
                            rows = slice(64 * h, 64 * h + 64)
                            act.wait_ge(weighted, it * TASKS + (j + 1))
                            dst = o_hi[rows, ds(it, 1), 0:TP].rearrange("p o (i r) -> p o r i", r=NR)[:, :, r, :]
                            act.activation(dst, psO[IDLE[what, k]][rows, :].unsqueeze(1), ACT.Copy).then_inc(o_hid, 1)
                        if 0 <= k - 1 < TASKS:
                            j = k - 1
                            act.wait_ge(turned, it * TASKS + (j + 1))
                            if j >= 2:
                                act.wait_ge(weighted, it * TASKS + (j - 1))
                            act.activation(PT[:, j % 2, :], psT[:, 0:768], ACT.Copy).then_inc(copied, 1)
                        if k < TASKS:
                            act.wait_ge(maxed, it * TASKS + (k + 1))
                            act.activation(S[:, k % 2, :], S[:, k % 2, :], ACT.Exp, bias=neg_max[:, k % 2, :], scale=-1.0,
                                           accum_out=den[:, k % 2, :]).then_inc(expd, 1)

            for q in range(4):
                act.wait_ge(pooled, q + 1)
                if q == 0:
                    done("pairs", PAIRS - 1, TURN_UNITS - 1)
                act.activation(act_hi[:, 2 * q:2 * q + 2, :], uT[:, 2 * q:2 * q + 2, :], ACT.Copy).then_inc(act_ready, 1)
            act.wait_ge(rows_turned, 1)
            act.activation(smp_rows[0:3 * NG * NB, :], psT[0:3 * NG * NB, 0:DA], ACT.Copy).then_inc(smp_ready, 1)
            act.wait_ge(tail_turned, 1)
            act.activation(tail_rows[0:TAIL, :], psS[0:TAIL, :], ACT.Copy).then_inc(tail_ready, 1)
            act.wait_ge(pooled_split, 4)
            for pos, (what, m) in enumerate(MID):
                if what == "map":
                    for q in range(4):
                        i = 4 * m + q
                        if q < 3:
                            act.wait_ge(part_done, 3 * m + q + 1)
                        else:
                            done("mid", 0, pos)
                        act.activation(halves(mix_hi[:, i, :]), accv[i % 2], ACT.Identity, scale=vec[:, 80 + i:81 + i]).then_inc(mixed_hid, 1)
                if (what, m) == ("pp", 6):
                    act.wait_ge(smp_max, 1)
                    act.activation(sc[0:NB * NS, :], sc[0:NB * NS, :], ACT.Exp, bias=bh_stat[0:NB * NS, 0:1], scale=1.0,
                                   accum_out=bh_stat[0:NB * NS, 1:2]).then_inc(smp_exp, 1)
                if what in ("ada", "pp"):
                    done("mid", 0, pos)
                if what == "pa":
                    for q in range(2):
                        i = 2 * m + q
                        act.wait_ge(merged, i + 1)
                        act.activation(act_hi[:, i, :], tha[:, i, :], ACT.Copy, scale=0.5).then_inc(act_ready, 1)
                    done("mid", 0, pos)
                split("mid", 0, pos)
                if (what, m) == ("pp", 7):
                    act.wait_ge(smp_summed, 1)
                    for h in range(2):
                        rows = slice(HD * h, HD * h + HD)
                        src = psT[rows, 0:NB * NS].rearrange("p (b q h) -> p q b h", b=NB, h=2)[:, :, :, h]
                        act.activation(o_hi[rows, :, TP:TC], src, ACT.Copy).then_inc(os_hid, 1)

            with act.Fori(0, 2) as it:
                for k in range(4):
                    done("out", it, 2 * k)
                    act.activation(halves_at(mixT, it * 4 + k), accv[k % 2].unsqueeze(1), ACT.Copy)
                    act.wait_ge(ssqd, it * 4 + (k + 1))
                    act.activation(halves(sq[:, k % 2, :]), accv[k % 2], ACT.Square).then_inc(acc_free[k % 2], 1)
                    split("out", it, 2 * k)
                    done("out", it, 2 * k + 1)
                    split("out", it, 2 * k + 1)
            root(norm_view, 9)
            squares(9)
            root(norm_view, 17)
            for k in range(KT):
                act.wait_ge(u_ready, KT + k + 1)
                act.activation(act_hi[:, k, :], norm_u[:, k, :], ACT.Copy).then_inc(act_ready, 1)

            act.activation(seed[:, 12:13], eps[:, :], ACT.Gelu_apprx_tanh)

            with act.Fori(0, FT // 2) as it:
                for k in range(4):
                    m, half = k // 2, k % 2
                    done("up", it, k)
                    w2 = vec[:, ds(it * 2 + (176 + m + half * FT), 1)]
                    bc = vec[:, ds(it * 2 + (220 + m + half * FT), 1)]
                    act.wait_ge(taps, it * 4 + (k + 1))
                    act.wait_ge(hu_tailed, it * 4 + (k + 1))
                    act.activation(halves(he[half][m][:, 2:2 + TC]), accv[k % 2], ACT.Copy)
                    act.activation(halves(cv[half][m][:, :]), accv[k % 2], ACT.Identity, bias=bc, scale=w2).then_inc(acc_free[k % 2], 1)
                    split("up", it, k)
                    if half == 1:
                        act.wait_ge(taps, it * 4 + (4 + 2 * m + 1))
                        act.wait_ge(g_lod, it * 2 + (m + 1))
                        act.activation(gm[m][:, :], cv[0][m][:, :], ACT.Gelu_apprx_tanh).then_inc(gelud, 1)
                        act.wait_ge(gated, it * 2 + (m + 1))
                        act.activation(g_hi[:, ds(it * 2 + m, 1), :].rearrange("p o n -> p (o n)"), gm[m][:, :], ACT.Copy).then_inc(g_hid, 1)

            for i, t in enumerate((psS, psT)):
                act.wait_ge(hu_turned, i + 1)
                act.activation(hu_rows[0:2 * FT, 5 * i:5 * i + 5, :].rearrange("p a b -> p (a b)"), t[0:2 * FT, 0:5 * P], ACT.Copy).then_inc(hu_rowed, 1)

            def down(seg, it, m0):
                for k in range(6):
                    done(seg, it, k)
                    if not (seg == "last" and k >= 4):
                        split(seg, it, k)
                    if k % 3 == 2:
                        b = k // 3
                        act.activation(halves_at(ffn, m0 + b), accv[b].unsqueeze(1), ACT.Copy)
                        act.wait_ge(ssqd, it * 2 + ((9 if seg == "down" else 15) + b))
                        act.activation(halves(sq[:, b, :]), accv[b], ACT.Square).then_inc(acc_free[b], 1)

            with act.Fori(0, 3) as it:
                down("down", it, it * 2)
            down("last", 0, 6)
            root(norm_view, 18)
            for k in range(KT):
                act.wait_ge(y_turned, k + 1)
                act.activation(y_rows[:, :, k * P:(k + 1) * P], psT[:, 512 * (k % 2):512 * (k % 2) + 512].rearrange("p (a b) -> p a b", a=4),
                               ACT.Copy).then_inc(y_ready, 1)
            act.wait_ge(ys_turned, 1)
            act.activation(ys_rows[0:NB, :], acc[0][0:NB, :, :].rearrange("p a b -> p (a b)"), ACT.Copy).then_inc(ys_ready, 1)

        @block.vector
        def _(dve):
            n = [0]

            def mark(ins_):
                n[0] += 1
                ins_.then_inc(dve_step, 1)
                return n[0]

            def mine():
                dve.wait_ge(dve_step, n[0])

            def split(seg, it, pos, ahead=2):
                units = SEGMENTS[seg][1]
                if units % 2 and pos >= units - 2:
                    if pos == units - 2:
                        return
                    if ahead == 2:
                        split(seg, it, pos, 1)
                pos += ahead
                s = pos - units if pos >= units else pos
                cols = 6 * P if seg in ("down", "last") and pos in (2, 5) else UW
                dve.wait_ge(hi_ready, st.number(seg, it, pos) + 1)
                dve.tensor_tensor(w_lo[:, s % HL, 0:cols], raw[:, s % RAW, 0:cols], w_hi[:, s % HL, 0:cols].bitcast(F32), ALU.subtract).then_inc(lo_ready, 1)

            def done(seg, it, pos):
                dve.wait_ge(unit_done, st.number(seg, it, pos) + 1)

            def ada_evac(seg, it, pos, k, dst, src):
                done(seg, it, pos)
                if k % 2:
                    dve.tensor_copy(dst[0:2 * MC, k - 1:k + 1, :].rearrange("p a b -> p (a b)"), src[0:2 * MC, :]).then_inc(ada_rowed, 1)
                split(seg, it, pos)

            def modulation(t0, n, src, count):
                dve.wait_ge(folded, count)
                dve.tensor_tensor(mod[:, ds(t0, n), :], src.rearrange("p (a b) -> p a b", b=MC)[:, 0:n, :],
                                  vec[:, ds(t0, n)].unsqueeze(2).to_broadcast([P, n, MC]), ALU.add).then_inc(ada_out, 1)

            for i, (s, c) in enumerate(((acc_free[0], 1), (acc_free[1], 1), (lo_ready, RAW), (o_lod, 1), (k_out, 16), (v_out, 16), (ssqd, 1), (taps, 4),
                         (hu_tailed, 4), (g_lod, 2))):
                dve.memset(seed[:, i:i + 1], 0.0).then_inc(s, c)
            dve.memset(silu2[:, KT * 2 * MC:].bitcast(F32), 0.0).then_inc(silu_zeroed, 1)
            dve.wait_ge(c_tanhed, 1)
            dve.scalar_tensor_tensor(c_silu[0:MC, :], c_tanh[0:MC, :], 1.0, c_rows[0:MC, :], ALU.add, ALU.mult).then_inc(c_ready, 1)
            dve.wait_ge(pool_k, 1)
            dve.tensor_tensor(fold[0:2 * MC, :], ident[0:2 * MC, 0:MC], ident[0:2 * MC, MC:2 * MC], ALU.add).then_inc(fold_ready, 1)
            split("start", 0, -2)
            dve.wait_ge(silu_hid, 1)
            silu = silu2[:, 0:KT * 2 * MC].rearrange("p (k j c) -> p k j c", k=KT, j=2)
            dve.scalar_tensor_tensor(silu[:, :, 1, :], acc[1][:, 0, 0:KT * MC].rearrange("p (k c) -> p k c", k=KT), 0.5,
                                     silu[:, :, 0, :].bitcast(F32), ALU.mult, ALU.subtract).then_inc(silu_out, 1)
            split("start", 0, -1)
            for t in range(NSTART):
                ada_evac("start", 0, t, t, ada_start, start_at(t))
            mark(dve.tensor_reduce(ind4[:, 0, :], ident[:, :].rearrange("p (a b) -> p b a", b=4), AX_X, ALU.add))
            mine()
            mark(dve.tensor_scalar(ind4[:, 1, :], ind4[:, 0, :], -NEG, NEG, ALU.mult, ALU.add))
            mine()
            dve.wait_ge(pool_k, 2)
            for r in range(NR):
                m2 = mask[:, r, TP + P:TP + 2 * P].rearrange("p (a b) -> p a b", b=4)
                mark(dve.tensor_tensor(m2, m2, ind4[:, 1, :].unsqueeze(1).to_broadcast([P, 32, 4]), ALU.add))
            dve.wait_ge(hist_turned, 1)
            for gi in range(4):
                win = 2 ** (gi + 1)
                src = acc[0][:, gi // 2, (gi % 2) * 240:(gi % 2) * 240 + 240].rearrange("p (k b t) -> p k b t", k=2, b=NB)[:, :, :, 16 - win:]
                ins_ = dve.tensor_reduce(hist_sum[:, 2 * gi:2 * gi + 2, :], src, AX_X, ALU.add)
            ins_.then_inc(hist_ready, 1)

            dve.wait_ge(vec_out, 1)
            modulation(0, NSTART, psS[:, 0:NSTART * MC], 1)
            dve.wait_ge(std_ready, 1)
            mark(dve.reciprocal(rs[:, :], rs[:, :]))
            dve.wait_ge(ada_out, 1)

            def gains(dst, scale0, g0, plus):
                v = vec[:, g0:g0 + 8].unsqueeze(2).to_broadcast([P, 8, MC])
                return mark(dve.scalar_tensor_tensor(dst[:, :, :], mod[:, scale0:scale0 + 8, :], plus, v, ALU.add, ALU.mult))

            gains(a_m, 8, 48, 1.0)
            mine()

            def modulated(u, a, shift0, base):
                us, xs = u[:, :, TP:TC], xT[:, :, TP:TC]
                mark(dve.tensor_tensor(small[:, :, :], xs, rs[:, TP:TC].unsqueeze(1).to_broadcast([P, KT, NB]), ALU.mult))
                mine()
                mark(dve.tensor_tensor(small[:, :, :], small[:, :, :], a[:, :, 0:NB], ALU.mult))
                mine()
                mark(dve.tensor_tensor(us, small[:, :, :], mod[:, shift0:shift0 + 8, 0:NB], ALU.add))
                for k in range(KT + 1):
                    if k < KT:
                        mark(dve.tensor_tensor(u[:, k, 0:TP], xT[:, k, 0:TP], rs[:, 0:TP], ALU.mult))
                        mine()
                        dve.tensor_scalar(u[:, k, 0:TP], u[:, k, 0:TP], a[:, k, PROMPT:MC], mod[:, shift0 + k, PROMPT:MC], ALU.mult, ALU.add).then_inc(u_ready, 1)
                    if k >= 1:
                        dve.wait_ge(act_ready, base + k)
                        dve.tensor_tensor(act_lo[:, k - 1, :], u[:, k - 1, :], act_hi[:, k - 1, :].bitcast(F32), ALU.subtract).then_inc(act_split, 1)

            modulated(uT, a_m, 0, 0)

            with dve.Fori(0, PAIRS) as it:
                for what, k in TURN:
                    if what == "ada":
                        ada_evac("pairs", it, POS[what, k], k, ada_rows, psA)
                    elif what == "unit":
                        pos = POS[what, k]
                        if k < 9 and k % 3 == 2:
                            b = k % 2
                            done("pairs", it, pos)
                            dve.tensor_copy(halves(qkvT[:, k, :]), accv[b]).then_inc(acc_free[b], 1)
                        split("pairs", it, pos)
                    elif what == "turn":
                        dve.wait_ge(v_turned, it * 3 + (k + 1))
                        dve.wait_ge(v_out, it * 48 + 16)
                        dve.tensor_copy(vN[:, k, :, :].rearrange("p a b -> p (a b)"), psT[:, 0:512]).then_inc(v_nat, 1)
                        if k == 2:
                            dve.tensor_copy(smpT[:, ds(it, 1), :, :], qkvT[:, :, TP:TC].unsqueeze(1)).then_inc(smpT_ready, 1)
                    elif what == "step":
                        if 0 <= k - 2 < TASKS:
                            j = k - 2
                            r, h = j // 2, j % 2
                            rows = slice(64 * h, 64 * h + 64)
                            dve.wait_ge(o_hid, it * TASKS + (j + 1))
                            hi, lo = (x[rows, ds(it, 1), 0:TP].rearrange("p o (i r) -> p o r i", r=NR)[:, :, r, :] for x in (o_hi, o_lo))
                            dve.tensor_tensor(lo, psO[IDLE[what, k]][rows, :].unsqueeze(1), hi.bitcast(F32), ALU.subtract).then_inc(o_lod, 1)
                        if k < TASKS:
                            dve.wait_ge(scored, it * TASKS + (k + 1))
                            if k >= 2:
                                dve.wait_ge(turned, it * TASKS + (k - 1))
                            dve.memset(seed[:, 10:11], 0.0)
                            dve.tensor_tensor_reduce(S[:, k % 2, :], psS[:, 0:768], mask[:, k // 2, :], -1.0, BIG, ALU.add, ALU.min,
                                                     neg_max[:, k % 2, :]).then_inc(maxed, 1)
                            dve.wait_ge(expd, it * TASKS + (k + 1))
                            dve.reciprocal(rden[:, k % 2, :], den[:, k % 2, :]).then_inc(rdend, 1)
                            dve.wait_ge(rdend, it * TASKS + (k + 1))
                            dve.tensor_scalar(S[:, k % 2, :], S[:, k % 2, :], rden[:, k % 2, :], None, ALU.mult).then_inc(normed, 1)
                    elif what == "fold":
                        modulation(it * NA + NSTART, NA, psM[IDLE[what, k]], it + 2)

            for q in range(4):
                dve.wait_ge(act_ready, 8 + q + 1)
                dve.tensor_tensor(act_lo[:, 2 * q:2 * q + 2, :], uT[:, 2 * q:2 * q + 2, :], act_hi[:, 2 * q:2 * q + 2, :].bitcast(F32),
                                  ALU.subtract).then_inc(pooled_split, 1)
            def sample_scores(i):
                g, h = divmod(i, 2)
                dve.wait_ge(prod_done, i + 1)
                src = kq[2 * (i % 2)][:, :, :].rearrange("p b (s d) -> p b s d", d=HD)
                dve.tensor_reduce(sall[:, g, 4 * h:4 * h + 4, :], src, AX_X, ALU.add).then_inc(score_sum, 1)

            def sample_softmax():
                bs = slice(0, NB * NS)
                dve.wait_ge(smp_back, 16)
                parts = bh[bs, :, :].rearrange("p (g t) d -> p t g d", t=3)
                mark(dve.tensor_tensor(bh_tmp[bs, :, :], parts[:, 0], parts[:, 1], ALU.mult))
                mine()
                mark(dve.tensor_reduce(sc[bs, NG * P:], bh_tmp[bs, :, :], AX_X, ALU.add))
                dve.wait_ge(smp_in, 1)
                mark(dve.tensor_copy(sc[bs, 0:NG * P], psT[bs, 512:512 + NG * P]))
                mine()
                mark(dve.tensor_reduce(bh_stat[bs, 2:3], sc[bs, :], AX_X, ALU.max))
                mine()
                dve.tensor_scalar(bh_stat[bs, 0:1], bh_stat[bs, 2:3], -1.0, None, ALU.mult).then_inc(smp_max, 1)
                dve.wait_ge(smp_exp, 1)
                mark(dve.reciprocal(bh_stat[bs, 3:4], bh_stat[bs, 1:2]))
                mine()
                mark(dve.tensor_scalar(sc[bs, :], sc[bs, :], bh_stat[bs, 3:4], None, ALU.mult))
                mine()
                mark(dve.tensor_scalar(o_new[bs, 0, :], bh[bs, 2, :], sc[bs, NG * P:NG * P + 1], None, ALU.mult))
                for g in range(1, NG):
                    mine()
                    mark(dve.scalar_tensor_tensor(o_new[bs, 0, :], bh[bs, 3 * g + 2, :], sc[bs, NG * P + g:NG * P + g + 1],
                                                  o_new[bs, 0, :], ALU.mult, ALU.add))
                mine()
                dve.tensor_copy(o_new[bs, 1, :], o_new[bs, 0, :]).then_inc(o_new_ready, 1)

            def merge_lo(i):
                dve.wait_ge(act_ready, 12 + i + 1)
                dve.scalar_tensor_tensor(act_lo[:, i, :], tha[:, i, :], 0.5, act_hi[:, i, :].bitcast(F32), ALU.mult, ALU.subtract).then_inc(merged_split, 1)

            for pos, (what, m) in enumerate(MID):
                if what == "map":
                    for q in range(4):
                        i = 4 * m + q
                        dve.wait_ge(mixed_hid, i + 1)
                        dve.scalar_tensor_tensor(halves(mix_lo[:, i, :]), accv[i % 2], vec[:, 80 + i:81 + i], halves(mix_hi[:, i, :].bitcast(F32)), ALU.mult, ALU.subtract).then_inc(acc_free[i % 2], 1)
                    split("mid", 0, pos)
                if what == "ada":
                    ada_evac("mid", 0, pos, m % 4, ada_rows, psA_mid)
                if what == "pp":
                    if m <= 5:
                        sample_scores(m)
                    if m == 6:
                        sample_softmax()
                    if m == 7:
                        dve.wait_ge(smp_turned, 1)
                        dve.tensor_copy(prT[:, :, :].rearrange("p a b -> p (a b)"), psT[:, 0:NG * NB * NS]).then_inc(pr_ready, 1)
                    done("mid", 0, pos)
                    v = halves(thp[:, m, :])
                    dve.scalar_tensor_tensor(v, v, 1.0, accv[m % 2], ALU.add, ALU.mult).then_inc(acc_free[m % 2], 1)
                    split("mid", 0, pos)
                    if m % 4 == 3:
                        modulation(NSTART + PAIRS * NA + m - 3, 4, psM_mid, PAIRS + 2 + m // 4)
                    if m == 7:
                        dve.wait_ge(os_hid, 2)
                        for h in range(2):
                            rows = slice(HD * h, HD * h + HD)
                            src = psT[rows, 0:NB * NS].rearrange("p (b q h) -> p q b h", b=NB, h=2)[:, :, :, h]
                            dve.tensor_tensor(o_lo[rows, :, TP:TC], src, o_hi[rows, :, TP:TC].bitcast(F32), ALU.subtract).then_inc(os_lod, 1)
                        dve.wait_ge(ada_out, PAIRS + 3)
                        gains(gg_m, 16, 56, 0.0)
                        gains(a_f, 32, 64, 1.0)
                if what == "pa":
                    for q in range(2):
                        i = 2 * m + q
                        if i >= 1:
                            merge_lo(i - 1)
                        if q:
                            done("mid", 0, pos)
                        else:
                            dve.wait_ge(part_done, 6 + m + 1)
                        v = halves(tha[:, i, :])
                        dve.scalar_tensor_tensor(v, v, 1.0, accv[i % 2], ALU.add, ALU.mult).then_inc(acc_free[i % 2], 1)
                        dve.wait_ge(acc_free[i % 2], acc_uses["att"][i % 2] + i // 2 + 2)
                        dve.tensor_tensor(tha[:, i, :], tha[:, i, :], thp[:, i, :], ALU.add).then_inc(merged, 1)
                    split("mid", 0, pos)
            merge_lo(7)

            dve.wait_ge(conv_turned, 1)
            for j in range(2):
                src = psT[:, 512 * j:512 * j + NB * 2 * FT].rearrange("p (b m) -> p b m", b=NB)
                w = vec[:, 88 + 44 * j:132 + 44 * j].unsqueeze(1).to_broadcast([P, NB, 2 * FT])
                mark(dve.tensor_tensor(cst[:, j, :].rearrange("p (b m) -> p b m", b=NB), src, w, ALU.mult))
            mine()
            mark(dve.tensor_tensor(hsc[:, :, :].rearrange("p b m -> p (b m)"), cst[:, 0, :], cst[:, 1, :], ALU.add))
            dve.wait_ge(smp_stored, 16)
            dve.wait_ge(new_rows, 16 * 2 * NG)
            mark(dve.memset(ssq[:, :], 0.0))
            mine()

            with dve.Fori(0, 2) as it:
                for k in range(4):
                    dve.wait_ge(acc_free[k % 2], it * 2 + (acc_uses["out"][k % 2] + k // 2 + 2))
                    dve.wait_ge(ssqd, it * 4 + (k + 1))
                    dve.tensor_tensor(ssq[:, :], ssq[:, :], sq[:, k % 2, :], ALU.add).then_inc(ssqd, 1)
                    split("out", it, 2 * k)
                    ada_evac("out", it, 2 * k + 1, k, ada_rows, psA_mid)
                modulation(it * 4 + (NADA - 8), 4, psM_mid, it + (PAIRS + 4))
            dve.wait_ge(ada_out, PAIRS + 5)

            def post_norm(src, gg, roots):
                dve.wait_ge(std_ready, roots)
                mark(dve.reciprocal(rs[:, :], rs[:, :]))
                mine()
                mark(dve.tensor_tensor(small[:, :, :], src[:, :, TP:TC], rs[:, TP:TC].unsqueeze(1).to_broadcast([P, KT, NB]), ALU.mult))
                mine()
                mark(dve.tensor_tensor(small[:, :, :], small[:, :, :], gg[:, :, 0:NB], ALU.mult))
                mine()
                mark(dve.tensor_tensor(xT[:, :, TP:TC], xT[:, :, TP:TC], small[:, :, :], ALU.add))
                for k in range(KT + 1):
                    if k < KT:
                        mark(dve.scalar_tensor_tensor(src[:, k, 0:TP], src[:, k, 0:TP], gg[:, k, PROMPT:MC], rs[:, 0:TP], ALU.mult, ALU.mult))
                        mine()
                        dve.tensor_tensor(xT[:, k, 0:TP], xT[:, k, 0:TP], src[:, k, 0:TP], ALU.add).then_inc(x_upd, 1)

            post_norm(mixT, gg_m, 2)
            gains(gg_f, 40, 72, 0.0)
            for h in (*he[0], *he[1]):
                mark(dve.memset(h[:, 0:2], 0.0))
            dve.wait_ge(std_ready, 3)
            mark(dve.reciprocal(rs[:, :], rs[:, :]))
            mine()
            modulated(norm_u, a_f, 24, 20)
            mark(dve.memset(ssq[:, :], 0.0))
            mine()

            with dve.Fori(0, FT // 2) as it:
                for k in range(4):
                    m, half = k // 2, k % 2
                    dve.wait_ge(acc_free[k % 2], it * 2 + (acc_uses["up"][k % 2] + k // 2 + 2))
                    c, h = cv[half][m], he[half][m]
                    w0, w1 = (vec[:, ds(it * 2 + (88 + 44 * j + m + half * FT), 1)] for j in range(2))
                    dve.tensor_tensor(c[:, TP:TC], c[:, TP:TC], hsc[:, :, ds(it * 2 + (m + half * FT), 1)].rearrange("p b o -> p (b o)"), ALU.add)
                    dve.scalar_tensor_tensor(c[:, 0:TP], h[:, 1:1 + TP], w1, c[:, 0:TP], ALU.mult, ALU.add).then_inc(tap1, 1)
                    dve.wait_ge(tap1, it * 4 + (k + 1))
                    dve.scalar_tensor_tensor(c[:, 0:TP], h[:, 0:TP], w0, c[:, 0:TP], ALU.mult, ALU.add).then_inc(taps, 1)
                    split("up", it, k)
                    if half == 1:
                        dve.wait_ge(gelud, it * 2 + (m + 1))
                        dve.wait_ge(taps, it * 4 + (4 + k + 1))
                        dve.tensor_tensor(gm[m][:, :], gm[m][:, :], c[:, :], ALU.mult).then_inc(gated, 1)
                        dve.wait_ge(g_hid, it * 2 + (m + 1))
                        hi, lo = (x[:, ds(it * 2 + m, 1), :].rearrange("p o n -> p (o n)") for x in (g_hi, g_lo))
                        dve.tensor_tensor(lo, gm[m][:, :], hi.bitcast(F32), ALU.subtract).then_inc(g_lod, 1)

            def down(seg, it):
                for k in range(6):
                    if not (seg == "last" and k >= 4):
                        split(seg, it, k)
                    if k % 3 == 2:
                        b = k // 3
                        dve.wait_ge(acc_free[b], it + (acc_uses[seg][b] + 2))
                        dve.wait_ge(ssqd, it * 2 + ((9 if seg == "down" else 15) + b))
                        dve.tensor_tensor(ssq[:, :], ssq[:, :], sq[:, b, :], ALU.add).then_inc(ssqd, 1)

            with dve.Fori(0, 3) as it:
                down("down", it)
            down("last", 0)
            post_norm(ffn, gg_f, 4)

        @block.tensor
        def _(pe):
            def blocks(b, s, pairs, hi, lo, first=True, last=True):
                for i, (blk, t) in enumerate(pairs):
                    wh, wl = w_hi[:, s, blk * P:(blk + 1) * P], w_lo[:, s, blk * P:(blk + 1) * P]
                    for j, (w, x) in enumerate(((wh, hi), (wh, lo), (wl, hi))):
                        for half in range(2):
                            ins_ = pe.matmul(acc[b][:, half, 0:HALF], w, x[:, t, half * HALF:(half + 1) * HALF],
                                             start=first and i == 0 and j == 0, stop=last and i == len(pairs) - 1 and j == 2)
                return ins_

            def ready(seg, it, pos):
                pe.wait_ge(lo_ready, st.number(seg, it, pos) + 1 + RAW)

            def free(b, uses):
                pe.wait_ge(acc_free[b], uses + 1)

            def ada(s, half, where):
                for k in range(4):
                    at = 2 * MC * (4 * half + k)
                    for j, w in enumerate((w_hi, w_lo)):
                        ins_ = pe.matmul(where, silu2[:, at:at + P], w[:, s, k * 2 * P:(k + 1) * 2 * P],
                                         start=half == 0 and k == 0 and j == 0, stop=half == 1 and k == 3 and j == 1)
                ins_.then_inc(unit_done, 1)

            def turn_rows(rows, n, where):
                for i in range(n):
                    ins_ = pe.matmul(where[:, i * MC:(i + 1) * MC], rows[0:2 * MC, i, :], fold[0:2 * MC, :], start=True, stop=True)
                ins_.then_inc(folded, 1)

            pe.wait_ge(pool_k, 1)
            pe.wait_ge(c_ready, 1)
            for k in range(KT):
                ins_ = pe.transpose(acc[1][:, 0, k * MC:(k + 1) * MC], c_silu[0:MC, k * P:(k + 1) * P], ident[0:MC, 0:MC])
            ins_.then_inc(silu_turned, 1)
            pe.wait_ge(vec_loaded, 16 * 9)
            for i in range(3):
                ins_ = pe.transpose(acc[1][:, 1, 88 * i:88 * i + 88], vec_rows[0:88, i, :], ident[0:88, 0:88])
            ins_.then_inc(vec_turned, 1)

            def sum_squares(src, where, start=True, stop=True):
                for half in range(2):
                    ins_ = pe.matmul(where[half], ones[:, :], src[:, half * HALF:(half + 1) * HALF], start=start, stop=stop)
                ins_.then_inc(summed, 1)

            norm_acc = [psS[:, 0:HALF], psS[:, 512:512 + HALF]]
            pe.wait_ge(silu_out, 1)
            for t in range(NSTART):
                ready("start", 0, t)
                if t >= 4:
                    pe.wait_ge(ada_rowed, t // 2 - 1)
                ada(t % HL, t % 2, start_at(t))
                if t % 2:
                    k = t // 2
                    if k == 0:
                        pe.wait_ge(x_loaded, 32)
                    if k >= 2:
                        pe.wait_ge(x_out, k - 1)
                    for i in range(4):
                        at = 512 * (k % 2) + i * P
                        ins_ = pe.transpose(psT[:, at:at + P], x_rows[:, i, k * P:(k + 1) * P], ident[:, :])
                    ins_.then_inc(x_turned, 1)
            pe.wait_ge(hist_loaded, 16)
            for k in range(KT):
                ins_ = pe.transpose(acc[0][:, 1, 256 + k * NB:256 + (k + 1) * NB], xs_rows[0:NB, k * P:(k + 1) * P], ident[0:NB, 0:NB])
            ins_.then_inc(xs_turned, 1)
            pe.wait_ge(fold_ready, 1)
            pe.wait_ge(ada_rowed, NSTART // 2)
            turn_rows(ada_start, NSTART, psS[:, 0:NSTART * MC])
            pe.wait_ge(xs_out, 1)
            for k in range(KT):
                at = (k % 4) * NB * POOL_HIST
                ins_ = pe.transpose(acc[0][:, k // 4, at:at + NB * POOL_HIST], hist_rows[0:NB * POOL_HIST, k * P:(k + 1) * P],
                                    ident[0:NB * POOL_HIST, 0:NB * POOL_HIST])
            ins_.then_inc(hist_turned, 1)
            for k in range(KT):
                pe.wait_ge(squared, k + 1)
                sum_squares(sq[:, k % 2, :], [acc[1][:, h, 0:HALF] for h in range(2)], k == 0, k == KT - 1)

            def idle_is_read(it, what, k, folds):
                b = IDLE[what, k]
                at = TURN.index((what, k))
                free(b, it * (8 - b) + sum(w == "unit" and u % 2 == b for w, u in TURN[:at]))
                pe.wait_ge(ada_out, it + (1 + folds))

            with pe.Fori(0, PAIRS) as it:
                steps, adas, folds = 0, 0, 0
                for what, k in TURN:
                    if what in ("half", "unit"):
                        halved, pos = ("half", k) in TURN, POS["unit", k]
                        if what == "half" or not halved:
                            ready("pairs", it, pos)
                            free(k % 2, it * (8 - k % 2) + k // 2)
                            pe.wait_ge(o_lod, it * TASKS + (steps + 1))
                            pe.wait_ge(ada_out, it + (1 + folds))
                        if k == 0:
                            pe.wait_ge(act_split, 8)
                        part = range(KT) if not halved else range(KT // 2) if what == "half" else range(KT // 2, KT)
                        ins_ = blocks(k % 2, pos % HL, [(i, i) for i in part], act_hi, act_lo, first=0 in part, last=KT - 1 in part)
                        if what == "unit":
                            ins_.then_inc(unit_done, 1)
                    elif what == "turn":
                        v = 3 * k + 2
                        pe.wait_ge(acc_free[v % 2], it * (8 - v % 2) + (v // 2 + 2))
                        if k:
                            pe.wait_ge(v_nat, it * 3 + k)
                            pe.wait_ge(k_nat, it * 3 + k)
                        for which, t0, done in ((v, 0, v_turned), (v - 1, 512, k_turned)):
                            for r in range(4):
                                if k == 0 and which == v - 1 and r:
                                    continue
                                if k == 0:
                                    src = qkvT[:, which, r * P:(r + 1) * P] if which == v else qkvT[:, which, TP - P:TP]
                                else:
                                    src = qkvT[:, which, 0:TP].rearrange("p (i r) -> p r i", r=NR)[:, r, :]
                                ins_ = pe.transpose(psT[:, t0 + r * P:t0 + (r + 1) * P], src, ident[:, :])
                            ins_.then_inc(done, 1)
                    elif what == "step":
                        if 0 <= k - 2 < TASKS:
                            j = k - 2
                            r, h = j // 2, j % 2
                            rows = slice(64 * h, 64 * h + 64)
                            pe.wait_ge(copied, it * TASKS + (j + 1))
                            idle_is_read(it, what, k, folds)
                            pe.wait_ge(o_lod, it * TASKS + (j + 1))
                            vs = [vN[:, 0, c, rows] for c in range(4)] + [vN[:, 1, r, rows], vN[:, 2, r, rows]]
                            for c in range(6):
                                ins_ = pe.matmul(psO[IDLE[what, k]][rows, :], vs[c], PT[:, j % 2, c * P:(c + 1) * P], start=c == 0, stop=c == 5)
                            ins_.then_inc(weighted, 1)
                            steps = j + 1
                        if k < TASKS:
                            r, h = k // 2, k % 2
                            rows = slice(64 * h, 64 * h + 64)
                            if k:
                                pe.wait_ge(maxed, it * TASKS + k)
                            def cls(i, r=r, rows=rows):
                                return qkvT[rows, i, 0:TP].rearrange("p (i r) -> p r i", r=NR)[:, r, :]
                            pe.matmul(psS[:, 0:TP], cls(0), qkvT[rows, 1, 0:TP], start=True, stop=True)
                            pe.matmul(psS[:, TP:TP + P], cls(3), cls(4), start=True, stop=True)
                            pe.matmul(psS[:, TP + P:TP + 2 * P], cls(6), cls(7), start=True, stop=True).then_inc(scored, 1)
                        if 0 <= k - 1 < TASKS:
                            j = k - 1
                            pe.wait_ge(normed, it * TASKS + (j + 1))
                            if j == 0:
                                pe.wait_ge(v_nat, it * 3 + 3)
                                pe.wait_ge(k_nat, it * 3 + 3)
                            else:
                                pe.wait_ge(copied, it * TASKS + j)
                            pe.wait_ge(ada_rowed, it * 2 + (NSTART // 2 + adas // 2))
                            for c in range(6):
                                ins_ = pe.transpose(psT[:, c * P:(c + 1) * P], S[:, j % 2, c * P:(c + 1) * P], ident[:, :])
                            ins_.then_inc(turned, 1)
                    elif what == "ada":
                        ready("pairs", it, POS[what, k])
                        pe.wait_ge(copied, it * TASKS + steps + 1)
                        pe.wait_ge(ada_rowed, it * 2 + (NSTART // 2 + adas // 2))
                        ada(POS[what, k] % HL, k % 2, psA)
                        adas += 1
                    elif what == "fold":
                        pe.wait_ge(o_lod, it * TASKS + (steps + 1))
                        idle_is_read(it, what, k, folds)
                        pe.wait_ge(ada_rowed, it * 2 + (NSTART // 2 + 2))
                        turn_rows(ada_rows, NA, psM[IDLE[what, k]])
                        folds += 1

            pe.wait_ge(smpT_ready, PAIRS)
            pe.wait_ge(copied, PAIRS * TASKS)
            for p in range(PAIRS):
                ins_ = pe.transpose(psT[0:9 * NB, p * P:(p + 1) * P], smpT[:, p, :, :].rearrange("p a b -> p (a b)"), ident[:, :])
            ins_.then_inc(rows_turned, 1)
            pe.wait_ge(pooled, 4)
            pe.wait_ge(o_lod, PAIRS * TASKS + 1)
            for k in range(KT):
                ins_ = pe.transpose(psS[0:TAIL, k * P:(k + 1) * P], u_tail[:, k, :], ident[:, :])
            ins_.then_inc(tail_turned, 1)

            uses = [4 * 8, 4 * 7]

            def take(b):
                free(b, uses[b])
                uses[b] += 1

            def sample_in():
                pe.wait_ge(score_sum, 6)
                pe.wait_ge(smp_ready, 1)
                for g in range(NG):
                    ins_ = pe.transpose(psT[0:NB * NS, 512 + g * P:512 + (g + 1) * P], sall[:, g, :, :].rearrange("p a b -> p (a b)"), ident[:, :])
                ins_.then_inc(smp_in, 1)

            def sample_turn():
                pe.wait_ge(o_new_ready, 1)
                for g in range(NG):
                    ins_ = pe.transpose(psT[:, g * NB * NS:(g + 1) * NB * NS], sc[0:NB * NS, g * P:(g + 1) * P], ident[0:NB * NS, 0:NB * NS])
                ins_.then_inc(smp_turned, 1)

            def sample_out():
                pe.wait_ge(pr_ready, 1)
                pe.matmul(psT[:, 0:NB * NS], o_new[0:NB * NS, :, :].rearrange("p a b -> p (a b)"), ident[0:NB * NS, 0:NB * NS],
                          start=True, stop=False, skip_group_check=True)
                for i in range(6):
                    g, h = divmod(i, 2)
                    pe.wait_ge(kq_full[i % 4], 16 * (3 + i // 4 + 1))
                    for b in range(4):
                        for hp in range(PAIRS):
                            c = (4 * h + b) * NS + 2 * hp
                            ins_ = pe.matmul(psT[:, c:c + 2], kq[i % 4][:, b, hp * P:(hp + 1) * P], prT[:, g, c:c + 2], start=False,
                                             stop=(i == 5 and b == 3 and hp == PAIRS - 1), skip_group_check=True)
                    ins_.then_inc(v_used, 1)
                pe.matmul(psT[:, 512:513], ident[:, :], eps[:, :], start=True, stop=True).then_inc(smp_summed, 1)

            for pos, (what, m) in enumerate(MID):
                if what == "pa" and m == 0:
                    pe.wait_ge(os_lod, 2)
                ready("mid", 0, pos)
                if what == "map":
                    for q in range(4):
                        g, d = 2 * m + q // 2, q % 2
                        i = 4 * m + q
                        pe.wait_ge(pooled_split, g + 1)
                        take(i % 2)
                        ins_ = blocks(i % 2, pos % HL, [(4 * (q // 2) + 2 * kt + d, 2 * g + kt) for kt in range(2)], act_hi, act_lo)
                        ins_.then_inc(unit_done if q == 3 else part_done, 1)
                if what == "ada":
                    if m == 4:
                        pe.wait_ge(ada_out, PAIRS + 2)
                    pe.wait_ge(tail_ready, 1)
                    pe.wait_ge(ada_rowed, NSTART // 2 + PAIRS * 2 + m // 2)
                    ada(pos % HL, m % 2, psA_mid)
                if what == "pp":
                    take(m % 2)
                    if m == 0:
                        pe.wait_ge(acc_free[1], uses[1] + 1)
                    blocks(m % 2, pos % HL, [(i, i) for i in range(KT)], mix_hi, mix_lo).then_inc(unit_done, 1)
                    if m == 5:
                        sample_in()
                    if m == 6:
                        sample_turn()
                    if m == 7:
                        sample_out()
                    if m % 4 == 3:
                        pe.wait_ge(ada_rowed, NSTART // 2 + PAIRS * 2 + m // 2 + 1)
                        turn_rows(ada_rows, 4, psM_mid)
                if what == "pa":
                    for q in range(2):
                        take(q)
                        ins_ = blocks(q, pos % HL, [(2 * kt + q, kt) for kt in range(4)], o_hi, o_lo)
                        ins_.then_inc(unit_done if q else part_done, 1)
            pe.wait_ge(conv_loaded, 16)
            for j in range(2):
                for b in range(NB):
                    at = 512 * j + b * 2 * FT
                    ins_ = pe.transpose(psT[:, at:at + 2 * FT], conv_rows[0:2 * FT, 2 * b + j, :], ident[0:2 * FT, 0:2 * FT])
            ins_.then_inc(conv_turned, 1)

            with pe.Fori(0, 2) as it:
                for k in range(4):
                    ready("out", it, 2 * k)
                    free(k % 2, it * 2 + (uses[k % 2] + k // 2))
                    if k == 0:
                        pe.wait_ge(merged_split, 8)
                    blocks(k % 2, 0, [(i, i) for i in range(KT)], act_hi, act_lo).then_inc(unit_done, 1)
                    ready("out", it, 2 * k + 1)
                    if k == 0:
                        pe.wait_ge(ada_out, it + (PAIRS + 3))
                    pe.wait_ge(ada_rowed, it * 2 + (NSTART // 2 + PAIRS * 2 + 4 + k // 2))
                    ada(1, k % 2, psA_mid)
                pe.wait_ge(ada_rowed, it * 2 + (NSTART // 2 + PAIRS * 2 + 6))
                turn_rows(ada_rows, 4, psM_mid)
            assert tuple(uses) == acc_uses["out"]

            pe.wait_ge(ssqd, 9)
            pe.wait_ge(ada_out, PAIRS + 5)
            sum_squares(ssq[:, :], norm_acc)
            for k in range(KT):
                pe.wait_ge(squared, KT + k + 1)
                sum_squares(sq[:, k % 2, :], norm_acc, k == 0, k == KT - 1)

            with pe.Fori(0, FT // 2) as it:
                for k in range(4):
                    ready("up", it, k)
                    free(k % 2, it * 2 + (acc_uses["up"][k % 2] + k // 2))
                    if k == 0:
                        pe.wait_ge(act_split, 16)
                    blocks(k % 2, k % HL, [(i, i) for i in range(KT)], act_hi, act_lo).then_inc(unit_done, 1)
            pe.wait_ge(g_lod, FT + 2)
            pe.wait_ge(hu_tailed, 2 * FT + 4)
            for j in range(CONV_TAIL):
                t, at = (psS, psT)[j // 5], j % 5 * P
                ins_ = pe.transpose(t[0:2 * FT, at:at + P], hu_tail[:, :, j], ident[:, :])
                if j % 5 == 4:
                    ins_.then_inc(hu_turned, 1)

            def down(seg, it):
                for k in range(6):
                    ready(seg, it, k)
                    b, part = divmod(k, 3)
                    if part == 0:
                        free(b, it + acc_uses[seg][b])
                    t0 = 8 * part
                    ins_ = blocks(b, k % HL, [(i, t0 + i) for i in range(min(8, FT - t0))], g_hi, g_lo, first=part == 0, last=part == 2)
                    ins_.then_inc(unit_done, 1)

            with pe.Fori(0, 3) as it:
                down("down", it)
            down("last", 0)
            pe.wait_ge(ssqd, 17)
            sum_squares(ssq[:, :], norm_acc)
            for k in range(KT):
                pe.wait_ge(x_upd, KT + k + 1)
                if k >= 2:
                    pe.wait_ge(y_ready, k - 1)
                for t in range(4):
                    at = 512 * (k % 2) + t * P
                    ins_ = pe.transpose(psT[:, at:at + P], xT[:, k, t * P:(t + 1) * P], ident[:, :])
                ins_.then_inc(y_turned, 1)
            for k in range(KT):
                ins_ = pe.transpose(acc[0][0:NB, k // 4, (k % 4) * P:(k % 4 + 1) * P], xT[:, k, TP:TC], ident[:, :])
            ins_.then_inc(ys_turned, 1)


def kernel(**inputs):
    import numpy as np
    from concourse import bacc
    from concourse.bass_utils import run_bass_kernel_spmd

    nc = bacc.Bacc("TRN2", target_bir_lowering=False, num_devices=1, dynamic_dma_scratch_size=1024)
    arrays, ins = {}, {}
    for name, a in inputs.items():
        a = np.ascontiguousarray(a)
        arrays[f"in_{name}"] = a
        ins[name] = nc.dram_tensor(f"in_{name}", a.shape, mybir.dt.from_np(a.dtype), kind="ExternalInput").ap()
    names = []

    def out(name, *shape):
        names.append(f"out_{name}")
        return nc.dram_tensor(f"out_{name}", shape, F32, kind="ExternalOutput").ap()

    outs = {"y": (out("y_prompt", 1, TP, D), out("y_sample", NB, 1, D)), "new": []}
    for w in WINS:
        outs["new"].append([(out(f"{x}{w}_prompt", 1, 1, min(w, TP), NS, HD), out(f"{x}{w}_sample", 1, NB, w, NS, HD)) for x in "kv"])
    outs["pool"] = (out("pool_prompt", 1, 1, POOL_HIST, D), out("pool_sample", 1, NB, POOL_HIST, D))
    outs["conv"] = (out("conv_prompt", 1, 1, 2, 2 * FF), out("conv_sample", 1, NB, 2, 2 * FF))
    program(nc, ins, outs)
    r = run_bass_kernel_spmd(nc, [arrays], core_ids=[0])
    return tuple(r.results[0][n] for n in names)
```

```python
from contextlib import ExitStack

import concourse.bass as bass
from concourse import mybir

F32 = mybir.dt.float32
F32R = mybir.dt.float32r
BF16 = mybir.dt.bfloat16
ALU = mybir.AluOpType
ACT = mybir.ActivationFunctionType
AX_X = mybir.AxisListType.X
ds = bass.ds

P = 128
D = 1024
KT = D // P
TP = 512
NB = 8
TC = TP + NB
HALF = TC // 2
NS, HD = 8, 64
DA = NS * HD
DILS = (1, 4, 16)
NG = len(DILS)
WINS = tuple(P * d for d in DILS)
PAIRS = NS // 2
NR = 4
POOL_HIST = 15
FF = 2816
FT = FF // P
EPS = 1e-6
NEG = -1e30
BIG = 3e38
NADA = 6 * KT
MC = NB + 1
PROMPT = NB
BLK = 8
RAW, HL = 4, 2
UW = BLK * P
TAIL = POOL_HIST + NB
PRW = NB * NS - NS + NB * NB * NS
CONV_TAIL = 2 + NB

TURN = (
    [("unit", k) for k in range(4)] + [("turn", 0)] + [("unit", k) for k in range(4, 7)] + [("turn", 1)]
    + [("unit", 7), ("unit", 8), ("half", 9), ("turn", 2), ("step", 0), ("unit", 9), ("step", 1), ("half", 10), ("step", 2), ("unit", 10),
       ("step", 3), ("ada", 0), ("unit", 11), ("ada", 1), ("step", 4), ("half", 12), ("step", 5), ("unit", 12), ("step", 6),
       ("half", 13), ("step", 7), ("unit", 13), ("step", 8), ("ada", 2), ("unit", 14), ("ada", 3), ("fold", 0), ("step", 9)]
)
STREAMED = [x for x in TURN if x[0] in ("unit", "ada")]
POS = {x: i for i, x in enumerate(STREAMED)}
NA = 4
IDLE, last = {}, 1
for what, k in TURN:
    if what in ("half", "unit"):
        last = k % 2
    else:
        IDLE[what, k] = 1 - last
TURN_UNITS = len(STREAMED)
TASKS = 2 * NR
MID = [("map", 0), ("map", 1)] + [("pp", q) for q in range(8)] + [("pa", q) for q in range(4)]
NSTART = 2 * KT
SEGMENTS = {"start": (1, NSTART), "pairs": (PAIRS, TURN_UNITS), "mid": (1, len(MID)), "out": (2, 4), "up": (11, 4), "down": (3, 6), "last": (1, 6)}


class Stream:

    def __init__(self):
        self.first, self.fills, n, prev = {}, {}, 0, None
        fills = [0] * RAW
        self.dist = {}
        for name, (iters, units) in SEGMENTS.items():
            self.first[name], self.fills[name] = n, list(fills)
            for pos in range(units):
                gaps = []
                if pos >= RAW:
                    gaps = [RAW]
                else:
                    for u in ([units] if iters > 1 else []) + ([prev] if prev else []):
                        gaps.append(pos + u - max(q for q in range(u) if q % RAW == pos % RAW))
                self.dist[name, pos] = min(gaps, default=RAW)
            n += iters * units
            for s in range(RAW):
                fills[s] += iters * len(range(s, units, RAW))
            prev = units
        self.total = n

    def number(self, seg, it, pos):
        return it * SEGMENTS[seg][1] + (self.first[seg] + pos)

    def fill(self, seg, it, pos):
        units = SEGMENTS[seg][1]
        s = (pos - units if pos >= units else pos) % RAW
        per = len(range(s, units, RAW))
        done = per + 1 if pos >= units else pos // RAW + 1
        return it * per + (self.fills[seg][s] + done)


def tiles(x):
    return x.rearrange("(k p) n -> p k n", p=P)


def program(nc, ins, outs):
    st = Stream()
    w_in, w_up, w_down = ins["w_in"][0], ins["w_up"][0], ins["w_down"][0]
    w_ada, w_out = ins["w_ada"][0], ins["w_out"][0]
    caches = [(ins[f"cache_k_w{w}"], ins[f"cache_v_w{w}"]) for w in WINS]
    scratch = nc.dram_tensor("sample_qkv", (3 * NG, NB, DA), F32, kind="Internal").ap()

    with ExitStack() as ctx:
        def sem(name):
            return ctx.enter_context(nc.semaphore(name))

        def psum(name, shape):
            return ctx.enter_context(nc.psum_tensor(name, shape, F32))

        top = [2048]

        def region(nbytes):
            at = top[0]
            top[0] = at + (nbytes + 31) // 32 * 32
            assert top[0] <= 229344, top[0]
            return at

        def put(name, shape, dt, at):
            return nc.alloc_sbuf_tensor_at(name, [P, *shape], dt, offset=at)

        def new(name, shape, dt=F32):
            n = 2 if dt == BF16 else 4
            for s in shape:
                n *= s
            return put(name, shape, dt, region(n))

        FULL = KT * TC * 4
        r_act = region(2 * FULL)
        act_hi, act_lo = put("act_hi", [KT, TC], F32R, r_act), put("act_lo", [KT, TC], F32R, r_act + FULL)
        ffn = put("ffn", [KT, TC], F32, r_act)
        r_x = region(FULL)
        xT = put("xT", [KT, TC], F32, r_x)
        raw = new("raw", [RAW, UW])
        w_hi, w_lo = new("w_hi", [HL, UW], F32R), new("w_lo", [HL, UW], F32R)
        more_hi, more_lo = put("more_hi", [2, UW], F32R, r_act), put("more_lo", [2, UW], F32R, r_act + 8 * UW)
        r_ff = top[0]
        r_z = region(2 * FULL)
        thp, tha = put("thp", [KT, TC], F32, r_z), put("tha", [KT, TC], F32, r_z + FULL)
        x_rows = put("x_rows", [4, D], F32, r_z)
        xs_rows = put("xs_rows", [D], F32, r_z + FULL)
        c_rows, c_tanh, c_silu = (put(n, [D], F32, r_z + FULL + 4096 * i) for i, n in ((1, "c_rows"), (2, "c_tanh"), (3, "c_silu")))
        r_u = region(FULL)
        uT = put("uT", [KT, TC], F32, r_u)
        mix_hi = put("mixed_hi", [KT, TC], F32R, r_u)
        mixT = put("mixT", [KT, TC], F32, r_u)
        norm_u = put("norm_u", [KT, TC], F32, r_z)
        r_att = region(9 * TC * 4)
        qkvT = put("qkvT", [9, TC], F32, r_att)
        mix_lo = put("mixed_lo", [KT, TC], F32R, r_att)
        o_hi, o_lo = new("o_hi", [PAIRS, TC], F32R), new("o_lo", [PAIRS, TC], F32R)
        r_rows = region(NA * P * 4)
        ada_rows = put("ada_rows", [NA, P], F32, r_rows)
        r_ada = region(4 * UW * 4)
        ada_start = put("ada_start", [NSTART, P], F32, r_ada)
        vN = new("vN", [NG, 4, P])
        kN = new("kN", [4, P])
        mask = new("mask", [NR, 768], BF16)
        r_s = region(2 * 768 * 4)
        S = put("S", [2, 768], F32, r_s)
        sq = put("sq", [2, TC], F32, r_s)
        r_pt = region(2 * 768 * 4)
        PT = put("PT", [2, 768], F32, r_pt)
        ssq = put("ssq", [TC], F32, r_pt + 2080)
        pw = new("pw", [2, 16 + TP])
        vec_rows = put("vec_rows", [3, P], F32, r_u)
        hist_rows = put("hist_rows", [D], F32, r_u + 2048)
        mod = new("mod", [NADA, MC])
        silu2 = new("silu2", [KT * 2 * MC + P - 2 * MC], F32R)
        siluT = new("siluT", [KT, MC])
        sel = new("sel", [NG * NB], F32R)
        own_head, own_sample = new("own_head", [NS]), new("own_sample", [NB])
        fold = new("fold", [MC])
        vec = new("vec", [3 * 88])
        a_m, a_f, gg_m, gg_f = (new(n, [KT, MC]) for n in ("a_m", "a_f", "gg_m", "gg_f"))
        ident, ones = new("ident", [P]), new("ones", [P])
        smpT = new("smpT", [PAIRS, 9, NB])
        u_tail = new("u_tail", [KT, TAIL])
        hist_sum = new("hist_sum", [KT, NB])
        inv_count = new("inv_count", [16])
        eps = new("eps", [1])
        nrm = new("nrm", [6, 5])
        ind4 = new("ind4", [2, 4])
        neg_max, den, rden = new("neg_max", [2, 1]), new("den", [2, 1]), new("rden", [2, 1])
        small = new("small", [KT, NB])
        seed = new("seed", [14])
        r_more = r_ada + 16384
        slots = [put(f"cached{i}", [4, DA], F32, r_ada + 8192 * i if i < 2 else r_act + 8192 * (i - 2)) for i in range(6)]
        kS = [slots[i] for i in (0, 1, 2, 3, 0, 1)]
        qB = [put(f"qB{i}", [4, DA], F32, r_more + 8192 * i) for i in range(2)]
        vS = [slots[i] for i in (4, 5, 2, 3, 0, 1)]
        prT = put("prT", [NG, PRW], F32, r_more)
        qhl = put("qhl", [DA], F32R, r_rows)
        ada_raw = put("ada_raw", [4, UW], F32, r_z + FULL)
        r_sa = r_more + 16384
        bh = put("bh", [9, HD], F32, r_sa)
        sc = put("sc", [NG * P + NG], F32, r_sa + 2304)
        sall = put("sall", [NG, NB, NS], F32, r_sa + 2304 + 1568)
        o_new = put("o_new", [HD], F32, r_sa + 2304 + 1568 + 1536)
        bh_tmp = put("bh_tmp", [NG, HD], F32, r_sa + 2304 + 1568 + 2048)
        bh_stat = put("bh_stat", [4], F32, r_sa + 2304 + 1568 + 2816)
        smp_rows = put("smp_rows", [DA], F32, r_sa + 2304 + 1568 + 2848)
        o_rows = put("o_rows", [NS, HD], F32, r_sa + 2304 + 1568 + 2848)
        assert r_sa + 2304 + 1568 + 2848 + 2048 <= r_pt + 6144
        tail_rows = put("tail_rows", [D], F32, r_pt + 6144)
        g_hi, g_lo = put("g_hi", [FT, TC], F32R, r_ff), put("g_lo", [FT, TC], F32R, r_ff + FT * TC * 4)
        r_cv = r_ff + 2 * FT * TC * 4
        cv = [[put(f"cv{a}{b}", [TC], F32, r_cv + (2 * a + b) * 2080) for b in range(2)] for a in range(2)]
        gm = [put(f"gm{b}", [TC], F32, r_cv + (4 + b) * 2080) for b in range(2)]
        late_rows = put("late_rows", [NA, P], F32, r_cv + 4 * 2080)
        r_he = r_cv + 6 * 2080
        he = [[put(f"he{a}{b}", [2 + TC], F32, r_he + (2 * a + b) * 2112) for b in range(2)] for a in range(2)]
        r_cs = r_he + 4 * 2112
        hsc = put("hsc", [NB, 2 * FT], F32, r_cs)
        assert r_cs + NB * 2 * FT * 4 <= r_s
        hu_tail = put("hu_tail", [2 * FT, CONV_TAIL], F32, r_pt + 6144)
        conv_rows = put("conv_rows", [2 * NB, P], F32, r_ada)
        cst = put("cst", [2, NB * 2 * FT], F32, r_ada + 8192)
        hu_rows = put("hu_rows", [CONV_TAIL, P], F32, r_cv)
        y_rows = put("y_rows", [4, D], F32, r_ff)
        ys_rows = put("ys_rows", [D], F32, r_ff + 16384)

        acc = [psum("acc0", [P, 2, 512]), psum("acc1", [P, 2, 512])]
        psS = psum("psS", [P, 1024])
        psT = psum("psT", [P, 1024])
        psO, psM = [a[:, 0, 264:392] for a in acc], [a[:, 1, 264:264 + NA * MC] for a in acc]
        rs_p, rs_s = psS[:, 0:TP], psS[:, TP + P - NB:TP + P]
        psA, psA_mid, psM_mid = psS[:, 768:1024], psT[:, 0:256], psT[:, 512:512 + NA * MC]
        accv = [a[:, :, 0:HALF] for a in acc]
        def x_tiles(t):
            return [] if t < 3 or t % 2 == 0 else [(t - 3) // 2] if t < NSTART - 1 else [KT - 2, KT - 1]

        def slot(seg, pos):
            if seg == "start" and pos < NSTART and pos % 4 >= 2:
                return more_hi[:, pos % 2, :], more_lo[:, pos % 2, :]
            return w_hi[:, pos % HL, :], w_lo[:, pos % HL, :]

        psR = acc[1][:, 0, 400:405]

        def start_at(t):
            return psS[:, 512 * (t // 2 % 2):512 * (t // 2 % 2) + 256]

        acc_uses, used = {}, [0, 0]
        for name, counts in (("pairs", (PAIRS * 8, PAIRS * 7)), ("map", (4, 4)), ("pool", (4, 4)), ("att", (4, 4)), ("out", (4, 4)),
                             ("up", (FT, FT)), ("down", (3, 3)), ("last", (1, 1))):
            acc_uses[name] = tuple(used)
            used = [u + c for u, c in zip(used, counts)]

        def halves(x):
            return x.rearrange("p (a b) -> p a b", a=2)

        def halves_at(x, i):
            return x[:, ds(i, 1), :].rearrange("p o (a b) -> p o a b", a=2)

        raw_full = [sem(f"raw_full{i}") for i in range(RAW)]
        kS_full = [sem(f"kS_full{i}") for i in range(4)]
        vS_full = sem("vS_full")
        ada_full = [sem(f"ada_full{i}") for i in range(4)]
        ada_done = sem("ada_done")
        q_split, q_cast, q_out, pr_zeroed, pv_done = sem("q_split"), sem("q_cast"), sem("q_out"), sem("pr_zeroed"), sem("pv_done")
        masks_ready, o_rowed = sem("masks_ready"), sem("o_rowed")
        hi_ready, lo_ready = sem("hi_ready"), sem("lo_ready")
        unit_done, part_done = sem("unit_done"), sem("part_done")
        acc_free = [sem("acc_free0"), sem("acc_free1")]
        ada_rowed, folded, ada_out = sem("ada_rowed"), sem("folded"), sem("ada_out")
        c_loaded, vec_loaded, x_loaded, hist_loaded, conv_loaded = (
            sem(x) for x in ("c_loaded", "vec_loaded", "x_loaded", "hist_loaded", "conv_loaded"))
        pool_k, pool_step, pooled = sem("pool_constants"), sem("pool_step"), sem("pooled")
        dve_step = sem("dve_step")
        c_tanhed, c_ready, silu_turned, silu_out, vec_turned, vec_out = (
            sem(x) for x in ("c_tanhed", "c_ready", "silu_turned", "silu_out", "vec_turned", "vec_out"))
        xs_loaded = sem("xs_loaded")
        x_turned, x_out, xs_turned, xs_out, hist_turned, hist_ready = (
            sem(x) for x in ("x_turned", "x_out", "xs_turned", "xs_out", "hist_turned", "hist_ready"))
        squared, summed, mean_ready, std_ready, rooted, rs_ready = (
            sem(x) for x in ("squared", "summed", "mean_ready", "std_ready", "rooted", "rs_ready"))
        xr_ready = sem("xr_ready")
        u_ready, act_ready, act_split, x_upd = sem("u_ready"), sem("act_ready"), sem("act_split"), sem("x_upd")
        v_turned, k_turned, v_nat, k_nat = sem("v_turned"), sem("k_turned"), sem("v_nat"), sem("k_nat")
        v_out, k_out = sem("v_out"), sem("k_out")
        scored, maxed, expd, rdend, normed = sem("scored"), sem("maxed"), sem("expd"), sem("rdend"), sem("normed")
        turned, copied, weighted, o_hid, o_lod = sem("turned"), sem("copied"), sem("weighted"), sem("o_hid"), sem("o_lod")
        smpT_ready, rows_turned, smp_ready, smp_stored, smp_back, new_rows = (
            sem(x) for x in ("smpT_ready", "rows_turned", "smp_ready", "smp_stored", "smp_back", "new_rows"))
        tail_turned, tail_ready, tail_stored = sem("tail_turned"), sem("tail_ready"), sem("tail_stored")
        pooled_split, mixed_hid, merged, merged_split = sem("pooled_split"), sem("mixed_hid"), sem("merged"), sem("merged_split")
        prod_done, score_sum, smp_in, smp_max, smp_exp = sem("prod_done"), sem("score_sum"), sem("smp_in"), sem("smp_max"), sem("smp_exp")
        o_new_ready, smp_turned, pr_ready, v_used, smp_summed, os_hid, os_lod = (
            sem(x) for x in ("o_new_ready", "smp_turned", "pr_ready", "v_used", "smp_summed", "os_hid", "os_lod"))
        conv_used = sem("conv_used")
        conv_turned, ssqd = sem("conv_turned"), sem("ssqd")
        tap1, taps, hu_tailed, gelud, gated, g_hid, g_lod = (
            sem(x) for x in ("tap1", "taps", "hu_tailed", "gelud", "gated", "g_hid", "g_lod"))
        hu_turned, hu_rowed, y_turned, ys_turned, y_ready, ys_ready, y_out = (
            sem(x) for x in ("hu_turned", "hu_rowed", "y_turned", "ys_turned", "y_ready", "ys_ready", "y_out"))
        silu_zeroed, silu_hid, fold_ready = sem("silu_zeroed"), sem("silu_hid"), sem("fold_ready")
        copy_done, rows_done = sem("copy_done"), sem("rows_done")

        block = ctx.enter_context(nc.Block())

        @block.sync
        def _(sp):
            def unit(seg, it, pos, src, cols=UW):
                sp.wait_ge(lo_ready, st.number(seg, it, pos) - st.dist[seg, pos] + 1 + RAW)
                s = pos % RAW
                sp.dma_start(raw[:, s, 0:cols].rearrange("p (k n) -> p k n", n=src.shape[-1]), src).then_inc(raw_full[s], 16)

            def block_of(w, at, cols=P):
                return tiles(w)[:, :, ds(at, cols)]

            def ada_of(t, half):
                return tiles(w_ada)[:, half * 4:half * 4 + 4, ds(t * P, 2 * P)]

            def shifted(g, kv):
                j, n = ((4, 1016), (16, 1022), (89, 736))[g]
                a = caches[g][kv][0].rearrange("b l s d -> b (l s d)")[:, DA:]
                o = outs["new"][g][kv][1][0].rearrange("b l s d -> b (l s d)")[:, 0:(WINS[g] - 1) * DA]
                return tuple(x.rearrange("b (e j n) -> e b j n", e=16, n=n) for x in (o, a)), j

            def copy(g, j):
                for kv in range(2):
                    (o, a), _ = shifted(g, kv)
                    sp.dma_start(o[:, :, ds(j, 1), :], a[:, :, ds(j, 1), :]).then_inc(copy_done, 16)

            sp.dma_start(c_rows[0:NB, :], ins["c_sample"]).then_inc(c_loaded, 16)
            sp.dma_start(c_rows[NB:MC, :], ins["c_prompt"]).then_inc(c_loaded, 16)
            sp.dma_start(xs_rows[0:NB, :], ins["x_sample"].rearrange("b t n -> (b t) n")).then_inc(xs_loaded, 16)
            rows = lambda x: x.rearrange("a (m c) -> (a m) c", c=P)
            sp.dma_start(vec_rows[0:48, 0, :], rows(ins["b_ada"])).then_inc(vec_loaded, 16)
            for i, n in enumerate(("g_pre_mix", "g_post_mix", "g_pre_ffn", "g_post_ffn", "pool_scale")):
                sp.dma_start(vec_rows[48 + 8 * i:56 + 8 * i, 0, :], rows(ins[n])).then_inc(vec_loaded, 16)
            wc = rows(ins["w_conv"][0])
            sp.dma_start(vec_rows[0:88, 1, :], wc[0:88, :]).then_inc(vec_loaded, 16)
            sp.dma_start(vec_rows[0:44, 2, :], wc[88:132, :]).then_inc(vec_loaded, 16)
            sp.dma_start(vec_rows[44:88, 2, :], rows(ins["b_conv"])).then_inc(vec_loaded, 16)
            for t in range(NSTART):
                unit("start", 0, t, ada_of(t - t % 2, t % 2))
                if t == 3:
                    sp.dma_start(x_rows[:, :, :], ins["x_prompt"][0].rearrange("(t p) n -> p t n", p=P)).then_inc(x_loaded, 16)
            sp.dma_start(hist_rows[0:NB * POOL_HIST, :], ins["state_pool"][0].rearrange("b t n -> (b t) n")).then_inc(hist_loaded, 16)

            with sp.Fori(0, PAIRS) as it:
                for pos, (what, k) in enumerate(STREAMED):
                    if what == "ada":
                        unit("pairs", it, pos, ada_of(it * NA + (NSTART + k - k % 2), k % 2))
                        continue
                    if k < 9:
                        g, part = divmod(k, 3)
                        at = it * P + (D + part * NG * DA + g * DA)
                    elif k < 11:
                        at = it * (2 * P) + (k - 9) * P
                    else:
                        at = it * (2 * P) + (D + 3 * NG * DA + (k - 11) // 2 * D + (k - 11) % 2 * P)
                    unit("pairs", it, pos, block_of(w_in, at))
                    if k in (1, 3, 4, 6, 7, 9, 10, 12, 13):
                        copy(2, it * 9 + (1, 3, 4, 6, 7, 9, 10, 12, 13).index(k))
                    if k in (0, 2, 5, 11):
                        copy(1, it * 4 + (0, 2, 5, 11).index(k))
                    if k == 8:
                        copy(0, it)
                    if k in (8, 11, 14):
                        g = (k - 8) // 3
                        for kv, (src, ready, done) in enumerate(((kN[:, :, :], k_nat, k_out), (vN[:, g, :, :], v_nat, v_out))):
                            sp.wait_ge(ready, it * 3 + (g + 1))
                            o = outs["new"][g][kv][0][0, 0].rearrange("t s d -> t (s d)")[:, ds((it + PAIRS) * P - DA, P)]
                            if g:
                                o = o.rearrange("(i r) c -> i r c", r=NR)
                            else:
                                src = src[:, 0, :] if kv == 0 else src[:, 3, :]
                            sp.dma_start(o, src).then_inc(done, 16)

            for i in range(2):
                wm = ins["w_pool_map"][0, 2 * i:2 * i + 2].rearrange("g (k p) n -> p (g k) n", p=P)
                unit("mid", 0, MID.index(("map", i)), wm)
            def cached(i, kv):
                g, h = divmod(i, 2)
                return caches[g][kv][0, 4 * h:4 * h + 4].rearrange("b (i e) s d -> i b e (s d)", e=DILS[g])[:, :, 0, :]

            def load_k(i):
                if i == 2:
                    sp.wait_ge(unit_done, st.number("mid", 0, 2))
                if i >= 4:
                    sp.wait_ge(score_sum, i - 3)
                sp.dma_start(kS[i][:, :, :], cached(i, 0)).then_inc(kS_full[i % 4], 16)

            def load_v(i):
                if i >= 2:
                    sp.wait_ge(score_sum, i + 1)
                sp.dma_start(vS[i][:, :, :], cached(i, 1)).then_inc(vS_full, 16)

            def proj_pool(i):
                unit("mid", 0, MID.index(("pp", i)), block_of(ins["w_proj_pool"][0], i * P))

            def proj_att(i):
                unit("mid", 0, MID.index(("pa", i)), tiles(ins["w_proj_att"][0])[:, :, i * 2 * P:(i + 1) * 2 * P])

            load_k(0)
            load_k(1)
            proj_pool(0)
            proj_pool(1)
            sp.wait_ge(smp_ready, 1)
            sp.dma_start(scratch.rearrange("m b n -> (m b) n"), smp_rows[0:3 * NG * NB, :]).then_inc(smp_stored, 16)
            for g in range(NG):
                for kv in range(2):
                    o = outs["new"][g][kv][1][0, :, WINS[g] - 1].rearrange("b s d -> b (s d)")
                    r0 = ((1 + kv) * NG + g) * NB
                    sp.dma_start(o, smp_rows[r0:r0 + NB, :]).then_inc(new_rows, 16)
            sp.wait_ge(smp_stored, 16)
            sp.dma_start(bh[0:NB * NS, :, :], scratch.rearrange("m b (h d) -> (b h) m d", d=HD)).then_inc(smp_back, 16)
            for i in range(2, 6):
                proj_pool(i)
            load_k(2)
            load_k(3)
            proj_pool(6)
            load_k(4)
            load_v(0)
            proj_pool(7)
            load_k(5)
            load_v(1)
            proj_att(0)
            load_v(2)
            proj_att(1)
            load_v(3)
            proj_att(2)
            load_v(4)
            load_v(5)
            proj_att(3)
            sp.dma_start(outs["pool"][1][0, :, 0:POOL_HIST - 1], ins["state_pool"][0, :, 1:]).then_inc(rows_done, 16)
            sp.wait_ge(tail_ready, 1)
            sp.dma_start(outs["pool"][0][0, 0], tail_rows[0:POOL_HIST, :]).then_inc(tail_stored, 16)
            sp.dma_start(outs["pool"][1][0, :, POOL_HIST - 1], tail_rows[POOL_HIST:TAIL, :]).then_inc(tail_stored, 16)
            sp.dma_start(outs["conv"][1][0, :, 0], ins["state_conv"][0, :, 1]).then_inc(rows_done, 16)
            sp.wait_ge(pv_done, 1)
            sp.dma_start(conv_rows[0:2 * FT, :, :], ins["state_conv"][0].rearrange("b j (m c) -> m (b j) c", c=P)).then_inc(conv_loaded, 16)
            with sp.Fori(0, 2) as it:
                for k in range(4):
                    unit("out", it, k, block_of(w_out, it * (4 * P) + k * P))
                sp.wait_ge(merged_split, 8)
                for k in range(4):
                    sp.wait_ge(ada_done, it * 4 + (k + 1))
                    sp.dma_start(ada_raw[:, k, :].rearrange("p (k n) -> p k n", n=2 * P), ada_of(it * 4 + (NADA - 16 + k - k % 2), k % 2)).then_inc(ada_full[k], 16)
            def last_ada(t):
                sp.wait_ge(ada_done, 8 + t + 1)
                sp.dma_start(ada_raw[:, t % 4, :].rearrange("p (k n) -> p k n", n=2 * P), ada_of(NADA - 8 + t - t % 2, t % 2)).then_inc(ada_full[t % 4], 16)

            def up(it):
                for k in range(4):
                    unit("up", it, k, block_of(w_up, it * (2 * P) + (k // 2 * P + k % 2 * FF)))
                    copy(2, it * 4 + (36 + k))

            for t in range(4):
                last_ada(t)
            up(0)
            for t in range(4, 8):
                last_ada(t)
            with sp.Fori(1, FT // 2) as it:
                up(it)
            def down(seg, it, m0):
                for k in range(6):
                    r0, r1 = 8 * (k % 3), min(8 * (k % 3) + 8, FT)
                    unit(seg, it, k, tiles(w_down)[:, r0:r1, ds(m0 + k // 3 * P, P)], cols=(r1 - r0) * P)
                    if seg == "down" and k % 2 == 1:
                        copy(2, it * 3 + (80 + k // 2))

            with sp.Fori(0, 3) as it:
                down("down", it, it * (2 * P))
            down("last", 0, 6 * P)
            sp.wait_ge(hu_rowed, 2)
            for j in range(CONV_TAIL):
                o = outs["conv"][0][0, 0, j] if j < 2 else outs["conv"][1][0, j - 2, 1]
                sp.dma_start(o.rearrange("(m c) -> m c", c=P), hu_rows[0:2 * FT, j, :]).then_inc(rows_done, 16)
            for q in range(4):
                sp.wait_ge(y_ready, 2 * q + 2)
                o = outs["y"][0][0].rearrange("(t p) n -> p t n", p=P)
                sp.dma_start(o[:, :, 2 * P * q:2 * P * q + 2 * P], y_rows[:, :, 2 * P * q:2 * P * q + 2 * P]).then_inc(y_out, 16)
            sp.wait_ge(ys_ready, 1)
            sp.dma_start(outs["y"][1].rearrange("b t n -> (b t) n"), ys_rows[0:NB, :]).then_inc(y_out, 16)
            sp.wait_ge(y_out, 16 * 5)
            sp.wait_ge(rows_done, 16 * (2 + CONV_TAIL))
            sp.wait_ge(new_rows, 16 * 2 * NG)
            sp.wait_ge(tail_stored, 32)
            sp.wait_ge(copy_done, 16 * 2 * (89 + 16 + 4))
            sp.wait_ge(k_out, 16 + 16 * 12)
            sp.wait_ge(v_out, 16 + 16 * 12)

        @block.gpsimd
        def _(pool):
            n = [0]

            def step(ins_):
                n[0] += 1
                ins_.then_inc(pool_step, 1)
                pool.wait_ge(pool_step, n[0])

            step(pool.memset(ident[:, :], 0.0))
            step(pool.memset(ones[:, :], 1.0))
            step(pool.memset(eps[:, :], EPS))
            pool.affine_select(out=ident[:, :], in_=ident[:, :], compare_op=ALU.not_equal, fill=1.0, base=0,
                               pattern=[[-1, P]], channel_multiplier=1).then_inc(pool_k, 1)
            step(pool.memset(mask[:, :, :], 0.0))
            step(pool.memset(pw[:, :, 0:16], 0.0))
            for t in range(16):
                step(pool.memset(inv_count[:, t:t + 1], 1.0 / (t + 1)))
            for r in range(NR):
                m0, m1 = mask[:, r, 0:TP], mask[:, r, TP:TP + P]
                step(pool.affine_select(out=m0, in_=m0, compare_op=ALU.is_ge, fill=NEG, base=r, pattern=[[-1, TP]], channel_multiplier=4))
                step(pool.affine_select(out=m0, in_=m0, compare_op=ALU.is_ge, fill=NEG, base=P - r, pattern=[[1, TP]], channel_multiplier=-4))
                step(pool.affine_select(out=m1, in_=m1, compare_op=ALU.is_ge, fill=NEG, base=0, pattern=[[-1, P]], channel_multiplier=1))
                m2 = mask[:, r, TP + P:TP + 2 * P]
                ins_ = pool.affine_select(out=m2, in_=m2, compare_op=ALU.is_ge, fill=NEG, base=0, pattern=[[-1, P]], channel_multiplier=1)
                if r == NR - 1:
                    ins_.then_inc(pool_k, 1)
                else:
                    step(ins_)

            def sum_tiles(base):
                for k in range(KT):
                    pool.wait_ge(squared, (0 if base == 1 else KT) + k + 1)
                    if k == 0:
                        pool.tensor_copy(ssq[:, :], sq[:, 0, :]).then_inc(ssqd, 1)
                    else:
                        pool.wait_ge(ssqd, base + k)
                        pool.tensor_tensor(ssq[:, :], ssq[:, :], sq[:, k % 2, :], ALU.add).then_inc(ssqd, 1)

            sum_tiles(1)

            for gi in range(4):
                win = 2 ** (gi + 1)
                pool.wait_ge(acc_free[0], 1 + 8 * gi + 6)
                t0 = 2 * gi
                step(pool.tensor_copy(u_tail[:, t0:t0 + 2, :], uT[:, t0:t0 + 2, TP - POOL_HIST:TC]))
                for t in (t0, t0 + 1):
                    u = uT[:, t, 0:TP]
                    step(pool.tensor_copy(pw[:, 0, 16:17], uT[:, t, 0:1]))
                    step(pool.tensor_tensor(pw[:, 0, 17:16 + TP], uT[:, t, 1:TP], uT[:, t, 0:TP - 1], ALU.add))
                    b = 0
                    for lv in range(1, gi + 1):
                        sh = 2 ** lv
                        step(pool.tensor_tensor(pw[:, 1 - b, 16:16 + TP], pw[:, b, 16:16 + TP], pw[:, b, 16 - sh:16 + TP - sh], ALU.add))
                        b = 1 - b
                    head = win - 1
                    step(pool.tensor_tensor(pw[:, b, 16:16 + head], pw[:, b, 16:16 + head], inv_count[:, 0:head], ALU.mult))
                    step(pool.tensor_scalar(pw[:, b, 16 + head:16 + TP], pw[:, b, 16 + head:16 + TP], 1.0 / win, 0.0, ALU.mult, ALU.add))
                    step(pool.tensor_tensor(u, pw[:, b, 16:16 + TP], u, ALU.subtract))
                if gi == 0:
                    pool.wait_ge(hist_ready, 1)
                us = uT[:, t0:t0 + 2, TP:TC]
                tmp = pw[:, 0, 16:32].rearrange("p (a b) -> p a b", a=2)
                step(pool.tensor_tensor(tmp, us, hist_sum[:, t0:t0 + 2, :], ALU.add))
                step(pool.tensor_scalar(tmp, tmp, 1.0 / win, 0.0, ALU.mult, ALU.add))
                pool.tensor_tensor(us, tmp, us, ALU.subtract).then_inc(pooled, 1)
                if gi < 3:
                    pool.wait_ge(pooled, gi + 1)

            for i in range(6):
                pool.wait_ge(kS_full[i % 4], 16 * (i // 4 + 1))
                pool.wait_ge(q_out, 4 * i + 4)
                pool.tensor_tensor(kS[i][:, :, :], kS[i][:, :, :], qB[i % 2][:, :, :], ALU.mult).then_inc(prod_done, 1)
            pool.wait_ge(prod_done, 6)
            pool.memset(prT[:, :, :], 0.0).then_inc(pr_zeroed, 1)

            for i in range(8):
                pool.wait_ge(acc_free[i % 2], acc_uses["att"][i % 2] + i // 2 + 2)
                pool.tensor_tensor(tha[:, i, :], tha[:, i, :], thp[:, i, :], ALU.add).then_inc(merged, 1)

            sum_tiles(17)

            pool.wait_ge(tail_stored, 32)
            with pool.Fori(0, FT // 2) as it:
                for k in range(4):
                    pool.wait_ge(acc_free[k % 2], it * 2 + (acc_uses["up"][k % 2] + k // 2 + 2))
                    m, half = k // 2, k % 2
                    pool.tensor_copy(hu_tail[:, ds(it * 2 + (m + half * FT), 1), :], he[half][m][:, 2 + TP - 2:2 + TC].unsqueeze(1)).then_inc(hu_tailed, 1)

        @block.scalar
        def _(act):
            def split(seg, it, pos, ahead=2):
                units = SEGMENTS[seg][1]
                if units % 2 and pos >= units - 2:
                    if pos == units - 2:
                        return
                    if ahead == 2:
                        split(seg, it, pos, 1)
                pos += ahead
                s = pos - units if pos >= units else pos
                cols = 6 * P if seg in ("down", "last") and pos in (2, 5) else UW
                act.wait_ge(raw_full[s % RAW], st.fill(seg, it, pos) * 16)
                act.activation(slot(seg if pos < units else "", s)[0][:, 0:cols], raw[:, s % RAW, 0:cols], ACT.Copy).then_inc(hi_ready, 1)

            def done(seg, it, pos):
                act.wait_ge(unit_done, st.number(seg, it, pos) + 1)

            act.wait_ge(c_loaded, 32)
            act.activation(c_tanh[0:MC, :], c_rows[0:MC, :], ACT.Tanh, scale=0.5).then_inc(c_tanhed, 1)
            silu_hi = silu2[:, 0:KT * 2 * MC].rearrange("p (k j c) -> p k j c", k=KT, j=2)[:, :, 0, :]
            split("start", 0, -2)
            act.wait_ge(silu_turned, 1)
            act.wait_ge(silu_zeroed, 1)
            act.activation(siluT[:, :, :], acc[1][:, 0, 0:KT * MC].rearrange("p (k c) -> p k c", k=KT), ACT.Copy, scale=0.5)
            act.activation(silu_hi, acc[1][:, 0, 0:KT * MC].rearrange("p (k c) -> p k c", k=KT), ACT.Copy, scale=0.5).then_inc(silu_hid, 1)
            split("start", 0, -1)
            act.wait_ge(xs_turned, 1)
            act.activation(xT[:, :, TP:TC], acc[0][:, 1, 256:256 + KT * NB].rearrange("p (a b) -> p a b", a=KT), ACT.Copy).then_inc(xs_out, 1)
            act.wait_ge(vec_turned, 1)
            act.activation(vec[:, :], acc[1][:, 1, 0:3 * 88], ACT.Copy).then_inc(vec_out, 1)
            split("start", 0, 0)
            split("start", 0, 1)
            for t in range(NSTART):
                done("start", 0, t)
                if t + 4 < NSTART:
                    split("start", 0, t + 2)
                for k in x_tiles(t):
                    act.wait_ge(x_turned, k + 1)
                    act.activation(xT[:, k, 0:TP], psT[:, 512 * (k % 2):512 * (k % 2) + 512], ACT.Copy).then_inc(x_out, 1)
                    act.wait_ge(x_out, k + 1)
                    act.wait_ge(xs_out, 1)
                    if k >= 2:
                        act.wait_ge(ssqd, k)
                    act.activation(sq[:, k % 2, :], xT[:, k, :], ACT.Square).then_inc(squared, 1)
            split("start", 0, NSTART - 2)
            split("start", 0, NSTART - 1)

            def root(n):
                act.wait_ge(mean_ready, n)
                act.activation(nrm[:, 1, :], nrm[:, 0, :], ACT.Sqrt).then_inc(std_ready, 1)

            def modulate(u, a, shift0, before):
                for k in range(KT):
                    act.wait_ge(xr_ready, before + k + 1)
                    act.activation(u[:, k, 0:TP], u[:, k, 0:TP], ACT.Identity, bias=mod[:, shift0 + k, PROMPT:MC], scale=a[:, k, PROMPT:MC]).then_inc(u_ready, 1)
                    act.wait_ge(u_ready, before + k + 1)
                    act.activation(act_hi[:, k, :], u[:, k, :], ACT.Copy).then_inc(act_ready, 1)

            root(1)
            modulate(uT, a_m, 0, 0)
            act.activation(seed[:, 12:13], eps[:, :], ACT.Tanh)

            with act.Fori(0, PAIRS) as it:
                for what, k in TURN:
                    if what in ("unit", "ada"):
                        pos = POS[what, k]
                        done("pairs", it, pos)
                    if what == "ada":
                        split("pairs", it, pos)
                    elif what == "unit":
                        b = k % 2
                        if k >= 9:
                            split("pairs", it, pos)
                        if k < 9 and k % 3 != 2:
                            act.activation(halves(qkvT[:, k, :]), accv[b], ACT.Copy, scale=0.125 if k % 3 == 0 else 1.0).then_inc(acc_free[b], 1)
                        elif k >= 9:
                            dst = halves_at((uT, thp, tha)[(k - 9) // 2], it * 2 + (k - 9) % 2)
                            act.activation(dst, accv[b].unsqueeze(1), ACT.Copy if k < 11 else ACT.Tanh, scale=1.0 if k < 11 else 0.5).then_inc(acc_free[b], 1)
                        if k < 9:
                            split("pairs", it, pos)
                    elif what == "turn":
                        act.wait_ge(k_turned, it * 3 + (k + 1))
                        act.wait_ge(k_out, it * 48 + (16 * k + 16))
                        w = 1 if k == 0 else 4
                        act.activation(kN[:, 0:w, :].rearrange("p a b -> p (a b)"), psT[:, 512:512 + w * P], ACT.Copy).then_inc(k_nat, 1)
                    elif what == "step":
                        if 0 <= k - 2 < TASKS:
                            j = k - 2
                            r, h = j // 2, j % 2
                            rows = slice(64 * h, 64 * h + 64)
                            act.wait_ge(weighted, it * TASKS + (j + 1))
                            dst = o_hi[rows, ds(it, 1), 0:TP].rearrange("p o (i r) -> p o r i", r=NR)[:, :, r, :]
                            act.activation(dst, psO[IDLE[what, k]][rows, :].unsqueeze(1), ACT.Copy).then_inc(o_hid, 1)
                        if 0 <= k - 1 < TASKS:
                            j = k - 1
                            act.wait_ge(turned, it * TASKS + (j + 1))
                            if j >= 2:
                                act.wait_ge(weighted, it * TASKS + (j - 1))
                            act.activation(PT[:, j % 2, :], psT[:, 0:768], ACT.Copy).then_inc(copied, 1)
                        if k < TASKS:
                            act.wait_ge(maxed, it * TASKS + (k + 1))
                            act.activation(S[:, k % 2, :], S[:, k % 2, :], ACT.Exp, bias=neg_max[:, k % 2, :], scale=-1.0,
                                           accum_out=den[:, k % 2, :]).then_inc(expd, 1)

            def pooled_hi(q):
                act.wait_ge(pooled, q + 1)
                act.activation(act_hi[:, 2 * q:2 * q + 2, :], uT[:, 2 * q:2 * q + 2, :], ACT.Copy).then_inc(act_ready, 1)

            done("pairs", PAIRS - 1, TURN_UNITS - 1)
            pooled_hi(0)
            pooled_hi(1)
            act.wait_ge(rows_turned, 1)
            act.wait_ge(ada_out, PAIRS + 1)
            act.activation(qhl[0:64, :], psT[0:64, 0:DA], ACT.Copy)
            act.activation(smp_rows[0:3 * NG * NB, :], psT[0:3 * NG * NB, 0:DA], ACT.Copy).then_inc(smp_ready, 1)
            act.wait_ge(tail_turned, 1)
            act.activation(tail_rows[0:TAIL, :], psS[0:TAIL, :], ACT.Copy).then_inc(tail_ready, 1)
            pooled_hi(2)
            pooled_hi(3)
            act.wait_ge(pooled_split, 4)
            for pos, (what, m) in enumerate(MID):
                if 1 <= pos < 7:
                    i = pos - 1
                    if i >= 2:
                        act.wait_ge(prod_done, i - 1)
                    for b in range(4):
                        act.wait_ge(q_cast, 4 * i + b + 1)
                        act.activation(qB[i % 2][:, b, :], psS[:, 512 * (b % 2):512 * (b % 2) + 512], ACT.Copy).then_inc(q_out, 1)
                if what == "map":
                    for q in range(4):
                        i = 4 * m + q
                        if q < 3:
                            act.wait_ge(part_done, 3 * m + q + 1)
                        else:
                            done("mid", 0, pos)
                        act.activation(halves(mix_hi[:, i, :]), accv[i % 2], ACT.Identity, scale=vec[:, 80 + i:81 + i]).then_inc(mixed_hid, 1)
                if (what, m) == ("pp", 6):
                    act.wait_ge(smp_max, 1)
                    act.activation(sc[0:NB * NS, :], sc[0:NB * NS, :], ACT.Exp, bias=bh_stat[0:NB * NS, 0:1], scale=1.0,
                                   accum_out=bh_stat[0:NB * NS, 1:2]).then_inc(smp_exp, 1)
                if what == "pp":
                    done("mid", 0, pos)
                def merged_hi(i):
                    act.wait_ge(merged, i + 1)
                    act.activation(act_hi[:, i, :], tha[:, i, :], ACT.Copy).then_inc(act_ready, 1)

                if what == "pa":
                    merged_hi(2 * m)
                    done("mid", 0, pos)
                split("mid", 0, pos)
                if what == "pa":
                    merged_hi(2 * m + 1)
                if (what, m) == ("pp", 7):
                    act.wait_ge(smp_summed, 1)
                    act.activation(o_hi[:, :, TP:TC], psT[:, 0:PAIRS * NB].rearrange("p (a b) -> p a b", a=PAIRS), ACT.Copy).then_inc(os_hid, 1)

            with act.Fori(0, 2) as it:
                for k in range(4):
                    done("out", it, k)
                    split("out", it, k)
                    act.activation(halves_at(mixT, it * 4 + k), accv[k % 2].unsqueeze(1), ACT.Copy, scale=0.5)
                    act.wait_ge(ssqd, it * 4 + (9 + k))
                    act.activation(halves(sq[:, k % 2, :]), accv[k % 2], ACT.Square, scale=0.5).then_inc(acc_free[k % 2], 1)
            root(2)
            for k in range(KT):
                act.wait_ge(x_upd, k + 1)
                if k >= 2:
                    act.wait_ge(ssqd, 17 + k - 1)
                act.activation(sq[:, k % 2, :], xT[:, k, :], ACT.Square).then_inc(squared, 1)
            root(3)
            modulate(norm_u, a_f, 24, KT)
            act.activation(seed[:, 13:14], eps[:, :], ACT.Gelu_apprx_tanh)

            with act.Fori(0, FT // 2) as it:
                for k in range(4):
                    m, half = k // 2, k % 2
                    done("up", it, k)
                    w2 = vec[:, ds(it * 2 + (176 + m + half * FT), 1)]
                    bc = vec[:, ds(it * 2 + (220 + m + half * FT), 1)]
                    act.wait_ge(taps, it * 4 + (k + 1))
                    act.wait_ge(hu_tailed, it * 4 + (k + 1))
                    act.activation(halves(he[half][m][:, 2:2 + TC]), accv[k % 2], ACT.Copy)
                    act.activation(halves(cv[half][m][:, :]), accv[k % 2], ACT.Identity, bias=bc, scale=w2).then_inc(acc_free[k % 2], 1)
                    split("up", it, k)
                    if half == 1:
                        act.wait_ge(taps, it * 4 + (4 + 2 * m + 1))
                        act.wait_ge(g_lod, it * 2 + (m + 1))
                        act.activation(gm[m][:, :], cv[0][m][:, :], ACT.Gelu_apprx_tanh).then_inc(gelud, 1)
                        act.wait_ge(gated, it * 2 + (m + 1))
                        act.activation(g_hi[:, ds(it * 2 + m, 1), :].rearrange("p o n -> p (o n)"), gm[m][:, :], ACT.Copy).then_inc(g_hid, 1)

            def down(seg, it, m0):
                for k in range(6):
                    done(seg, it, k)
                    if not (seg == "last" and k >= 4):
                        split(seg, it, k)
                    if k % 3 == 2:
                        b = k // 3
                        act.activation(halves_at(ffn, m0 + b), accv[b].unsqueeze(1), ACT.Copy)
                        act.wait_ge(ssqd, it * 2 + ((25 if seg == "down" else 31) + b))
                        act.activation(halves(sq[:, b, :]), accv[b], ACT.Square).then_inc(acc_free[b], 1)

            with act.Fori(0, 3) as it:
                down("down", it, it * 2)
            for i, t in enumerate((psS, psT)):
                act.wait_ge(hu_turned, i + 1)
                act.activation(hu_rows[0:2 * FT, 5 * i:5 * i + 5, :].rearrange("p a b -> p (a b)"), t[0:2 * FT, 0:5 * P], ACT.Copy).then_inc(hu_rowed, 1)
            down("last", 0, 6)
            root(4)
            for k in range(KT):
                act.wait_ge(y_turned, k + 1)
                act.activation(y_rows[:, :, k * P:(k + 1) * P], psT[:, 512 * (k % 2):512 * (k % 2) + 512].rearrange("p (a b) -> p a b", a=4),
                               ACT.Copy).then_inc(y_ready, 1)
            act.wait_ge(ys_turned, 1)
            act.activation(ys_rows[0:NB, :], acc[0][0:NB, :, :].rearrange("p a b -> p (a b)"), ACT.Copy).then_inc(ys_ready, 1)

        @block.vector
        def _(dve):
            n = [0]

            def mark(ins_):
                n[0] += 1
                ins_.then_inc(dve_step, 1)
                return n[0]

            def mine():
                dve.wait_ge(dve_step, n[0])

            def split(seg, it, pos, ahead=2):
                units = SEGMENTS[seg][1]
                if units % 2 and pos >= units - 2:
                    if pos == units - 2:
                        return
                    if ahead == 2:
                        split(seg, it, pos, 1)
                pos += ahead
                s = pos - units if pos >= units else pos
                cols = 6 * P if seg in ("down", "last") and pos in (2, 5) else UW
                dve.wait_ge(hi_ready, st.number(seg, it, pos) + 1)
                hi, lo = slot(seg if pos < units else "", s)
                dve.tensor_tensor(lo[:, 0:cols], raw[:, s % RAW, 0:cols], hi[:, 0:cols].bitcast(F32), ALU.subtract).then_inc(lo_ready, 1)

            def done(seg, it, pos):
                dve.wait_ge(unit_done, st.number(seg, it, pos) + 1)

            def rows_out(n, k, dst, src):
                dve.tensor_copy(dst[0:n, k - 1:k + 1, :].rearrange("p a b -> p (a b)"), src[0:n, :]).then_inc(ada_rowed, 1)

            def ada_evac(seg, it, pos, k, dst, src):
                done(seg, it, pos)
                if k % 2:
                    rows_out(2 * MC, k, dst, src)
                split(seg, it, pos)

            def modulation(t0, n, src, count):
                dve.wait_ge(folded, count)
                dve.tensor_tensor(mod[:, ds(t0, n), :], src.rearrange("p (a b) -> p a b", b=MC)[:, 0:n, :],
                                  vec[:, ds(t0, n)].unsqueeze(2).to_broadcast([P, n, MC]), ALU.add).then_inc(ada_out, 1)

            for i, (s, c) in enumerate(((acc_free[0], 1), (acc_free[1], 1), (lo_ready, RAW), (o_lod, 2), (k_out, 16), (v_out, 16), (ssqd, 1), (taps, 4),
                         (hu_tailed, 4), (g_lod, 2), (ada_done, 4))):
                dve.memset(seed[:, i:i + 1], 0.0).then_inc(s, c)
            dve.memset(silu2[:, KT * 2 * MC:].bitcast(F32), 0.0).then_inc(silu_zeroed, 1)
            dve.wait_ge(c_tanhed, 1)
            dve.scalar_tensor_tensor(c_silu[0:MC, :], c_tanh[0:MC, :], 1.0, c_rows[0:MC, :], ALU.add, ALU.mult).then_inc(c_ready, 1)
            dve.wait_ge(pool_k, 1)
            dve.tensor_tensor(fold[0:2 * MC, :], ident[0:2 * MC, 0:MC], ident[0:2 * MC, MC:2 * MC], ALU.add).then_inc(fold_ready, 1)
            dve.tensor_tensor(sel[0:64, :], ident[0:64, 0:NG * NB], ident[0:64, 32:32 + NG * NB], ALU.add)
            bs = slice(0, NB * NS)
            dve.tensor_reduce(own_head[bs, :], ident[bs, bs].rearrange("p (b h) -> p h b", h=NS), AX_X, ALU.add)
            dve.tensor_reduce(own_sample[bs, :], ident[bs, bs].rearrange("p (b h) -> p b h", h=NS), AX_X, ALU.add).then_inc(masks_ready, 1)
            split("start", 0, -2)
            dve.wait_ge(silu_hid, 1)
            silu = silu2[:, 0:KT * 2 * MC].rearrange("p (k j c) -> p k j c", k=KT, j=2)
            dve.scalar_tensor_tensor(silu[:, :, 1, :], acc[1][:, 0, 0:KT * MC].rearrange("p (k c) -> p k c", k=KT), 0.5,
                                     silu[:, :, 0, :].bitcast(F32), ALU.mult, ALU.subtract).then_inc(silu_out, 1)
            for t in (-1, 0, 1):
                split("start", 0, t)
            for t in range(NSTART):
                if t % 2:
                    done("start", 0, t)
                    rows_out(2 * MC, t, ada_start, start_at(t))
                if t + 4 < NSTART:
                    split("start", 0, t + 2)
            split("start", 0, NSTART - 2)
            split("start", 0, NSTART - 1)
            mark(dve.tensor_reduce(ind4[:, 0, :], ident[:, :].rearrange("p (a b) -> p b a", b=4), AX_X, ALU.add))
            mine()
            mark(dve.tensor_scalar(ind4[:, 1, :], ind4[:, 0, :], -NEG, NEG, ALU.mult, ALU.add))
            mine()
            dve.wait_ge(pool_k, 2)
            for r in range(NR):
                m2 = mask[:, r, TP + P:TP + 2 * P].rearrange("p (a b) -> p a b", b=4)
                mark(dve.tensor_tensor(m2, m2, ind4[:, 1, :].unsqueeze(1).to_broadcast([P, 32, 4]), ALU.add))
            dve.wait_ge(hist_turned, 1)
            for gi in range(4):
                win = 2 ** (gi + 1)
                src = acc[0][:, gi // 2, (gi % 2) * 240:(gi % 2) * 240 + 240].rearrange("p (k b t) -> p k b t", k=2, b=NB)[:, :, :, 16 - win:]
                ins_ = dve.tensor_reduce(hist_sum[:, 2 * gi:2 * gi + 2, :], src, AX_X, ALU.add)
            ins_.then_inc(hist_ready, 1)

            dve.wait_ge(vec_out, 1)
            modulation(0, NSTART, psS[:, 0:NSTART * MC], 1)
            def inverse_root(n):
                v, r0, h, r1 = nrm[:, 0, :], nrm[:, 2, :], nrm[:, 3, :], nrm[:, 5, :]
                dve.wait_ge(summed, n)
                dve.tensor_scalar(v, psR, 1.0 / D, EPS, ALU.mult, ALU.add).then_inc(mean_ready, 1)
                dve.wait_ge(std_ready, n)
                mark(dve.reciprocal(r0, nrm[:, 1, :]))
                mine()
                mark(dve.scalar_tensor_tensor(h, v, -0.5, r0, ALU.mult, ALU.mult))
                mine()
                mark(dve.tensor_tensor(nrm[:, 4, :], h, r0, ALU.mult))
                mine()
                dve.scalar_tensor_tensor(r1, nrm[:, 4, :], 1.5, r0, ALU.add, ALU.mult).then_inc(rooted, 1)

            dve.wait_ge(ada_out, 1)

            def gains(dst, scale0, g0, plus):
                v = vec[:, g0:g0 + 8].unsqueeze(2).to_broadcast([P, 8, MC])
                return mark(dve.scalar_tensor_tensor(dst[:, :, :], mod[:, scale0:scale0 + 8, :], plus, v, ALU.add, ALU.mult))

            gains(a_m, 8, 48, 1.0)
            mine()

            def modulated(u, a, shift0, base, n):
                dve.wait_ge(rs_ready, n)
                us, xs = u[:, :, TP:TC], xT[:, :, TP:TC]
                mark(dve.tensor_tensor(small[:, :, :], xs, rs_s.unsqueeze(1).to_broadcast([P, KT, NB]), ALU.mult))
                mine()
                mark(dve.tensor_tensor(small[:, :, :], small[:, :, :], a[:, :, 0:NB], ALU.mult))
                mine()
                mark(dve.tensor_tensor(us, small[:, :, :], mod[:, shift0:shift0 + 8, 0:NB], ALU.add))
                for k in range(KT + 2):
                    if k < KT:
                        dve.tensor_tensor(u[:, k, 0:TP], xT[:, k, 0:TP], rs_p, ALU.mult).then_inc(xr_ready, 1)
                    if k >= 2:
                        dve.wait_ge(act_ready, base + k - 1)
                        dve.tensor_tensor(act_lo[:, k - 2, :], u[:, k - 2, :], act_hi[:, k - 2, :].bitcast(F32), ALU.subtract).then_inc(act_split, 1)

            inverse_root(1)
            modulated(uT, a_m, 0, 0, 1)

            with dve.Fori(0, PAIRS) as it:
                for what, k in TURN:
                    if what == "ada" and k % 2:
                        done("pairs", it, POS[what, k])
                        rows_out(2 * MC, k, ada_rows, psA)
                        split("pairs", it, POS[what, k] - 1)
                        split("pairs", it, POS[what, k])
                    elif what == "ada":
                        split("pairs", it, POS[what, k])
                    elif what == "unit":
                        pos = POS[what, k]
                        if k < 9 and k % 3 == 2:
                            b = k % 2
                            done("pairs", it, pos)
                            dve.tensor_copy(halves(qkvT[:, k, :]), accv[b]).then_inc(acc_free[b], 1)
                        if STREAMED[min(pos + 1, TURN_UNITS - 1)] not in (("ada", 1), ("ada", 3)):
                            split("pairs", it, pos)
                    elif what == "turn":
                        dve.wait_ge(v_turned, it * 3 + (k + 1))
                        dve.wait_ge(v_out, it * 48 + 16)
                        dve.tensor_copy(vN[:, k, :, :].rearrange("p a b -> p (a b)"), psT[:, 0:512]).then_inc(v_nat, 1)
                        if k == 2:
                            src = qkvT[:, :, TP:TC].rearrange("p (g t) b -> p t g b", t=3)
                            for t in range(3):
                                ins_ = dve.tensor_copy(smpT[:, ds(it, 1), t * NG:(t + 1) * NG, :], src[:, t].unsqueeze(1))
                            ins_.then_inc(smpT_ready, 1)
                    elif what == "step":
                        if 0 <= k - 2 < TASKS:
                            j = k - 2
                            r, h = j // 2, j % 2
                            rows = slice(64 * h, 64 * h + 64)
                            dve.wait_ge(o_hid, it * TASKS + (j + 1))
                            hi, lo = (x[rows, ds(it, 1), 0:TP].rearrange("p o (i r) -> p o r i", r=NR)[:, :, r, :] for x in (o_hi, o_lo))
                            dve.tensor_tensor(lo, psO[IDLE[what, k]][rows, :].unsqueeze(1), hi.bitcast(F32), ALU.subtract).then_inc(o_lod, 1)
                        if k < TASKS:
                            dve.wait_ge(scored, it * TASKS + (k + 1))
                            if k >= 2:
                                dve.wait_ge(turned, it * TASKS + (k - 1))
                            dve.memset(seed[:, 11:12], 0.0)
                            dve.tensor_tensor_reduce(S[:, k % 2, :], psS[:, 0:768], mask[:, k // 2, :], -1.0, BIG, ALU.add, ALU.min,
                                                     neg_max[:, k % 2, :]).then_inc(maxed, 1)
                            dve.wait_ge(expd, it * TASKS + (k + 1))
                            dve.reciprocal(rden[:, k % 2, :], den[:, k % 2, :]).then_inc(rdend, 1)
                            dve.wait_ge(rdend, it * TASKS + (k + 1))
                            dve.tensor_scalar(S[:, k % 2, :], S[:, k % 2, :], rden[:, k % 2, :], None, ALU.mult).then_inc(normed, 1)
                    elif what == "fold":
                        modulation(it * NA + NSTART, NA, psM[IDLE[what, k]], it + 2)

            for q in range(4):
                if q == 2:
                    dve.wait_ge(smp_ready, 1)
                    dve.tensor_tensor(qhl[32:32 + NG * NB, :], smp_rows[0:NG * NB, :], qhl[0:NG * NB, :].bitcast(F32), ALU.subtract).then_inc(q_split, 1)
                dve.wait_ge(act_ready, 8 + q + 1)
                dve.tensor_tensor(act_lo[:, 2 * q:2 * q + 2, :], uT[:, 2 * q:2 * q + 2, :], act_hi[:, 2 * q:2 * q + 2, :].bitcast(F32),
                                  ALU.subtract).then_inc(pooled_split, 1)

            def sample_scores(i):
                g, h = divmod(i, 2)
                dve.wait_ge(prod_done, i + 1)
                src = kS[i][:, :, :].rearrange("p b (s d) -> p b s d", d=HD)
                dve.tensor_reduce(sall[:, g, 4 * h:4 * h + 4, :], src, AX_X, ALU.add).then_inc(score_sum, 1)

            def sample_softmax():
                bs = slice(0, NB * NS)
                dve.wait_ge(smp_back, 16)
                mark(dve.tensor_tensor(bh_tmp[bs, :, :], bh[bs, 0:NG, :], bh[bs, NG:2 * NG, :], ALU.mult))
                mine()
                mark(dve.tensor_reduce(sc[bs, NG * P:], bh_tmp[bs, :, :], AX_X, ALU.add))
                dve.wait_ge(smp_in, 1)
                mark(dve.tensor_copy(sc[bs, 0:NG * P], psT[bs, 512:512 + NG * P]))
                mine()
                mark(dve.tensor_reduce(bh_stat[bs, 2:3], sc[bs, :], AX_X, ALU.max))
                mine()
                dve.tensor_scalar(bh_stat[bs, 0:1], bh_stat[bs, 2:3], -1.0, None, ALU.mult).then_inc(smp_max, 1)
                dve.wait_ge(smp_exp, 1)
                mark(dve.reciprocal(bh_stat[bs, 3:4], bh_stat[bs, 1:2]))
                mine()
                mark(dve.tensor_scalar(sc[bs, :], sc[bs, :], bh_stat[bs, 3:4], None, ALU.mult))
                mine()
                mark(dve.tensor_scalar(o_new[bs, :], bh[bs, 2 * NG, :], sc[bs, NG * P:NG * P + 1], None, ALU.mult))
                for g in range(1, NG):
                    mine()
                    ins_ = dve.scalar_tensor_tensor(o_new[bs, :], bh[bs, 2 * NG + g, :], sc[bs, NG * P + g:NG * P + g + 1],
                                                    o_new[bs, :], ALU.mult, ALU.add)
                    if g < NG - 1:
                        mark(ins_)
                ins_.then_inc(o_new_ready, 1)

            def merge_lo(i):
                dve.wait_ge(act_ready, 12 + i + 1)
                dve.tensor_tensor(act_lo[:, i, :], tha[:, i, :], act_hi[:, i, :].bitcast(F32), ALU.subtract).then_inc(merged_split, 1)

            for pos, (what, m) in enumerate(MID):
                if what == "map":
                    for q in range(4):
                        i = 4 * m + q
                        dve.wait_ge(mixed_hid, i + 1)
                        dve.scalar_tensor_tensor(halves(mix_lo[:, i, :]), accv[i % 2], vec[:, 80 + i:81 + i], halves(mix_hi[:, i, :].bitcast(F32)), ALU.mult, ALU.subtract).then_inc(acc_free[i % 2], 1)
                    split("mid", 0, pos)
                if what == "pp":
                    if m == 6:
                        sample_scores(5)
                        sample_softmax()
                    if m == 7:
                        dve.wait_ge(smp_turned, 1)
                        dve.wait_ge(pr_zeroed, 1)
                        for g in range(NG):
                            dst = prT[:, g, NB * NS - NS:].rearrange("p (b c) -> p b c", b=NB)[:, :, 0:NS]
                            ins_ = dve.tensor_copy(dst, psT[:, g * NB * NS:(g + 1) * NB * NS].rearrange("p (b h) -> p b h", b=NB))
                        ins_.then_inc(pr_ready, 1)
                        dve.wait_ge(pv_done, 1)
                        dve.wait_ge(smp_stored, 16)
                        dve.wait_ge(new_rows, 16 * 2 * NG)
                        mark(dve.tensor_tensor(o_rows[bs, :, :], psT[bs, 512:1024].rearrange("p (h d) -> p h d", h=NS),
                                               o_new[bs, :].unsqueeze(1).to_broadcast([NB * NS, NS, HD]), ALU.add))
                        mine()
                        dve.tensor_tensor(o_rows[bs, :, :], o_rows[bs, :, :], own_head[bs, :].unsqueeze(2).to_broadcast([NB * NS, NS, HD]),
                                          ALU.mult).then_inc(o_rowed, 1)
                    done("mid", 0, pos)
                    v = halves(thp[:, m, :])
                    dve.scalar_tensor_tensor(v, v, 1.0, accv[m % 2], ALU.add, ALU.mult).then_inc(acc_free[m % 2], 1)
                    split("mid", 0, pos)
                    if 1 <= m <= 5:
                        sample_scores(m - 1)
                    if m == 7:
                        dve.wait_ge(os_hid, 1)
                        dve.tensor_tensor(o_lo[:, :, TP:TC], psT[:, 0:PAIRS * NB].rearrange("p (a b) -> p a b", a=PAIRS),
                                          o_hi[:, :, TP:TC].bitcast(F32), ALU.subtract).then_inc(os_lod, 1)
                        dve.wait_ge(ada_out, PAIRS + 1)
                        gains(gg_m, 16, 56, 0.0)
                if what == "pa":
                    for q in range(2):
                        i = 2 * m + q
                        if i >= 1:
                            merge_lo(i - 1)
                        if q:
                            done("mid", 0, pos)
                        else:
                            dve.wait_ge(part_done, 6 + m + 1)
                        v = halves(tha[:, i, :])
                        dve.scalar_tensor_tensor(v, v, 1.0, accv[i % 2], ALU.add, ALU.mult).then_inc(acc_free[i % 2], 1)
                        if q:
                            split("mid", 0, pos)
            merge_lo(7)

            dve.wait_ge(conv_turned, 1)
            for j in range(2):
                src = psT[:, 512 * j:512 * j + NB * 2 * FT].rearrange("p (b m) -> p b m", b=NB)
                w = vec[:, 88 + 44 * j:132 + 44 * j].unsqueeze(1).to_broadcast([P, NB, 2 * FT])
                dve.tensor_tensor(cst[:, j, :].rearrange("p (b m) -> p b m", b=NB), src, w, ALU.mult).then_inc(conv_used, 1)
            dve.wait_ge(conv_used, 2)
            mark(dve.tensor_tensor(hsc[:, :, :].rearrange("p b m -> p (b m)"), cst[:, 0, :], cst[:, 1, :], ALU.add))
            mark(dve.memset(ssq[:, :], 0.0))
            mine()

            with dve.Fori(0, 2) as it:
                for k in range(4):
                    split("out", it, k)
                    dve.wait_ge(acc_free[k % 2], it * 2 + (acc_uses["out"][k % 2] + k // 2 + 2))
                    dve.wait_ge(ssqd, it * 4 + (9 + k))
                    dve.tensor_tensor(ssq[:, :], ssq[:, :], sq[:, k % 2, :], ALU.add).then_inc(ssqd, 1)
                    if k % 2:
                        dve.wait_ge(ada_done, it * 4 + (4 + k + 1))
                        rows_out(MC, k, ada_rows, psA_mid)
                modulation(it * 4 + (NADA - 16), 4, psM_mid, it + (PAIRS + 2))
            dve.wait_ge(ada_out, PAIRS + 3)
            gains(a_f, 32, 64, 1.0)

            def post_norm(src, gg, roots):
                inverse_root(roots)
                dve.wait_ge(rs_ready, roots)
                mark(dve.tensor_tensor(small[:, :, :], src[:, :, TP:TC], rs_s.unsqueeze(1).to_broadcast([P, KT, NB]), ALU.mult))
                mine()
                mark(dve.tensor_tensor(small[:, :, :], small[:, :, :], gg[:, :, 0:NB], ALU.mult))
                mine()
                mark(dve.tensor_tensor(xT[:, :, TP:TC], xT[:, :, TP:TC], small[:, :, :], ALU.add))
                for k in range(KT + 1):
                    if k < KT:
                        mark(dve.scalar_tensor_tensor(src[:, k, 0:TP], src[:, k, 0:TP], gg[:, k, PROMPT:MC], rs_p, ALU.mult, ALU.mult))
                        mine()
                        dve.tensor_tensor(xT[:, k, 0:TP], xT[:, k, 0:TP], src[:, k, 0:TP], ALU.add).then_inc(x_upd, 1)

            post_norm(mixT, gg_m, 2)
            for h in (*he[0], *he[1]):
                mark(dve.memset(h[:, 0:2], 0.0))
            inverse_root(3)
            modulated(norm_u, a_f, 24, 20, 3)
            mark(dve.memset(ssq[:, :], 0.0))
            mine()

            with dve.Fori(0, FT // 2) as it:
                for k in range(4):
                    m, half = k // 2, k % 2
                    dve.wait_ge(acc_free[k % 2], it * 2 + (acc_uses["up"][k % 2] + k // 2 + 2))
                    c, h = cv[half][m], he[half][m]
                    w0, w1 = (vec[:, ds(it * 2 + (88 + 44 * j + m + half * FT), 1)] for j in range(2))
                    dve.tensor_tensor(c[:, TP:TC], c[:, TP:TC], hsc[:, :, ds(it * 2 + (m + half * FT), 1)].rearrange("p b o -> p (b o)"), ALU.add)
                    dve.scalar_tensor_tensor(c[:, 0:TP], h[:, 1:1 + TP], w1, c[:, 0:TP], ALU.mult, ALU.add).then_inc(tap1, 1)
                    dve.wait_ge(tap1, it * 4 + (k + 1))
                    dve.scalar_tensor_tensor(c[:, 0:TP], h[:, 0:TP], w0, c[:, 0:TP], ALU.mult, ALU.add).then_inc(taps, 1)
                    split("up", it, k)
                    if half == 1:
                        dve.wait_ge(gelud, it * 2 + (m + 1))
                        dve.wait_ge(taps, it * 4 + (4 + k + 1))
                        dve.tensor_tensor(gm[m][:, :], gm[m][:, :], c[:, :], ALU.mult).then_inc(gated, 1)
                        dve.wait_ge(g_hid, it * 2 + (m + 1))
                        hi, lo = (x[:, ds(it * 2 + m, 1), :].rearrange("p o n -> p (o n)") for x in (g_hi, g_lo))
                        dve.tensor_tensor(lo, gm[m][:, :], hi.bitcast(F32), ALU.subtract).then_inc(g_lod, 1)

            def down(seg, it):
                for k in range(6):
                    if not (seg == "last" and k >= 4):
                        split(seg, it, k)
                    if k % 3 == 2:
                        b = k // 3
                        dve.wait_ge(acc_free[b], it + (acc_uses[seg][b] + 2))
                        dve.wait_ge(ssqd, it * 2 + ((25 if seg == "down" else 31) + b))
                        dve.tensor_tensor(ssq[:, :], ssq[:, :], sq[:, b, :], ALU.add).then_inc(ssqd, 1)

            with dve.Fori(0, 3) as it:
                down("down", it)
            dve.wait_ge(ada_done, 4 + 16)
            for q in range(2):
                if q:
                    dve.wait_ge(ada_out, PAIRS + 4)
                dve.tensor_copy(late_rows[0:MC, :, :].rearrange("p a b -> p (a b)"), psT[0:MC, 512 * q:512 * q + 512]).then_inc(ada_rowed, 1)
                modulation(NADA - 8 + 4 * q, 4, psM[1], PAIRS + 4 + q)
            dve.wait_ge(ada_out, PAIRS + 5)
            gains(gg_f, 40, 72, 0.0)
            down("last", 0)
            post_norm(ffn, gg_f, 4)

        @block.tensor
        def _(pe):
            def blocks(b, s, pairs, hi, lo, first=True, last=True, wait=None):
                for i, (blk, t) in enumerate(pairs):
                    if wait:
                        pe.wait_ge(wait[0], wait[1] + i + 1)
                    wh, wl = w_hi[:, s, blk * P:(blk + 1) * P], w_lo[:, s, blk * P:(blk + 1) * P]
                    for j, (w, x) in enumerate(((wh, hi), (wh, lo), (wl, hi))):
                        for half in range(2):
                            ins_ = pe.matmul(acc[b][:, half, 0:HALF], w, x[:, t, half * HALF:(half + 1) * HALF],
                                             start=first and i == 0 and j == 0, stop=last and i == len(pairs) - 1 and j == 2)
                return ins_

            def ready(seg, it, pos):
                pe.wait_ge(lo_ready, st.number(seg, it, pos) + 1 + RAW)

            def free(b, uses):
                pe.wait_ge(acc_free[b], uses + 1)

            def ada(s, half, where):
                for k in range(4):
                    at = 2 * MC * (4 * half + k)
                    for j, w in enumerate(s):
                        ins_ = pe.matmul(where, silu2[:, at:at + P], w[:, k * 2 * P:(k + 1) * 2 * P],
                                         start=half == 0 and k == 0 and j == 0, stop=half == 1 and k == 3 and j == 1)
                ins_.then_inc(unit_done, 1)

            def turn_rows(rows, n, where):
                for i in range(n):
                    ins_ = pe.matmul(where[:, i * MC:(i + 1) * MC], rows[0:2 * MC, i, :], fold[0:2 * MC, :], start=True, stop=True)
                ins_.then_inc(folded, 1)

            pe.wait_ge(pool_k, 1)
            pe.wait_ge(c_ready, 1)
            for k in range(KT):
                ins_ = pe.transpose(acc[1][:, 0, k * MC:(k + 1) * MC], c_silu[0:MC, k * P:(k + 1) * P], ident[0:MC, 0:MC])
            ins_.then_inc(silu_turned, 1)
            pe.wait_ge(xs_loaded, 16)
            for k in range(KT):
                ins_ = pe.transpose(acc[0][:, 1, 256 + k * NB:256 + (k + 1) * NB], xs_rows[0:NB, k * P:(k + 1) * P], ident[0:NB, 0:NB])
            ins_.then_inc(xs_turned, 1)
            pe.wait_ge(vec_loaded, 16 * 9)
            for i in range(3):
                ins_ = pe.transpose(acc[1][:, 1, 88 * i:88 * i + 88], vec_rows[0:88, i, :], ident[0:88, 0:88])
            ins_.then_inc(vec_turned, 1)

            def sum_columns():
                for j in range(5):
                    at = j * P if j < 4 else TC - P
                    ins_ = pe.matmul(psR[:, j:j + 1], ssq[:, at:at + P], ones[:, 0:1], start=True, stop=True)
                ins_.then_inc(summed, 1)

            def spread(n):
                pe.wait_ge(rooted, n)
                for j in range(5):
                    ins_ = pe.transpose(psS[:, j * P:(j + 1) * P], nrm[:, 5, j:j + 1].to_broadcast([P, P]), ident[:, :])
                ins_.then_inc(rs_ready, 1)

            pe.wait_ge(silu_out, 1)
            for t in range(NSTART):
                ready("start", 0, t)
                if t >= 4:
                    pe.wait_ge(ada_rowed, t // 2 - 1)
                ada(slot("start", t), t % 2, start_at(t))
                for k in x_tiles(t):
                    if k == 0:
                        pe.wait_ge(x_loaded, 16)
                    if k >= 2:
                        pe.wait_ge(x_out, k - 1)
                    for i in range(4):
                        at = 512 * (k % 2) + i * P
                        ins_ = pe.transpose(psT[:, at:at + P], x_rows[:, i, k * P:(k + 1) * P], ident[:, :])
                    ins_.then_inc(x_turned, 1)
            pe.wait_ge(hist_loaded, 16)
            pe.wait_ge(fold_ready, 1)
            pe.wait_ge(ada_rowed, NSTART // 2)
            turn_rows(ada_start, NSTART, psS[:, 0:NSTART * MC])
            pe.wait_ge(xs_out, 1)
            for k in range(KT):
                at = (k % 4) * NB * POOL_HIST
                ins_ = pe.transpose(acc[0][:, k // 4, at:at + NB * POOL_HIST], hist_rows[0:NB * POOL_HIST, k * P:(k + 1) * P],
                                    ident[0:NB * POOL_HIST, 0:NB * POOL_HIST])
            ins_.then_inc(hist_turned, 1)
            pe.wait_ge(ssqd, 9)
            sum_columns()
            pe.wait_ge(ada_out, 1)
            spread(1)

            def idle_is_read(it, what, k):
                b = IDLE[what, k]
                at = TURN.index((what, k))
                free(b, it * (8 - b) + sum(w == "unit" and u % 2 == b for w, u in TURN[:at]))

            with pe.Fori(0, PAIRS) as it:
                steps, adas, folds = 0, 0, 0
                for what, k in TURN:
                    if what in ("half", "unit"):
                        halved, pos = ("half", k) in TURN, POS["unit", k]
                        if what == "half" or not halved:
                            ready("pairs", it, pos)
                            free(k % 2, it * (8 - k % 2) + k // 2)
                            pe.wait_ge(o_lod, it * TASKS + (steps + (1 if k == 0 else 2)))
                            if k % 2 == IDLE["fold", 0]:
                                pe.wait_ge(ada_out, it + (1 + folds))
                        part = range(KT) if not halved else range(KT // 2) if what == "half" else range(KT // 2, KT)
                        ins_ = blocks(k % 2, pos % HL, [(i, i) for i in part], act_hi, act_lo, first=0 in part, last=KT - 1 in part,
                                      wait=(act_split, 0) if k == 0 else None)
                        if what == "unit":
                            ins_.then_inc(unit_done, 1)
                    elif what == "turn":
                        v = 3 * k + 2
                        pe.wait_ge(acc_free[v % 2], it * (8 - v % 2) + (v // 2 + 2))
                        if k:
                            pe.wait_ge(v_nat, it * 3 + k)
                            pe.wait_ge(k_nat, it * 3 + k)
                        for which, t0, done in ((v, 0, v_turned), (v - 1, 512, k_turned)):
                            for r in range(4):
                                if k == 0 and which == v - 1 and r:
                                    continue
                                if k == 0:
                                    src = qkvT[:, which, r * P:(r + 1) * P] if which == v else qkvT[:, which, TP - P:TP]
                                else:
                                    src = qkvT[:, which, 0:TP].rearrange("p (i r) -> p r i", r=NR)[:, r, :]
                                ins_ = pe.transpose(psT[:, t0 + r * P:t0 + (r + 1) * P], src, ident[:, :])
                            ins_.then_inc(done, 1)
                    elif what == "step":
                        if 0 <= k - 2 < TASKS:
                            j = k - 2
                            r, h = j // 2, j % 2
                            rows = slice(64 * h, 64 * h + 64)
                            pe.wait_ge(copied, it * TASKS + (j + 1))
                            idle_is_read(it, what, k)
                            pe.wait_ge(o_lod, it * TASKS + (j + 2))
                            vs = [vN[:, 0, c, rows] for c in range(4)] + [vN[:, 1, r, rows], vN[:, 2, r, rows]]
                            for c in range(6):
                                ins_ = pe.matmul(psO[IDLE[what, k]][rows, :], vs[c], PT[:, j % 2, c * P:(c + 1) * P], start=c == 0, stop=c == 5)
                            ins_.then_inc(weighted, 1)
                            steps = j + 1
                        if k < TASKS:
                            r, h = k // 2, k % 2
                            rows = slice(64 * h, 64 * h + 64)
                            if k:
                                pe.wait_ge(maxed, it * TASKS + k)
                            pe.wait_ge(ada_rowed, it * 2 + (NSTART // 2 + adas // 2))
                            seen = k + 1
                            def cls(i, r=r, rows=rows):
                                return qkvT[rows, i, 0:TP].rearrange("p (i r) -> p r i", r=NR)[:, r, :]
                            pe.matmul(psS[:, 0:TP], cls(0), qkvT[rows, 1, 0:TP], start=True, stop=True)
                            pe.matmul(psS[:, TP:TP + P], cls(3), cls(4), start=True, stop=True)
                            pe.matmul(psS[:, TP + P:TP + 2 * P], cls(6), cls(7), start=True, stop=True).then_inc(scored, 1)
                        if 0 <= k - 1 < TASKS:
                            j = k - 1
                            pe.wait_ge(normed, it * TASKS + (j + 1))
                            if j == 0:
                                pe.wait_ge(v_nat, it * 3 + 3)
                                pe.wait_ge(k_nat, it * 3 + 3)
                            else:
                                pe.wait_ge(copied, it * TASKS + j)
                            for c in range(6):
                                ins_ = pe.transpose(psT[:, c * P:(c + 1) * P], S[:, j % 2, c * P:(c + 1) * P], ident[:, :])
                            ins_.then_inc(turned, 1)
                    elif what == "ada":
                        ready("pairs", it, POS[what, k])
                        pe.wait_ge(maxed, it * TASKS + seen)
                        pe.wait_ge(ada_rowed, it * 2 + (NSTART // 2 + adas // 2))
                        ada(slot("pairs", POS[what, k]), k % 2, psA)
                        adas += 1
                    elif what == "fold":
                        idle_is_read(it, what, k)
                        pe.wait_ge(ada_rowed, it * 2 + (NSTART // 2 + 2))
                        turn_rows(ada_rows, NA, psM[IDLE[what, k]])
                        folds += 1

            pe.wait_ge(smpT_ready, PAIRS)
            pe.wait_ge(copied, PAIRS * TASKS)
            for p in range(PAIRS):
                ins_ = pe.transpose(psT[0:9 * NB, p * P:(p + 1) * P], smpT[:, p, :, :].rearrange("p a b -> p (a b)"), ident[:, :])
            ins_.then_inc(rows_turned, 1)
            pe.wait_ge(pooled, 4)
            pe.wait_ge(o_lod, PAIRS * TASKS + 2)
            for k in range(KT):
                ins_ = pe.transpose(psS[0:TAIL, k * P:(k + 1) * P], u_tail[:, k, :], ident[:, :])
            ins_.then_inc(tail_turned, 1)

            uses = [4 * 8, 4 * 7]

            def take(b):
                free(b, uses[b])
                uses[b] += 1

            def cast(i, h):
                for b in (2 * h, 2 * h + 1):
                    n = 4 * i + b
                    if n == 0:
                        pe.wait_ge(q_split, 1)
                        pe.wait_ge(masks_ready, 1)
                        pe.wait_ge(tail_ready, 1)
                    if n >= 2:
                        pe.wait_ge(q_out, n - 1)
                    r = i // 2 * NB + i % 2 * 4 + b
                    pe.matmul(psS[:, 512 * (b % 2):512 * (b % 2) + 512], sel[0:56, r:r + 1].to_broadcast([56, P]), qhl[0:56, :],
                              start=True, stop=True).then_inc(q_cast, 1)

            def sample_in():
                pe.wait_ge(score_sum, 6)
                pe.wait_ge(smp_ready, 1)
                for g in range(NG):
                    ins_ = pe.transpose(psT[0:NB * NS, 512 + g * P:512 + (g + 1) * P], sall[:, g, :, :].rearrange("p a b -> p (a b)"), ident[:, :])
                ins_.then_inc(smp_in, 1)

            def sample_turn():
                pe.wait_ge(o_new_ready, 1)
                for g in range(NG):
                    ins_ = pe.transpose(psT[:, g * NB * NS:(g + 1) * NB * NS], sc[0:NB * NS, g * P:(g + 1) * P], ident[0:NB * NS, 0:NB * NS])
                ins_.then_inc(smp_turned, 1)

            def sample_values():
                pe.wait_ge(pr_ready, 1)
                for i in range(6):
                    g, h = divmod(i, 2)
                    pe.wait_ge(vS_full, 96)
                    for j in range(4):
                        b = 4 * h + j
                        at = (NB * NS - NS) + (NB * NS - NS) * b
                        ins_ = pe.matmul(psT[0:NB * NS, 512:1024], prT[:, g, at:at + NB * NS], vS[i][:, j, :],
                                         start=i == 0 and j == 0, stop=i == 5 and j == 3)
                ins_.then_inc(pv_done, 1)

            def sample_out():
                pe.wait_ge(o_rowed, 1)
                for p in range(PAIRS):
                    ins_ = pe.matmul(psT[:, p * NB:(p + 1) * NB], o_rows[0:NB * NS, 2 * p:2 * p + 2, :].rearrange("p a b -> p (a b)"),
                                     own_sample[0:NB * NS, :], start=True, stop=True)
                ins_.then_inc(smp_summed, 1)

            for pos, (what, m) in enumerate(MID):
                ready("mid", 0, pos)
                if 1 <= pos < 7:
                    cast(pos - 1, 0)
                if what == "map":
                    for q in range(4):
                        g, d = 2 * m + q // 2, q % 2
                        i = 4 * m + q
                        if pos and q == 2:
                            cast(pos - 1, 1)
                        pe.wait_ge(pooled_split, g + 1)
                        take(i % 2)
                        ins_ = blocks(i % 2, pos % HL, [(4 * (q // 2) + 2 * kt + d, 2 * g + kt) for kt in range(2)], act_hi, act_lo)
                        ins_.then_inc(unit_done if q == 3 else part_done, 1)
                if what == "pp":
                    take(m % 2)
                    if m == 0:
                        pe.wait_ge(acc_free[1], uses[1] + 1)
                    blocks(m % 2, pos % HL, [(i, i) for i in range(KT // 2)], mix_hi, mix_lo, last=False)
                    if pos < 7:
                        cast(pos - 1, 1)
                    if m == 6:
                        sample_in()
                    if m == 7:
                        sample_values()
                    blocks(m % 2, pos % HL, [(i, i) for i in range(KT // 2, KT)], mix_hi, mix_lo, first=False).then_inc(unit_done, 1)
                    if m == 6:
                        sample_turn()
                    if m == 7:
                        sample_out()
                if what == "pa":
                    if m == 0:
                        pe.wait_ge(os_lod, 1)
                    for q in range(2):
                        take(q)
                        ins_ = blocks(q, pos % HL, [(2 * kt + q, kt) for kt in range(4)], o_hi, o_lo)
                        ins_.then_inc(unit_done if q else part_done, 1)
            pe.wait_ge(conv_loaded, 16)
            for j in range(2):
                for b in range(NB):
                    at = 512 * j + b * 2 * FT
                    ins_ = pe.transpose(psT[:, at:at + 2 * FT], conv_rows[0:2 * FT, 2 * b + j, :], ident[0:2 * FT, 0:2 * FT])
            ins_.then_inc(conv_turned, 1)

            def ada32(slot, half, fill, where):
                pe.wait_ge(ada_full[slot], fill)
                for k in range(4):
                    ins_ = pe.matmul(where[0:MC, :], siluT[:, 4 * half + k, :], ada_raw[:, slot, k * 2 * P:(k + 1) * 2 * P],
                                     start=half == 0 and k == 0, stop=half == 1 and k == 3)
                ins_.then_inc(ada_done, 1)

            def turn_rows32(rows, where):
                for i in range(4):
                    ins_ = pe.matmul(where[:, i * MC:(i + 1) * MC], rows[0:MC, i, :], ident[0:MC, 0:MC], start=True, stop=True)
                ins_.then_inc(folded, 1)

            with pe.Fori(0, 2) as it:
                for k in range(4):
                    ready("out", it, k)
                    free(k % 2, it * 2 + (uses[k % 2] + k // 2))
                    if k == 0:
                        pe.wait_ge(merged_split, 8)
                    blocks(k % 2, k % HL, [(i, i) for i in range(KT)], act_hi, act_lo).then_inc(unit_done, 1)
                    if k == 0:
                        pe.wait_ge(conv_used, 2)
                    pe.wait_ge(ada_rowed, it * 2 + (NSTART // 2 + PAIRS * 2 + k // 2))
                    pe.wait_ge(ada_out, it + (PAIRS + 1))
                    ada32(k, k % 2, it * 16 + 16, psA_mid)
                pe.wait_ge(ada_rowed, it * 2 + (NSTART // 2 + PAIRS * 2 + 2))
                turn_rows32(ada_rows, psM_mid)
            assert tuple(uses) == acc_uses["out"]

            pe.wait_ge(ssqd, 17)
            pe.wait_ge(ada_out, PAIRS + 3)
            sum_columns()
            def late(t):
                ada32(t % 4, t % 2, 16 * (t // 4 + 3), psT[:, 256 * (t // 2):256 * (t // 2) + 256])

            spread(2)
            for t in range(6):
                late(t)
            pe.wait_ge(ssqd, 25)
            sum_columns()
            spread(3)
            for t in range(6, 8):
                late(t)

            with pe.Fori(0, FT // 2) as it:
                for k in range(4):
                    ready("up", it, k)
                    free(k % 2, it * 2 + (acc_uses["up"][k % 2] + k // 2))
                    blocks(k % 2, k % HL, [(i, i) for i in range(KT)], act_hi, act_lo, wait=(act_split, 8) if k == 0 else None).then_inc(unit_done, 1)
            def down(seg, it):
                for k in range(6):
                    ready(seg, it, k)
                    b, part = divmod(k, 3)
                    if part == 0:
                        free(b, it + acc_uses[seg][b])
                    if part == 2:
                        pe.wait_ge(g_lod, FT + 2)
                    t0 = 8 * part
                    ins_ = blocks(b, k % HL, [(i, t0 + i) for i in range(min(8, FT - t0))], g_hi, g_lo, first=part == 0, last=part == 2)
                    ins_.then_inc(unit_done, 1)

            with pe.Fori(0, 3) as it:
                down("down", it)
            free(1, acc_uses["last"][1])
            for q in range(2):
                pe.wait_ge(ada_rowed, NSTART // 2 + PAIRS * 2 + 4 + q + 1)
                if q:
                    pe.wait_ge(ada_out, PAIRS + 4)
                turn_rows32(late_rows, psM[1])
            pe.wait_ge(ada_out, PAIRS + 5)
            pe.wait_ge(hu_tailed, 2 * FT + 4)
            for j in range(CONV_TAIL):
                t, at = (psS, psT)[j // 5], j % 5 * P
                ins_ = pe.transpose(t[0:2 * FT, at:at + P], hu_tail[:, :, j], ident[:, :])
                if j % 5 == 4:
                    ins_.then_inc(hu_turned, 1)

            down("last", 0)
            pe.wait_ge(ssqd, 33)
            sum_columns()
            spread(4)
            for k in range(KT):
                pe.wait_ge(x_upd, KT + k + 1)
                if k >= 2:
                    pe.wait_ge(y_ready, k - 1)
                for t in range(4):
                    at = 512 * (k % 2) + t * P
                    ins_ = pe.transpose(psT[:, at:at + P], xT[:, k, t * P:(t + 1) * P], ident[:, :])
                ins_.then_inc(y_turned, 1)
            for k in range(KT):
                ins_ = pe.transpose(acc[0][0:NB, k // 4, (k % 4) * P:(k % 4 + 1) * P], xT[:, k, TP:TC], ident[:, :])
            ins_.then_inc(ys_turned, 1)


def kernel(**inputs):
    import numpy as np
    from concourse import bacc
    from concourse.bass_utils import run_bass_kernel_spmd

    nc = bacc.Bacc("TRN2", target_bir_lowering=False, num_devices=1, dynamic_dma_scratch_size=1024)
    arrays, ins = {}, {}
    for name, a in inputs.items():
        a = np.ascontiguousarray(a)
        arrays[f"in_{name}"] = a
        ins[name] = nc.dram_tensor(f"in_{name}", a.shape, mybir.dt.from_np(a.dtype), kind="ExternalInput").ap()
    names = []

    def out(name, *shape):
        names.append(f"out_{name}")
        return nc.dram_tensor(f"out_{name}", shape, F32, kind="ExternalOutput").ap()

    outs = {"y": (out("y_prompt", 1, TP, D), out("y_sample", NB, 1, D)), "new": []}
    for w in WINS:
        outs["new"].append([(out(f"{x}{w}_prompt", 1, 1, min(w, TP), NS, HD), out(f"{x}{w}_sample", 1, NB, w, NS, HD)) for x in "kv"])
    outs["pool"] = (out("pool_prompt", 1, 1, POOL_HIST, D), out("pool_sample", 1, NB, POOL_HIST, D))
    outs["conv"] = (out("conv_prompt", 1, 1, 2, 2 * FF), out("conv_sample", 1, NB, 2, 2 * FF))
    program(nc, ins, outs)
    r = run_bass_kernel_spmd(nc, [arrays], core_ids=[0])
    return tuple(r.results[0][n] for n in names)
```
